# Optimizing a Trainium2 kernel written in Bass

```python
import math
import jax, jax.numpy as jnp
from jax import lax
import numpy as np

D_MODEL = 2048
BATCH = 1
SEQ = 256
DEPTH = 2

MEM_LEN = 256
MEM_HEADS = 4
MEM_HEAD_DIM = 128
MEM_WIDTH = MEM_HEADS * MEM_HEAD_DIM
MIX_WIDTH = D_MODEL - MEM_WIDTH
POOL_WINDOWS = (2, 4, 8, 16)
N_POOL_GROUPS = len(POOL_WINDOWS)
POOL_GROUP_DIM = MIX_WIDTH // N_POOL_GROUPS
DIFF_HEADS = 12
DIFF_QK_DIM = 64
DIFF_V_DIM = 2 * DIFF_QK_DIM
ROPE_DIM = DIFF_QK_DIM // 4
ROPE_THETA = 500000.0
Q_BLOCK = 128
D_FF = 5632
CONV_WIDTH = 3
LN_EPS = 1e-5
RMS_EPS = 1e-6
DEEPNORM_ALPHA = (2.0 * DEPTH) ** 0.25
DEEPNORM_BETA = (8.0 * DEPTH) ** -0.25
N_POOL_LAYERS = (DEPTH + 1) // 2
N_DIFF_LAYERS = DEPTH // 2
POOL_IN_WIDTH = MIX_WIDTH + MEM_WIDTH
DIFF_IN_WIDTH = 3 * MIX_WIDTH + MEM_WIDTH

kernel_name = 'hybrid_pool_diffattn_deepnorm'

def _layernorm(x, g, b):
    xf = x.astype(jnp.float32)
    mu = jnp.mean(xf, axis=-1, keepdims=True)
    var = jnp.mean(jnp.square(xf - mu), axis=-1, keepdims=True)
    y = (xf - mu) * lax.rsqrt(var + LN_EPS)
    return (y * g.astype(jnp.float32) + b.astype(jnp.float32)).astype(x.dtype)

def _rmsnorm(x, g):
    xf = x.astype(jnp.float32)
    y = xf * lax.rsqrt(jnp.mean(jnp.square(xf), axis=-1, keepdims=True) + RMS_EPS)
    return (y * g.astype(jnp.float32)).astype(x.dtype)

def _rotary(x, cos, sin):
    half = ROPE_DIM // 2
    x1 = x[..., :half]
    x2 = x[..., half:ROPE_DIM]
    return jnp.concatenate([x1 * cos - x2 * sin, x2 * cos + x1 * sin, x[..., ROPE_DIM:]], axis=-1)

def _pool_mixer(h, w_groups, scale):
    B, S, _ = h.shape
    hf = h.astype(jnp.float32).reshape(B, S, N_POOL_GROUPS, POOL_GROUP_DIM)
    csum = jnp.cumsum(hf, axis=1)
    t = jnp.arange(1, S + 1, dtype=jnp.float32)
    outs = []
    for g, w in enumerate(POOL_WINDOWS):
        cg = csum[:, :, g]
        lag = jnp.pad(cg, ((0, 0), (w, 0), (0, 0)))[:, :S]
        cnt = jnp.minimum(t, float(w))[None, :, None]
        outs.append((cg - lag) / cnt - hf[:, :, g])
    d = jnp.stack(outs, axis=2).astype(h.dtype)
    y = jnp.einsum('bsgc,gcd->bsgd', d, w_groups).reshape(B, S, MIX_WIDTH)
    return y * scale

def _diff_attention(q, k, v, lam):
    B, S = q.shape[:2]
    n_blk = S // Q_BLOCK
    scale = DIFF_QK_DIM ** -0.5
    qb = jnp.moveaxis(q.reshape(B, n_blk, Q_BLOCK, DIFF_HEADS, 2, DIFF_QK_DIM), 1, 0)
    starts = jnp.arange(n_blk, dtype=jnp.int32) * Q_BLOCK
    key_pos = jnp.arange(S, dtype=jnp.int32)

    def one_block(args):
        q_blk, start = args
        s = jnp.einsum('bqhcd,bkhcd->bhcqk', q_blk, k).astype(jnp.float32) * scale
        q_pos = start + jnp.arange(Q_BLOCK, dtype=jnp.int32)
        causal = key_pos[None, :] <= q_pos[:, None]
        s = jnp.where(causal, s, -jnp.inf)
        p = jax.nn.softmax(s, axis=-1)
        a = p[:, :, 0] - lam * p[:, :, 1]
        return jnp.einsum('bhqk,bkhd->bqhd', a.astype(v.dtype), v)

    o = lax.map(one_block, (qb, starts))
    return jnp.moveaxis(o, 0, 1).reshape(B, S, DIFF_HEADS, DIFF_V_DIM)

def _mem_attention(q_mem, mem, w_kv):
    B, S, _ = q_mem.shape
    q = q_mem.reshape(B, S, MEM_HEADS, MEM_HEAD_DIM)
    kv = mem @ w_kv
    k = kv[..., :MEM_WIDTH].reshape(B, MEM_LEN, MEM_HEADS, MEM_HEAD_DIM)
    v = kv[..., MEM_WIDTH:].reshape(B, MEM_LEN, MEM_HEADS, MEM_HEAD_DIM)
    s = jnp.einsum('bshd,bmhd->bhsm', q, k).astype(jnp.float32) * (MEM_HEAD_DIM ** -0.5)
    p = jax.nn.softmax(s, axis=-1)
    o = jnp.einsum('bhsm,bmhd->bshd', p.astype(v.dtype), v)
    return o.reshape(B, S, MEM_WIDTH)

def _conv_ffn(x, w_up, conv_w, conv_b, w_down):
    S = x.shape[1]
    h = x @ w_up
    hp = jnp.pad(h, ((0, 0), (CONV_WIDTH - 1, 0), (0, 0)))
    hc = conv_b + sum(conv_w[kk] * hp[:, kk:kk + S] for kk in range(CONV_WIDTH))
    gate = hc[..., :D_FF]
    up = hc[..., D_FF:]
    return (jax.nn.silu(gate) * up) @ w_down

def setup_inputs(seed: int = 0) -> dict:
    key = jax.random.key(seed)
    ks = jax.random.split(key, 24)

    def nrm(k, shape, scale):
        return jax.random.normal(k, shape, jnp.float32) * scale

    x = nrm(ks[0], (BATCH, SEQ, D_MODEL), 1.0)
    mem = nrm(ks[1], (BATCH, MEM_LEN, D_MODEL), 1.0)
    positions = jnp.broadcast_to(jnp.arange(SEQ, dtype=jnp.int32)[None, :], (BATCH, SEQ))
    pool_w_in = nrm(ks[2], (N_POOL_LAYERS, D_MODEL, POOL_IN_WIDTH), D_MODEL ** -0.5)
    pool_w = nrm(ks[3], (N_POOL_LAYERS, N_POOL_GROUPS, POOL_GROUP_DIM, POOL_GROUP_DIM), POOL_GROUP_DIM ** -0.5)
    pool_scale = 1.0 + nrm(ks[4], (N_POOL_LAYERS, MIX_WIDTH), 0.1)
    diff_w_in = nrm(ks[5], (N_DIFF_LAYERS, D_MODEL, DIFF_IN_WIDTH), D_MODEL ** -0.5)
    diff_lambda_q1 = nrm(ks[6], (N_DIFF_LAYERS, DIFF_QK_DIM), 0.1)
    diff_lambda_k1 = nrm(ks[7], (N_DIFF_LAYERS, DIFF_QK_DIM), 0.1)
    diff_lambda_q2 = nrm(ks[8], (N_DIFF_LAYERS, DIFF_QK_DIM), 0.1)
    diff_lambda_k2 = nrm(ks[9], (N_DIFF_LAYERS, DIFF_QK_DIM), 0.1)
    diff_subln_g = 1.0 + nrm(ks[10], (N_DIFF_LAYERS, DIFF_V_DIM), 0.02)
    mem_w_kv = nrm(ks[11], (DEPTH, D_MODEL, 2 * MEM_WIDTH), D_MODEL ** -0.5)
    w_out = nrm(ks[12], (DEPTH, D_MODEL, D_MODEL), DEEPNORM_BETA * D_MODEL ** -0.5)
    ln1_g = 1.0 + nrm(ks[13], (DEPTH, D_MODEL), 0.02)
    ln1_b = nrm(ks[14], (DEPTH, D_MODEL), 0.02)
    ffn_w_up = nrm(ks[15], (DEPTH, D_MODEL, 2 * D_FF), D_MODEL ** -0.5)
    ffn_conv_w = nrm(ks[16], (DEPTH, CONV_WIDTH, 2 * D_FF), CONV_WIDTH ** -0.5)
    ffn_conv_b = nrm(ks[17], (DEPTH, 2 * D_FF), 0.02)
    ffn_w_down = nrm(ks[18], (DEPTH, D_FF, D_MODEL), DEEPNORM_BETA * D_FF ** -0.5)
    ln2_g = 1.0 + nrm(ks[19], (DEPTH, D_MODEL), 0.02)
    ln2_b = nrm(ks[20], (DEPTH, D_MODEL), 0.02)
    return {'x': x, 'mem': mem, 'positions': positions,
            'pool_w_in': pool_w_in, 'pool_w': pool_w, 'pool_scale': pool_scale,
            'diff_w_in': diff_w_in, 'diff_lambda_q1': diff_lambda_q1, 'diff_lambda_k1': diff_lambda_k1,
            'diff_lambda_q2': diff_lambda_q2, 'diff_lambda_k2': diff_lambda_k2, 'diff_subln_g': diff_subln_g,
            'mem_w_kv': mem_w_kv, 'w_out': w_out, 'ln1_g': ln1_g, 'ln1_b': ln1_b,
            'ffn_w_up': ffn_w_up, 'ffn_conv_w': ffn_conv_w, 'ffn_conv_b': ffn_conv_b,
            'ffn_w_down': ffn_w_down, 'ln2_g': ln2_g, 'ln2_b': ln2_b}

def reference(x, mem, positions, pool_w_in, pool_w, pool_scale, diff_w_in, diff_lambda_q1,
              diff_lambda_k1, diff_lambda_q2, diff_lambda_k2, diff_subln_g, mem_w_kv, w_out,
              ln1_g, ln1_b, ffn_w_up, ffn_conv_w, ffn_conv_b, ffn_w_down, ln2_g, ln2_b):
    B, S, _ = x.shape
    inv_freq = ROPE_THETA ** (-jnp.arange(0, ROPE_DIM, 2, dtype=jnp.float32) / ROPE_DIM)
    ang = positions.astype(jnp.float32)[..., None] * inv_freq
    cos = jnp.cos(ang)[:, :, None, None, :].astype(x.dtype)
    sin = jnp.sin(ang)[:, :, None, None, :].astype(x.dtype)

    for i in range(DEPTH):
        j = i // 2
        if i % 2 == 0:
            h = x @ pool_w_in[j]
            mix = _pool_mixer(h[..., :MIX_WIDTH], pool_w[j], pool_scale[j])
            q_mem = h[..., MIX_WIDTH:]
        else:
            h = x @ diff_w_in[j]
            q = h[..., :MIX_WIDTH].reshape(B, S, DIFF_HEADS, 2, DIFF_QK_DIM)
            k = h[..., MIX_WIDTH:2 * MIX_WIDTH].reshape(B, S, DIFF_HEADS, 2, DIFF_QK_DIM)
            v = h[..., 2 * MIX_WIDTH:3 * MIX_WIDTH].reshape(B, S, DIFF_HEADS, DIFF_V_DIM)
            q_mem = h[..., 3 * MIX_WIDTH:]
            q = _rotary(q, cos, sin)
            k = _rotary(k, cos, sin)
            lam_init = 0.8 - 0.6 * math.exp(-0.3 * i)
            lam = (jnp.exp(jnp.sum(diff_lambda_q1[j].astype(jnp.float32) * diff_lambda_k1[j].astype(jnp.float32)))
                   - jnp.exp(jnp.sum(diff_lambda_q2[j].astype(jnp.float32) * diff_lambda_k2[j].astype(jnp.float32)))
                   + lam_init)
            o = _diff_attention(q, k, v, lam)
            mix = (_rmsnorm(o, diff_subln_g[j]) * (1.0 - lam_init)).reshape(B, S, MIX_WIDTH)
        mem_o = _mem_attention(q_mem, mem, mem_w_kv[i])
        y = jnp.concatenate([mix, mem_o], axis=-1) @ w_out[i]
        x = _layernorm(DEEPNORM_ALPHA * x + y, ln1_g[i], ln1_b[i])
        f = _conv_ffn(x, ffn_w_up[i], ffn_conv_w[i], ffn_conv_b[i], ffn_w_down[i])
        x = _layernorm(DEEPNORM_ALPHA * x + f, ln2_g[i], ln2_b[i])
    return x


_drawn_inputs = setup_inputs


def setup_inputs(seed=0):
    import zlib

    import numpy as np

    out = dict(_drawn_inputs(seed))
    spreads = {}
    factors = {'diff_lambda_q1': 200.0,
     'diff_lambda_k1': 3.535,
     'diff_lambda_k2': 77.971,
     'diff_subln_g': 23.081,
     'ffn_conv_b': 6.529}
    for name, (base, spread) in spreads.items():
        noise = np.random.default_rng([zlib.crc32(name.encode()), seed]).standard_normal(out[name].shape)
        drawn = base * np.exp(spread * noise) if base else spread * noise
        out[name] = __import__('jax').numpy.asarray(drawn.astype(out[name].dtype))
    for name, factor in factors.items():
        out[name] = (out[name] * factor).astype(out[name].dtype)
    return out
```

```python
import math
from contextlib import ExitStack

import numpy as np

import concourse.bass as bass
from concourse import mybir

F32 = mybir.dt.float32
F32R = mybir.dt.float32r
I32 = mybir.dt.int32
ALU = mybir.AluOpType
ACT = mybir.ActivationFunctionType
AX = mybir.AxisListType

P = 128
DEPTH = 2
S = 256
TT = S // P
D = 2048
KT = D // P
MEM_HEADS = 4
MEM_W = 512
MIX = D - MEM_W
MIX_T = MIX // P
WINDOWS = (2, 4, 8, 16)
GROUP_T = MIX_T // len(WINDOWS)
HEADS = 12
QK = 64
ROPE_HALF = 8
ROPE_THETA = 500000.0
D_FF = 5632
FF_T = D_FF // P
CHUNK = 512
PIECE = 4
SLOTS = 4
FF_CHUNKS = D_FF // CHUNK
DIFF_W = 3 * MIX + MEM_W
ALPHA = (2.0 * DEPTH) ** 0.25
LN_EPS = 1e-5
RMS_EPS = 1e-6
LAM_INIT = 0.8 - 0.6 * math.exp(-0.3 * 1)
RSQRT_MAGIC = 1597463007.0
MASKED = -1e30
PAD = max(WINDOWS)
CONV_COLS = 2 * FF_T
LN_COL = 4 * CONV_COLS
SCALE_COL = LN_COL + 4 * KT
TABLE = SCALE_COL + MIX_T


class Stream:

    def __init__(self, before, chunks, pieces, width=CHUNK):
        self.chunks, self.pieces, self.width = chunks, pieces, width
        self.first = before.first + before.chunks * before.pieces if before else 0
        self.uses = [len(range(s, pieces, SLOTS)) for s in range(SLOTS)]
        self.loads = [before.loads[s] + before.chunks * before.uses[s] if before else 0 for s in range(SLOTS)]
        self.tail = pieces % SLOTS != 0 or (before is not None and before.pieces % SLOTS != 0)

    def granule(self, c, k, j):
        return c * (self.pieces * PIECE) + ((self.first + k) * PIECE + j)

    def loaded(self, c, k):
        s = k % SLOTS
        return (c * self.uses[s] + (self.loads[s] + k // SLOTS + 1)) * 16

    def slot_split(self, c, k):
        back = 3 if self.tail and k < 3 else SLOTS
        return self.granule(c, k - back, PIECE)

    def used(self, c):
        return self.granule(c, self.pieces, 0)


class Order:

    def __init__(self, eng, sem):
        self.eng, self.sem, self.count, self.steps = eng, sem, 0, 0

    def then(self, ins):
        ins.then_inc(self.sem, 1)
        self.count = self.count + 1
        self.steps += 1

    def wait(self):
        self.eng.wait_ge(self.sem, self.count)

    def done(self, ins):
        self.then(ins)
        self.wait()


def build(nc, a):
    ctx = ExitStack()

    def sb(name, shape, dt=F32, stack=ctx):
        return stack.enter_context(nc.sbuf_tensor(name, shape, dt))

    def sem(name):
        return ctx.enter_context(nc.semaphore(name))

    raw = sb("raw", [P, SLOTS, PIECE * CHUNK])
    w_hi = sb("w_hi", [P, PIECE, CHUNK], F32R)
    w_lo = sb("w_lo", [P, PIECE, CHUNK], F32R)
    x_tok = sb("x_tok", [P, TT, D])
    conv = sb("conv", [P, 2, 2, 512])
    gb = sb("gb", [P, 2, CHUNK])
    table = sb("table", [P, DEPTH, TABLE])
    ident = sb("ident", [P, P])
    mask = sb("mask", [P, S])
    stats = sb("stats", [P, TT, 4, 6])
    mean_var = sb("mean_var", [P, TT, 2])
    rs_v = sb("rs_v", [P, 24])
    rs_y = sb("rs_y", [P, 24])
    rs_t = sb("rs_t", [P, 24])
    mx = sb("mx", [P, 16])
    sums = sb("sums", [P, 16])
    lam_in = sb("lam_in", [P, 4, QK])
    lam = sb("lam", [P, 4])
    subln = sb("subln", [P, 1])
    steps16 = sb("steps16", [P, PAD], I32)
    pool_fix = sb("pool_fix", [P, len(WINDOWS), PAD])
    pos_i = sb("pos_i", [P, TT], I32)
    trig = sb("trig", [P, 7, TT, ROPE_HALF])

    def region(name, parts):
        stack = ExitStack()
        made = [sb(f"{name}_{n}", shape, dt, stack) for n, shape, dt in parts]
        stack.close()
        return made

    split_x = ("xT", [P, KT, 2, S], F32R)
    split_dT = ("dT", [P, MIX_T, 2, S], F32R)
    xT, act = region("ffn", [split_x, ("act", [P, FF_T, 2, S], F32R)])
    _, kvbuf, qmT0, dT, mem_tok, memT = region("pool", [
        split_x, ("kv", [P, 8, 512], F32), ("qmT", [P, MEM_HEADS, S], F32), split_dT,
        ("mem", [P, TT, D], F32), ("memT", [P, KT, 2, S], F32R)])
    _, _, _, _, probs0, _, pool_h, pool_a, pool_b, rows = region("early", [
        split_x, ("kv", [P, 8, 512], F32), ("qmT", [P, MEM_HEADS, S], F32), split_dT,
        ("probs", [P, MEM_HEADS, TT, S], F32), ("rest", [P, MEM_HEADS, TT, S], F32),
        ("h", [P, 4, PAD + S], F32), ("a", [P, 4, PAD + S], F32), ("b", [P, 4, PAD + S], F32),
        ("rows", [P, DEPTH, 5, P], F32)])
    _, h_tok, qkT, qmT1, kv1, probs1, scores, attT = region("diff", [
        split_x, ("h_tok", [P, TT, DIFF_W], F32), ("qkT", [P, HEADS, 2, S], F32), ("qmT", [P, MEM_HEADS, S], F32),
        ("kv", [P, 4, 512], F32), ("probs", [P, MEM_HEADS, TT, S], F32),
        ("scores", [P, TT, 2, S], F32), ("attT", [P, TT, S], F32)])
    (out_gb,) = region("last", [("gb", [P, 2, D], F32)])
    acc = ctx.enter_context(nc.psum_tensor("acc", [P, 8, 512], F32))
    kv1_dram = nc.dram_tensor("kv1_dram", [P, 4, 512], F32, kind="Internal").ap()
    qmT = (qmT0, qmT1)
    probs = (probs0, probs1)
    kv = (kvbuf, kv1)

    def bank(b, lo, hi):
        if isinstance(b, int):
            return acc[:, b, lo:hi]
        return acc[:, bass.ds(b, 1), lo:hi].rearrange("p a n -> p (a n)")

    def stage_place(b):
        return conv[:, b // 2 % 2, b % 2, :]

    s_pool_in = Stream(None, 4, 4)
    s_kv = Stream(s_pool_in, 4, 4)
    s_pool_w = Stream(s_kv, 1, 3, MIX // 4)
    s_out0 = Stream(s_pool_w, 4, 4)
    s_up0 = Stream(s_out0, 2 * FF_CHUNKS, 4)
    s_down0 = Stream(s_up0, 4, FF_T // PIECE)
    s_diff = Stream(s_down0, DIFF_W // CHUNK, 4)
    s_out1 = Stream(s_diff, 4, 4)
    s_up1 = Stream(s_out1, 2 * FF_CHUNKS, 4)
    s_down1 = Stream(s_up1, 4, FF_T // PIECE)
    s_out, s_up, s_down = (s_out0, s_out1), (s_up0, s_up1), (s_down0, s_down1)

    piece_loaded = [sem(f"piece_loaded{s}") for s in range(SLOTS)]
    hi_made = sem("hi_made")
    lo_made = sem("lo_made")
    granule_used = sem("granule_used")

    x_loaded, mem_loaded = sem("x_loaded"), sem("mem_loaded")
    rows_loaded, small_loaded = sem("rows_loaded"), sem("small_loaded")
    ident_zero, ident_made, steps_made, pads_made = sem("ident_zero"), sem("ident_made"), sem("steps_made"), sem("pads_made")
    rows_transposed, table_made = sem("rows_transposed"), sem("table_made")
    pool_evacuated, pool_diffed, dT_hi, dT_made = sem("pool_evacuated"), sem("pool_diffed"), sem("dT_hi"), sem("dT_made")
    kv_evacuated = sem("kv_evacuated")
    kv1_stored, kv1_loaded = sem("kv1_stored"), sem("kv1_loaded")
    dve_order, pool_order = sem("dve_order"), sem("pool_order")
    out_gb_loaded = sem("out_gb_loaded")

    stages = ["x", "mem", "ln1_0", "ln2_0", "ln1_1", "pool_mix", "diff_mix", "mem_o0", "mem_o1"]
    banked = {s: sem(f"{s}_banked") for s in stages}
    scaled = {s: sem(f"{s}_scaled") for s in stages}
    hi_split = {s: sem(f"{s}_hi_split") for s in stages}
    split = {s: sem(f"{s}_split") for s in stages}

    mem_scored = [sem(f"mem_scored{l}") for l in range(2)]
    mem_shifted = [sem(f"mem_shifted{l}") for l in range(2)]
    mem_exped = [sem(f"mem_exped{l}") for l in range(2)]
    mem_probs = [sem(f"mem_probs{l}") for l in range(2)]
    mem_pT = [sem(f"mem_pT{l}") for l in range(2)]
    mem_pT_copied = [sem(f"mem_pT_copied{l}") for l in range(2)]
    resid_made = [[sem(f"resid_made{l}{n}") for n in range(2)] for l in range(2)]
    z_made = [[sem(f"z_made{l}{n}") for n in range(2)] for l in range(2)]
    gb_loaded, resid_affine = sem("gb_loaded"), sem("resid_affine")
    tap_now = [[sem(f"tap_now{l}{s}") for s in range(2)] for l in range(2)]
    conv_made = [[sem(f"conv_made{l}{s}") for s in range(2)] for l in range(2)]
    silu_made = [sem(f"silu_made{l}") for l in range(2)]
    product_made = [sem(f"product_made{l}") for l in range(2)]
    act_hi = [sem(f"act_hi{l}") for l in range(2)]
    act_made = [sem(f"act_made{l}") for l in range(2)]
    h_evacuated = [sem(f"h_evacuated{s}") for s in range(2)]
    trig_arg, trig_made = sem("trig_arg"), sem("trig_made")
    lam_sum, lam_exp, lam_made = sem("lam_sum"), sem("lam_exp"), sem("lam_made")
    rotated, qk_banked, qk_copied = sem("rotated"), sem("qk_banked"), sem("qk_copied")
    scored = [sem(f"scored{t}") for t in range(TT)]
    shifted = [sem(f"shifted{t}") for t in range(TT)]
    exped = [sem(f"exped{t}") for t in range(TT)]
    mixed = [sem(f"mixed{t}") for t in range(TT)]
    att_T = [sem(f"att_T{t}") for t in range(TT)]
    att_copied = [sem(f"att_copied{t}") for t in range(TT)]
    o_made = [sem(f"o_made{t}") for t in range(TT)]
    o_copied = [sem(f"o_copied{t}") for t in range(TT)]
    o_normed = sem("o_normed")
    out_made, out_stored = sem("out_made"), sem("out_stored")

    block = ctx.enter_context(nc.Block())

    @block.sync
    def _(sp):
        def load_chunk(st, c, rows_of, col):
            for k in range(st.pieces):
                free = st.slot_split(c, k)
                if not (isinstance(free, int) and free <= 0):
                    sp.wait_ge(lo_made, free)
                src = rows_of(k)[:, bass.ds(col, st.width)].rearrange("(j p) n -> p j n", p=P)
                dst = raw[:, k % SLOTS, :].rearrange("p (j n) -> p j n", n=CHUNK)[:, :, 0:st.width]
                sp.dma_start(dst, src).then_inc(piece_loaded[k % SLOTS], 16)

        def rows(w):
            return lambda k: w[k * PIECE * P:(k + 1) * PIECE * P, :]

        x_rows = a["x"][0].rearrange("(t p) n -> p t n", p=P)
        for c in range(4):
            sp.dma_start(x_tok[:, :, c * CHUNK:(c + 1) * CHUNK], x_rows[:, :, c * CHUNK:(c + 1) * CHUNK]).then_inc(x_loaded, 16)
        load_chunk(s_pool_in, 0, rows(a["pool_w_in"][0]), 0)
        with nc.sync.Fori(1, 4) as c:
            load_chunk(s_pool_in, c, rows(a["pool_w_in"][0]), c * CHUNK)
        for l in range(DEPTH):
            with nc.sync.Fori(0, 2) as c:
                load_chunk(s_kv, c + 2 * l, rows(a["mem_w_kv"][l]), c * CHUNK)
        load_chunk(s_pool_w, 0, rows(a["pool_w"][0].rearrange("g r n -> (g r) n")), 0)
        for l in range(DEPTH):
            if l == 1:
                with nc.sync.Fori(0, DIFF_W // CHUNK) as c:
                    load_chunk(s_diff, c, rows(a["diff_w_in"][0]), c * CHUNK)
            with nc.sync.Fori(0, 4) as c:
                load_chunk(s_out[l], c, rows(a["w_out"][l]), c * CHUNK)
            with nc.sync.Fori(0, FF_CHUNKS) as g:
                load_chunk(s_up[l], 2 * g, rows(a["ffn_w_up"][l]), g * CHUNK)
                load_chunk(s_up[l], 2 * g + 1, rows(a["ffn_w_up"][l]), g * CHUNK + D_FF)
            with nc.sync.Fori(0, 4) as c:
                load_chunk(s_down[l], c, rows(a["ffn_w_down"][l]), c * CHUNK)
        out_rows = a["out"][0].rearrange("(t p) n -> p t n", p=P)
        for n in range(4):
            t, half = n % 2, n // 2
            sp.wait_ge(out_made, n + 1)
            sp.dma_start(out_rows[:, t, half * 1024:(half + 1) * 1024],
                         x_tok[:, t, half * 1024:(half + 1) * 1024]).then_inc(out_stored, 16)
        sp.wait_ge(out_stored, 64)

    @block.gpsimd
    def _(pool):
        order = Order(pool, pool_order)
        mem_rows = a["mem"][0].rearrange("(t p) n -> p t n", p=P)
        order.then(nc.gpsimd.memset(ident[:, :], 0.0))
        order.done(nc.gpsimd.memset(mask[:, :], 0.0))
        nc.gpsimd.affine_select(out=ident[:, :], in_=ident[:, :], compare_op=ALU.not_equal, fill=1.0,
                                base=0, pattern=[[-1, P]], channel_multiplier=1).then_inc(ident_made, 1)
        nc.gpsimd.affine_select(out=mask[:, P:S], in_=mask[:, P:S], compare_op=ALU.is_ge, fill=MASKED,
                                base=0, pattern=[[-1, P]], channel_multiplier=1).then_inc(ident_made, 1)
        nc.gpsimd.iota(steps16[:, :], pattern=[[1, PAD]], base=1, channel_multiplier=0).then_inc(steps_made, 1)
        nc.gpsimd.memset(pool_h[:, :, 0:PAD], 0.0).then_inc(pads_made, 1)
        for c in range(4):
            pool.dma_start(mem_tok[:, :, c * CHUNK:(c + 1) * CHUNK], mem_rows[:, :, c * CHUNK:(c + 1) * CHUNK]).then_inc(mem_loaded, 16)

        def load_gb(l, n, c):
            for i, name in enumerate((f"ln{n + 1}_g", f"ln{n + 1}_b")):
                row = a[name][l:l + 1, bass.ds(c * CHUNK, CHUNK)]
                pool.dma_start(gb[:, i, :], row.broadcast_to([P, CHUNK])).then_inc(gb_loaded, 16)

        for n_ln, (l, n) in enumerate(((0, 0), (0, 1), (1, 0))):
            pool.wait_ge(banked[f"ln{n + 1}_{l}"], KT // 2)
            for c in range(4):
                load_gb(l, n, c)
                pool.wait_ge(gb_loaded, (c + (4 * n_ln + 1)) * 32)
                cols = x_tok[:, :, c * CHUNK:(c + 1) * CHUNK]
                g_all = gb[:, 0:1, :].broadcast_to([P, TT, CHUNK])
                b_all = gb[:, 1:2, :].broadcast_to([P, TT, CHUNK])
                order.done(nc.gpsimd.tensor_tensor(cols, cols, g_all, ALU.mult))
                nc.gpsimd.tensor_tensor(cols, cols, b_all, ALU.add).then_inc(resid_affine, 1)
                pool.wait_ge(resid_affine, c + (4 * n_ln + 1))
        pool.wait_ge(granule_used, s_up[1].used(2 * FF_CHUNKS - 1))
        for i, name in enumerate(("ln2_g", "ln2_b")):
            pool.dma_start(out_gb[:, i, :], a[name][1:2, :].broadcast_to([P, D])).then_inc(out_gb_loaded, 16)

    @block.scalar
    def _(act_e):
        def hi_piece(st, c, k):
            act_e.wait_ge(piece_loaded[k % SLOTS], st.loaded(c, k))
            for j in range(PIECE):
                free = st.granule(c, k, j) - PIECE + 1
                if not (isinstance(free, int) and free <= 0):
                    act_e.wait_ge(granule_used, free)
                nc.scalar.activation(w_hi[:, j, 0:st.width], raw[:, k % SLOTS, j * CHUNK:j * CHUNK + st.width],
                                     ACT.Copy).then_inc(hi_made, 1)

        def split_hi(stage, n_banks, dst, kt0, staged):
            for b in range(n_banks):
                to = dst[:, kt0 + 2 * b:kt0 + 2 * b + 2, 0, :]
                if staged:
                    act_e.wait_ge(scaled[stage], b + 1)
                    src = stage_place(b).rearrange("p (k s) -> p k s", k=2)
                else:
                    act_e.wait_ge(banked[stage], b + 1)
                    src = acc[:, b, :].rearrange("p (k s) -> p k s", k=2)
                nc.scalar.activation(to, src, ACT.Copy).then_inc(hi_split[stage], 1)

        def mem_attention(l):
            for h in range(MEM_HEADS):
                for t in range(TT):
                    i = h * TT + t
                    act_e.wait_ge(mem_shifted[l], h + 1)
                    nc.scalar.activation(probs[l][:, h, t, :], acc[:, h, t * S:(t + 1) * S], ACT.Exp,
                                         bias=mx[:, i:i + 1], scale=float(P) ** -0.5,
                                         accum_out=sums[:, i:i + 1]).then_inc(mem_exped[l], 1)
            for h in range(MEM_HEADS):
                act_e.wait_ge(mem_pT[l], h + 1)
                nc.scalar.activation(probs[l][:, h, :, :], acc[:, 4 + h, :].rearrange("p (m s) -> p m s", m=TT),
                                     ACT.Copy).then_inc(mem_pT_copied[l], 1)
            for h in range(MEM_HEADS):
                act_e.wait_ge(banked[f"mem_o{l}"], h + 1)
                nc.scalar.activation(xT[:, MIX_T + h, 0, :], acc[:, h, 0:S], ACT.Copy).then_inc(hi_split[f"mem_o{l}"], 1)

        def taps(l, s, g):
            act_e.wait_ge(granule_used, s_up[l].used(2 * g + s))
            if not isinstance(g, int) or g > 0:
                if s == 0:
                    act_e.wait_ge(product_made[l], g * 2)
                else:
                    act_e.wait_ge(act_made[l], g * 2)
            for b in range(2):
                for f in range(2):
                    col = g * 4 + (s * FF_T + 2 * b + f)
                    ins = nc.scalar.activation(conv[:, s, b, f * S:(f + 1) * S], acc[:, 2 * s + b, f * S:(f + 1) * S],
                                               ACT.Identity, bias=table[:, l, bass.ds(col + 3 * CONV_COLS, 1)],
                                               scale=table[:, l, bass.ds(col + 2 * CONV_COLS, 1)])
                ins.then_inc(tap_now[l][s], 1)

        def silu(l, b, g):
            act_e.wait_ge(conv_made[l][0], g * 2 + (b + 1))
            nc.scalar.activation(conv[:, 0, b, :], conv[:, 0, b, :], ACT.Silu).then_inc(silu_made[l], 1)

        def act_hi_part(l, b, g):
            act_e.wait_ge(product_made[l], g * 2 + (b + 1))
            nc.scalar.activation(act[:, bass.ds(g * 4 + 2 * b, 2), 0, :],
                                 conv[:, 1, b, :].rearrange("p (k s) -> p k s", k=2), ACT.Copy).then_inc(act_hi[l], 1)

        for l in range(DEPTH):
            vectors = [(0, a["ffn_conv_w"][l, 0]), (1, a["ffn_conv_w"][l, 1]), (2, a["ffn_conv_w"][l, 2]), (3, a["ffn_conv_b"][l])]
            for i, v in vectors:
                act_e.dma_start(rows[0:CONV_COLS, l, i, :], v.rearrange("(r n) -> r n", n=P)).then_inc(rows_loaded, 16)
            for i, name in enumerate(("ln1_g", "ln1_b", "ln2_g", "ln2_b")):
                act_e.dma_start(rows[i * KT:(i + 1) * KT, l, 4, :], a[name][l].rearrange("(r n) -> r n", n=P)).then_inc(rows_loaded, 16)
            act_e.dma_start(rows[4 * KT:4 * KT + MIX_T, l, 4, :], a["pool_scale"][0].rearrange("(r n) -> r n", n=P)).then_inc(rows_loaded, 16)
        for i, name in enumerate(("diff_lambda_q1", "diff_lambda_q2", "diff_lambda_k1", "diff_lambda_k2")):
            act_e.dma_start(lam_in[:, i, :], a[name][0:1, :].broadcast_to([P, QK])).then_inc(small_loaded, 16)
        act_e.dma_start(subln[:, :], a["diff_subln_g"].rearrange("a p -> p a")).then_inc(small_loaded, 16)
        for t in range(TT):
            act_e.dma_start(pos_i[:, t:t + 1], a["positions"][0:1, t * P:(t + 1) * P].rearrange("a p -> p a")).then_inc(small_loaded, 16)

        act_e.wait_ge(trig_arg, 1)
        nc.scalar.activation(trig[:, 0:2, :, :].rearrange("p a t n -> p (a t n)"),
                             trig[:, 2:4, :, :].rearrange("p a t n -> p (a t n)"), ACT.Sin).then_inc(trig_made, 1)
        act_e.wait_ge(lam_sum, 1)
        nc.scalar.activation(lam[:, 2:4], lam[:, 0:2], ACT.Exp).then_inc(lam_exp, 1)

        split_hi("x", KT // 2, xT, 0, staged=False)
        for c in range(5):
            if c < 4:
                hi_piece(s_pool_in, c, 0)
            if c > 0:
                act_e.wait_ge(granule_used, s_pool_in.used(c - 1))
                for b in range(2):
                    src = acc[:, 2 * (c - 1) + b, :].rearrange("p (k s) -> p k s", k=2)
                    if c < 4:
                        if c > 1:
                            act_e.wait_ge(dT_made, c - 1)
                        to = pool_h[:, 2 * b:2 * b + 2, PAD:PAD + S]
                    else:
                        to = qmT0[:, 2 * b:2 * b + 2, :]
                    nc.scalar.activation(to, src, ACT.Copy).then_inc(pool_evacuated, 1)
                if c < 4:
                    hi_piece(s_pool_in, c, 1)
                    act_e.wait_ge(pool_diffed, c)
                    nc.scalar.activation(dT[:, 4 * (c - 1):4 * c, 0, :], pool_h[:, :, PAD:PAD + S], ACT.Copy).then_inc(dT_hi, 1)
            elif c < 4:
                hi_piece(s_pool_in, c, 1)
            if c < 4:
                hi_piece(s_pool_in, c, 2)
                hi_piece(s_pool_in, c, 3)

        split_hi("mem", KT // 2, memT, 0, staged=False)

        def kv_out(c):
            act_e.wait_ge(granule_used, s_kv.used(c))
            nc.scalar.activation(kvbuf[:, bass.ds(c * 2, 2), :], acc[:, bass.ds(c * 2, 2), :], ACT.Copy).then_inc(kv_evacuated, 1)

        def kv_chunk(c, first):
            hi_piece(s_kv, c, 0)
            if not first:
                kv_out(c - 1)
            for k in range(1, 4):
                hi_piece(s_kv, c, k)

        kv_chunk(0, True)
        with nc.scalar.Fori(1, 4) as c:
            kv_chunk(c, False)
        kv_out(3)
        act_e.wait_ge(kv_evacuated, 4)
        act_e.dma_start(kv1_dram[:, :, :], kvbuf[:, 4:8, :]).then_inc(kv1_stored, 16)

        for l in range(DEPTH):
            if l == 0:
                mem_attention(0)
                for k in range(3):
                    hi_piece(s_pool_w, 0, k)
                split_hi("pool_mix", MIX_T // 2, xT, 0, staged=True)
            else:
                def h_out(c, s):
                    act_e.wait_ge(granule_used, s_diff.used(2 * c + s))
                    nc.scalar.activation(h_tok[:, :, bass.ds(c * (2 * CHUNK) + s * CHUNK, CHUNK)],
                                         acc[:, 2 * s:2 * s + 2, :], ACT.Copy).then_inc(h_evacuated[s], 1)

                def diff_chunks(c, first):
                    hi_piece(s_diff, 2 * c, 0)
                    if not first:
                        h_out(c - 1, 1)
                    for k in range(1, 4):
                        hi_piece(s_diff, 2 * c, k)
                    hi_piece(s_diff, 2 * c + 1, 0)
                    h_out(c, 0)
                    for k in range(1, 4):
                        hi_piece(s_diff, 2 * c + 1, k)

                split_hi("ln2_0", KT // 2, xT, 0, staged=True)
                act_e.wait_ge(granule_used, s_down[0].used(3))
                act_e.wait_ge(kv1_stored, 16)
                act_e.dma_start(kv1[:, :, :], kv1_dram[:, :, :]).then_inc(kv1_loaded, 16)
                diff_chunks(0, True)
                with nc.scalar.Fori(1, 5) as c:
                    diff_chunks(c, False)
                h_out(4, 1)
                for n in range(HEADS + 2):
                    act_e.wait_ge(qk_banked, n + 1)
                    src = acc[:, n % 8, :].rearrange("p (k s) -> p k s", k=2)
                    to = qkT[:, n, :, :] if n < HEADS else qmT1[:, 2 * (n - HEADS):2 * (n - HEADS) + 2, :]
                    nc.scalar.activation(to, src, ACT.Copy).then_inc(qk_copied, 1)
                mem_attention(1)
                with nc.scalar.Fori(0, HEADS) as h:
                    for t in range(TT):
                        keys = (t + 1) * P
                        act_e.wait_ge(shifted[t], h + 1)
                        for c in range(2):
                            i = 2 * t + c
                            ins = nc.scalar.activation(scores[:, t, c, 0:keys], scores[:, t, c, 0:keys], ACT.Exp,
                                                       bias=mx[:, i:i + 1], scale=float(QK) ** -0.5,
                                                       accum_out=sums[:, i:i + 1])
                            ins.then_inc(exped[t], 1)
                    for t in range(TT):
                        keys = (t + 1) * P
                        act_e.wait_ge(att_T[t], h + 1)
                        nc.scalar.activation(attT[:, t, 0:keys], acc[:, 4 + t, 0:keys], ACT.Copy).then_inc(att_copied[t], 1)
                    for t in range(TT):
                        act_e.wait_ge(o_made[t], h + 1)
                        nc.scalar.activation(h_tok[:, t, bass.ds(h * P, P)], acc[:, 6 + t, 0:P], ACT.Copy).then_inc(o_copied[t], 1)
                split_hi("diff_mix", MIX_T // 2, xT, 0, staged=True)
            with nc.scalar.Fori(0, 4) as c:
                for k in range(4):
                    hi_piece(s_out[l], c, k)
            split_hi(f"ln1_{l}", KT // 2, xT, 0, staged=True)

            if l == 0:
                act_e.wait_ge(kv1_stored, 16)
            def ffn_pair(g, first):
                hi_piece(s_up[l], 2 * g, 0)
                if not first:
                    taps(l, 1, g - 1)
                hi_piece(s_up[l], 2 * g, 1)
                if not first:
                    act_hi_part(l, 0, g - 1)
                hi_piece(s_up[l], 2 * g, 2)
                if not first:
                    act_hi_part(l, 1, g - 1)
                hi_piece(s_up[l], 2 * g, 3)
                hi_piece(s_up[l], 2 * g + 1, 0)
                taps(l, 0, g)
                hi_piece(s_up[l], 2 * g + 1, 1)
                silu(l, 0, g)
                hi_piece(s_up[l], 2 * g + 1, 2)
                silu(l, 1, g)
                hi_piece(s_up[l], 2 * g + 1, 3)

            ffn_pair(0, True)
            with nc.scalar.Fori(1, FF_CHUNKS) as g:
                ffn_pair(g, False)
            last = FF_CHUNKS - 1
            hi_piece(s_down[l], 0, 0)
            taps(l, 1, last)
            hi_piece(s_down[l], 0, 1)
            act_hi_part(l, 0, last)
            hi_piece(s_down[l], 0, 2)
            act_hi_part(l, 1, last)
            for k in range(3, FF_T // PIECE):
                hi_piece(s_down[l], 0, k)
            with nc.scalar.Fori(1, 4) as c:
                for k in range(FF_T // PIECE):
                    hi_piece(s_down[l], c, k)

    @block.vector
    def _(dve):
        order = Order(dve, dve_order)

        def loop(start, end, per, body):
            before, steps = order.count, order.steps
            with nc.vector.Fori(start, end) as i:
                order.count = before + (i - start) * per
                body(i)
                assert order.steps - steps == per, (order.steps - steps, per)
            order.count = before + (end - start) * per

        def lo_piece(st, c, k):
            for j in range(PIECE):
                dve.wait_ge(hi_made, st.granule(c, k, j) + 1)
                nc.vector.tensor_tensor(w_lo[:, j, 0:st.width], raw[:, k % SLOTS, j * CHUNK:j * CHUNK + st.width],
                                        w_hi[:, j, 0:st.width].bitcast(F32), ALU.subtract).then_inc(lo_made, 1)

        def two(ap):
            return ap.rearrange("p (k s) -> p k s", k=2)

        def split_lo(stage, n_banks, dst, kt0, gain=None, bias=None, filled=None):
            staged = gain is not None

            def scale(b):
                if filled:
                    dve.wait_ge(granule_used, filled(b))
                else:
                    dve.wait_ge(banked[stage], b + 1)
                if b >= 4:
                    dve.wait_ge(split[stage], b - 3)
                for f in range(2):
                    i = 2 * b + f
                    args = (bias(i), ALU.mult, ALU.add) if bias else (1.0, ALU.mult, ALU.mult)
                    ins = nc.vector.tensor_scalar(stage_place(b)[:, f * S:(f + 1) * S], acc[:, b, f * S:(f + 1) * S],
                                                  gain(i), *args)
                ins.then_inc(scaled[stage], 1)

            if staged:
                scale(0)
            for b in range(n_banks):
                if staged and b + 1 < n_banks:
                    scale(b + 1)
                dve.wait_ge(hi_split[stage], b + 1)
                src = two(stage_place(b)) if staged else two(acc[:, b, :])
                kts = slice(kt0 + 2 * b, kt0 + 2 * b + 2)
                nc.vector.tensor_tensor(dst[:, kts, 1, :], src, dst[:, kts, 0, :].bitcast(F32),
                                        ALU.subtract).then_inc(split[stage], 1)

        def rsqrt(n):
            v, y, t = rs_v[:, 0:n], rs_y[:, 0:n], rs_t[:, 0:n]
            order.done(nc.vector.tensor_scalar(y.bitcast(I32), v.bitcast(I32), -0.5, RSQRT_MAGIC, ALU.mult, ALU.add))
            for _ in range(4):
                order.done(nc.vector.tensor_tensor(t, y, y, ALU.mult))
                order.done(nc.vector.tensor_tensor(t, t, v, ALU.mult))
                order.done(nc.vector.tensor_scalar(t, t, -0.5, 1.5, ALU.mult, ALU.add))
                order.done(nc.vector.tensor_tensor(y, y, t, ALU.mult))

        def resid_out(l, n, st, c):
            dve.wait_ge(granule_used, st.used(c))
            for t in range(TT):
                cols = x_tok[:, t, bass.ds(c * CHUNK, CHUNK)]
                order.then(nc.vector.scalar_tensor_tensor(cols, cols, ALPHA, bank(2 * c + t, 0, CHUNK), ALU.mult, ALU.add))
            order.wait()
            for t in range(TT):
                order.then(nc.vector.bn_stats(stats[:, t, bass.ds(c, 1), :].rearrange("p a n -> p (a n)"), x_tok[:, t, bass.ds(c * CHUNK, CHUNK)]))

        def proj_chunk(l, n, st, c):
            lo_piece(st, c, 0)
            resid_out(l, n, st, c - 1)
            for k in range(1, st.pieces):
                lo_piece(st, c, k)

        def norm_stats():
            order.wait()
            for t in range(TT):
                order.then(nc.vector.bn_aggr(mean_var[:, t, :], stats[:, t, :, :]))
            order.wait()
            order.done(nc.vector.tensor_scalar(rs_v[:, 0:TT], mean_var[:, :, 1], LN_EPS, None, ALU.add))
            rsqrt(TT)

        def norm_z(l, n):
            norm_stats()
            for half in range(2):
                for t in range(TT):
                    cols = x_tok[:, t, half * 1024:(half + 1) * 1024]
                    nc.vector.tensor_scalar(cols, cols, mean_var[:, t, 0:1], rs_y[:, t:t + 1],
                                            ALU.subtract, ALU.mult).then_inc(z_made[l][n], 1)

        def ln_split(l, n):
            norm_z(l, n)
            g0 = LN_COL + 2 * n * KT
            split_lo(f"ln{n + 1}_{l}", KT // 2, xT, 0, gain=lambda i: table[:, l, g0 + i:g0 + i + 1],
                     bias=lambda i: table[:, l, g0 + KT + i:g0 + KT + i + 1])

        def mem_attention(l):
            for h in range(MEM_HEADS):
                dve.wait_ge(mem_scored[l], h + 1)
                order.done(nc.vector.tensor_reduce(mx[:, 8 + 2 * h:10 + 2 * h], two(acc[:, h, :]), AX.X, ALU.max))
                nc.vector.tensor_scalar(mx[:, 2 * h:2 * h + 2], mx[:, 8 + 2 * h:10 + 2 * h], -float(P) ** -0.5, None,
                                        ALU.mult).then_inc(mem_shifted[l], 1)
            for h in range(MEM_HEADS):
                dve.wait_ge(mem_exped[l], 2 * h + 2)
                order.done(nc.vector.reciprocal(sums[:, 8 + 2 * h:10 + 2 * h], sums[:, 2 * h:2 * h + 2]))
                for t in range(TT):
                    i = 8 + 2 * h + t
                    ins = nc.vector.tensor_scalar(probs[l][:, h, t, :], probs[l][:, h, t, :], sums[:, i:i + 1], None, ALU.mult)
                ins.then_inc(mem_probs[l], 1)
            for h in range(MEM_HEADS):
                dve.wait_ge(hi_split[f"mem_o{l}"], h + 1)
                nc.vector.tensor_tensor(xT[:, MIX_T + h, 1, :], acc[:, h, 0:S], xT[:, MIX_T + h, 0, :].bitcast(F32),
                                        ALU.subtract).then_inc(split[f"mem_o{l}"], 1)

        def conv_bank(l, s, b, g):
            dve.wait_ge(tap_now[l][s], g * 2 + (b + 1))
            for lag in (1, 2):
                for f in range(2):
                    col = g * 4 + (s * FF_T + 2 * b + f + (2 - lag) * CONV_COLS)
                    to = conv[:, s, b, f * S + lag:(f + 1) * S]
                    ins = nc.vector.scalar_tensor_tensor(to, acc[:, 2 * s + b, f * S:(f + 1) * S - lag],
                                                         table[:, l, bass.ds(col, 1)], to, ALU.mult, ALU.add)
                    if lag == 1:
                        order.then(ins)
                if lag == 1:
                    order.wait()
            ins.then_inc(conv_made[l][s], 1)

        def product(l, b, g):
            dve.wait_ge(silu_made[l], g * 2 + (b + 1))
            dve.wait_ge(conv_made[l][1], g * 2 + (b + 1))
            nc.vector.tensor_tensor(conv[:, 1, b, :], conv[:, 1, b, :], conv[:, 0, b, :], ALU.mult).then_inc(product_made[l], 1)

        def act_lo_part(l, b, g):
            dve.wait_ge(act_hi[l], g * 2 + (b + 1))
            kts = bass.ds(g * 4 + 2 * b, 2)
            nc.vector.tensor_tensor(act[:, kts, 1, :], two(conv[:, 1, b, :]), act[:, kts, 0, :].bitcast(F32),
                                    ALU.subtract).then_inc(act_made[l], 1)

        dve.wait_ge(steps_made, 1)
        for g, w in enumerate(WINDOWS):
            order.then(nc.vector.tensor_scalar(pool_fix[:, g, :], steps16[:, :], float(w), None, ALU.min))
        order.wait()
        order.done(nc.vector.reciprocal(pool_fix[:, :, :], pool_fix[:, :, :]))
        for g, w in enumerate(WINDOWS):
            order.then(nc.vector.tensor_scalar(pool_fix[:, g, :], pool_fix[:, g, :], float(w), None, ALU.mult))

        dve.wait_ge(small_loaded, 7 * 16)
        pos_f, ang, turn, part = trig[:, 6, :, 0:1], trig[:, 4, :, :], trig[:, 5, :, :], trig[:, 6, :, :]
        order.done(nc.vector.tensor_copy(pos_f, pos_i[:, :].rearrange("p (t a) -> p t a", a=1)))
        for n in range(ROPE_HALF):
            freq = float(np.float32(ROPE_THETA) ** np.float32(-2.0 * n / (2 * ROPE_HALF)))
            order.then(nc.vector.tensor_scalar(trig[:, 4, :, n:n + 1], pos_f, freq, None, ALU.mult))
        order.wait()
        two_pi, parts = 2 * math.pi, []
        rest = two_pi
        for bits in (7, 14, 21, 28, 36, 48):
            step = 2.0 ** (3 - bits)
            parts.append(math.floor(rest / step) * step)
            rest -= parts[-1]
        whole = 1.5 * 2.0 ** 23
        for turns in (4096.0, 1.0):
            order.done(nc.vector.tensor_scalar(turn, ang, 1.0 / (two_pi * turns), None, ALU.mult))
            order.done(nc.vector.tensor_scalar(turn, turn, whole, None, ALU.add))
            order.done(nc.vector.tensor_scalar(turn, turn, whole, None, ALU.subtract))
            for p_ in parts:
                order.done(nc.vector.tensor_scalar(part, turn, -p_ * turns, None, ALU.mult))
                order.done(nc.vector.tensor_tensor(ang, ang, part, ALU.add))
        pi = float(np.nextafter(np.float32(math.pi), np.float32(0)))
        order.done(nc.vector.tensor_scalar(trig[:, 3, :, :], ang, pi, -pi, ALU.min, ALU.max))
        order.done(nc.vector.tensor_scalar(part, trig[:, 3, :, :], -1.0, None, ALU.mult))
        order.done(nc.vector.tensor_tensor(part, part, trig[:, 3, :, :], ALU.max))
        nc.vector.tensor_scalar(trig[:, 2, :, :], part, -1.0, math.pi / 2, ALU.mult, ALU.add).then_inc(trig_arg, 1)

        order.done(nc.vector.tensor_tensor(lam_in[:, 0:2, :], lam_in[:, 0:2, :], lam_in[:, 2:4, :], ALU.mult))
        nc.vector.tensor_reduce(lam[:, 0:2], lam_in[:, 0:2, :], AX.X, ALU.add).then_inc(lam_sum, 1)
        dve.wait_ge(lam_exp, 1)
        order.done(nc.vector.tensor_tensor(lam[:, 0:1], lam[:, 2:3], lam[:, 3:4], ALU.subtract))
        order.done(nc.vector.tensor_scalar(lam[:, 0:1], lam[:, 0:1], LAM_INIT, None, ALU.add))
        order.done(nc.vector.tensor_scalar(subln[:, :], subln[:, :], 1.0 - LAM_INIT, None, ALU.mult))

        for l in range(DEPTH):
            dve.wait_ge(rows_transposed, l + 1)
            nc.vector.tensor_copy(table[:, l, :], acc[:, l, 0:TABLE]).then_inc(table_made, 1)

        split_lo("x", KT // 2, xT, 0)

        def pooled(c):
            dve.wait_ge(pool_evacuated, 2 * (c + 1))
            if c == 0:
                dve.wait_ge(pads_made, 1)
            runs, f = [], 0
            while f < 4:
                g = (4 * c + f) // GROUP_T
                n = min(4 - f, GROUP_T * (g + 1) - (4 * c + f))
                runs.append((f, n, g))
                f += n
            for f, n, g in runs:
                fs, src, dst, reach = slice(f, f + n), pool_h, pool_a, 1
                while reach < WINDOWS[g]:
                    lo = 2 * reach - 1
                    order.done(nc.vector.tensor_tensor(dst[:, fs, lo:], src[:, fs, lo:], src[:, fs, lo - reach:PAD + S - reach], ALU.add))
                    src, dst, reach = dst, (pool_b if dst is pool_a else pool_a), 2 * reach
                head = src[:, fs, PAD:2 * PAD]
                order.done(nc.vector.tensor_tensor(head, head, pool_fix[:, g:g + 1, :].broadcast_to([P, n, PAD]), ALU.mult))
                ins = nc.vector.scalar_tensor_tensor(pool_h[:, fs, PAD:PAD + S], src[:, fs, PAD:PAD + S], 1.0 / WINDOWS[g],
                                                     pool_h[:, fs, PAD:PAD + S], ALU.mult, ALU.subtract)
            ins.then_inc(pool_diffed, 1)

        for c in range(4):
            lo_piece(s_pool_in, c, 0)
            if c > 0:
                pooled(c - 1)
            lo_piece(s_pool_in, c, 1)
            if c > 0:
                dve.wait_ge(dT_hi, c)
                dve.wait_ge(pool_diffed, c)
                nc.vector.tensor_tensor(dT[:, 4 * (c - 1):4 * c, 1, :], pool_h[:, :, PAD:PAD + S],
                                        dT[:, 4 * (c - 1):4 * c, 0, :].bitcast(F32), ALU.subtract).then_inc(dT_made, 1)
            lo_piece(s_pool_in, c, 2)
            lo_piece(s_pool_in, c, 3)

        split_lo("mem", KT // 2, memT, 0)

        def kv_chunk(c):
            for k in range(4):
                lo_piece(s_kv, c, k)

        loop(0, 4, 0, kv_chunk)

        for l in range(DEPTH):
            if l == 0:
                mem_attention(0)
                for k in range(3):
                    lo_piece(s_pool_w, 0, k)
                split_lo("pool_mix", MIX_T // 2, xT, 0, gain=lambda i: table[:, 0, SCALE_COL + i:SCALE_COL + i + 1],
                         filled=lambda b: s_pool_w.granule(0, 0, GROUP_T * ((2 * b + 1) // GROUP_T + 1)))
            else:
                def diff_chunk(c):
                    for k in range(4):
                        lo_piece(s_diff, c, k)

                loop(0, DIFF_W // CHUNK, 0, diff_chunk)
                dve.wait_ge(h_evacuated[0], 5)
                dve.wait_ge(h_evacuated[1], 5)
                dve.wait_ge(trig_made, 1)
                for t in range(TT):
                    v = h_tok[:, t, 0:2 * MIX].rearrange("p (h n) -> p h n", n=QK)
                    x1, x2 = v[:, :, 0:ROPE_HALF], v[:, :, ROPE_HALF:2 * ROPE_HALF]
                    n = 4 * HEADS
                    cos = trig[:, 0, t:t + 1, :].broadcast_to([P, n, ROPE_HALF])
                    sin = trig[:, 1, t:t + 1, :].broadcast_to([P, n, ROPE_HALF])
                    tmp = [scores[:, :, :, :].rearrange("p a b s -> p (a b s)")[:, i * 384:i * 384 + 384].rearrange("p (h n) -> p h n", n=ROPE_HALF)
                           for i in range(2)]
                    tmp += [probs1[:, 0:2, :, :].rearrange("p a b s -> p (a b s)")[:, i * 384:i * 384 + 384].rearrange("p (h n) -> p h n", n=ROPE_HALF)
                            for i in range(2)]
                    if t > 0:
                        dve.wait_ge(rotated, 2 * t)
                    order.then(nc.vector.tensor_tensor(tmp[0], x1, cos, ALU.mult))
                    order.then(nc.vector.tensor_tensor(tmp[1], x2, sin, ALU.mult))
                    order.then(nc.vector.tensor_tensor(tmp[2], x2, cos, ALU.mult))
                    order.done(nc.vector.tensor_tensor(tmp[3], x1, sin, ALU.mult))
                    nc.vector.tensor_tensor(x1, tmp[0], tmp[1], ALU.subtract).then_inc(rotated, 1)
                    nc.vector.tensor_tensor(x2, tmp[2], tmp[3], ALU.add).then_inc(rotated, 1)
                mem_attention(1)

                def head(h):
                    for t in range(TT):
                        keys = (t + 1) * P
                        dve.wait_ge(scored[t], h + 1)
                        s_all = scores[:, t, :, 0:keys]
                        dve.wait_ge(att_T[t], h)
                        order.done(nc.vector.tensor_tensor(s_all, acc[:, 2 * t:2 * t + 2, 0:keys],
                                                           mask[:, S - keys:S].rearrange("p (a s) -> p a s", a=1).broadcast_to([P, 2, keys]), ALU.add))
                        order.done(nc.vector.tensor_reduce(mx[:, 4 + 2 * t:6 + 2 * t], s_all, AX.X, ALU.max))
                        nc.vector.tensor_scalar(mx[:, 2 * t:2 * t + 2], mx[:, 4 + 2 * t:6 + 2 * t], -float(QK) ** -0.5, None,
                                                ALU.mult).then_inc(shifted[t], 1)
                    for t in range(TT):
                        keys = (t + 1) * P
                        dve.wait_ge(exped[t], h * 2 + 2)
                        r = 4 + 2 * t
                        order.done(nc.vector.reciprocal(sums[:, r:r + 2], sums[:, 2 * t:2 * t + 2]))
                        order.done(nc.vector.tensor_scalar(sums[:, r + 1:r + 2], sums[:, r + 1:r + 2], lam[:, 0:1], None, ALU.mult))
                        order.done(nc.vector.tensor_scalar(scores[:, t, 1, 0:keys], scores[:, t, 1, 0:keys], sums[:, r + 1:r + 2], None, ALU.mult))
                        nc.vector.scalar_tensor_tensor(scores[:, t, 0, 0:keys], scores[:, t, 0, 0:keys], sums[:, r:r + 1],
                                                       scores[:, t, 1, 0:keys], ALU.mult, ALU.subtract).then_inc(mixed[t], 1)

                loop(0, HEADS, 2 * TT + 3 * TT, head)
                for t in range(TT):
                    dve.wait_ge(o_copied[t], HEADS)
                for t in range(TT):
                    order.then(nc.vector.tensor_tensor(h_tok[:, t, MIX:2 * MIX], h_tok[:, t, 0:MIX], h_tok[:, t, 0:MIX], ALU.mult))
                order.wait()
                for t in range(TT):
                    order.then(nc.vector.tensor_reduce(rs_v[:, t * HEADS:(t + 1) * HEADS], h_tok[:, t, MIX:2 * MIX].rearrange("p (h n) -> p h n", n=P), AX.X, ALU.add))
                order.wait()
                order.done(nc.vector.tensor_scalar(rs_v[:, :], rs_v[:, :], 1.0 / P, RMS_EPS, ALU.mult, ALU.add))
                rsqrt(TT * HEADS)
                for t in range(TT):
                    o = h_tok[:, t, 0:MIX].rearrange("p (h n) -> p h n", n=P)
                    r = rs_y[:, t * HEADS:(t + 1) * HEADS].rearrange("p (h a) -> p h a", a=1).broadcast_to([P, HEADS, P])
                    nc.vector.tensor_tensor(o, o, r, ALU.mult).then_inc(o_normed, 1)
                split_lo("diff_mix", MIX_T // 2, xT, 0, gain=lambda i: subln[:, 0:1])

            for k in range(4):
                lo_piece(s_out[l], 0, k)
            if l > 0:
                dve.wait_ge(resid_affine, 8)
            loop(1, 4, 4, lambda c: proj_chunk(l, 0, s_out[l], c))
            resid_out(l, 0, s_out[l], 3)
            ln_split(l, 0)

            def ffn_pair(g, first):
                lo_piece(s_up[l], 2 * g, 0)
                if not first:
                    conv_bank(l, 1, 0, g - 1)
                lo_piece(s_up[l], 2 * g, 1)
                if not first:
                    conv_bank(l, 1, 1, g - 1)
                    product(l, 0, g - 1)
                lo_piece(s_up[l], 2 * g, 2)
                if not first:
                    product(l, 1, g - 1)
                    act_lo_part(l, 0, g - 1)
                lo_piece(s_up[l], 2 * g, 3)
                if not first:
                    act_lo_part(l, 1, g - 1)
                lo_piece(s_up[l], 2 * g + 1, 0)
                conv_bank(l, 0, 0, g)
                lo_piece(s_up[l], 2 * g + 1, 1)
                conv_bank(l, 0, 1, g)
                lo_piece(s_up[l], 2 * g + 1, 2)
                lo_piece(s_up[l], 2 * g + 1, 3)

            ffn_pair(0, True)
            loop(1, FF_CHUNKS, 8, lambda g: ffn_pair(g, False))
            last = FF_CHUNKS - 1
            lo_piece(s_down[l], 0, 0)
            conv_bank(l, 1, 0, last)
            lo_piece(s_down[l], 0, 1)
            conv_bank(l, 1, 1, last)
            product(l, 0, last)
            lo_piece(s_down[l], 0, 2)
            product(l, 1, last)
            act_lo_part(l, 0, last)
            lo_piece(s_down[l], 0, 3)
            act_lo_part(l, 1, last)
            for k in range(4, FF_T // PIECE):
                lo_piece(s_down[l], 0, k)
            dve.wait_ge(resid_affine, 8 * l + 4)
            loop(1, 4, 4, lambda c: proj_chunk(l, 1, s_down[l], c))
            resid_out(l, 1, s_down[l], 3)
            if l == 0:
                ln_split(0, 1)
        norm_stats()
        dve.wait_ge(out_gb_loaded, 32)
        for half in range(2):
            for t in range(TT):
                cs = slice(half * 1024, (half + 1) * 1024)
                cols = x_tok[:, t, cs]
                order.done(nc.vector.scalar_tensor_tensor(cols, cols, mean_var[:, t, 0:1], out_gb[:, 0, cs], ALU.subtract, ALU.mult))
                nc.vector.scalar_tensor_tensor(cols, cols, rs_y[:, t:t + 1], out_gb[:, 1, cs], ALU.mult, ALU.add).then_inc(out_made, 1)

    @block.tensor
    def _(pe):
        def product3(out, w, x, start, stop):
            pe.matmul(out, w[0], x[0], start=start, stop=False, skip_group_check=True)
            pe.matmul(out, w[0], x[1], start=False, stop=False, skip_group_check=True)
            return pe.matmul(out, w[1], x[0], start=False, stop=stop, skip_group_check=True)

        def features_chunk(st, c, src, bank0, ready=None):
            for k in range(4):
                for j in range(PIECE):
                    kt = PIECE * k + j
                    if ready is not None and kt % 2 == 0:
                        pe.wait_ge(ready, max(2, kt // 2 + 1))
                    pe.wait_ge(lo_made, st.granule(c, k, j) + 1)
                    for f in range(4):
                        fs = slice(f * P, (f + 1) * P)
                        ins = product3(bank(bank0 + f // 2, (f % 2) * S, (f % 2 + 1) * S), (w_hi[:, j, fs], w_lo[:, j, fs]),
                                       (src[:, kt, 0, :], src[:, kt, 1, :]), kt == 0 and f % 2 == 0, kt == KT - 1)
                    ins.then_inc(granule_used, 1)

        def tokens_chunk(st, c, src, bank0, ready=None, last_ready=None):
            n = st.pieces * PIECE
            for k in range(st.pieces):
                for j in range(PIECE):
                    kt = PIECE * k + j
                    if ready is not None and kt % 2 == 0:
                        pe.wait_ge(ready, max(4, kt // 2 + 1))
                    if last_ready is not None and kt % 2 == 0:
                        pe.wait_ge(last_ready, kt // 2 + 1)
                    pe.wait_ge(lo_made, st.granule(c, k, j) + 1)
                    for t in range(TT):
                        ts = slice(t * P, (t + 1) * P)
                        ins = product3(bank(bank0 + t, 0, CHUNK), (src[:, kt, 0, ts], src[:, kt, 1, ts]),
                                       (w_hi[:, j, :], w_lo[:, j, :]), kt == 0, kt == n - 1)
                    ins.then_inc(granule_used, 1)

        def to_features(stage, n_banks, src, need=None):
            for b in range(n_banks):
                if need is not None:
                    need(b)
                for i in range(2):
                    for t in range(TT):
                        kt = 2 * b + i
                        ins = pe.transpose(acc[:, b, i * S + t * P:i * S + (t + 1) * P], src[:, t, kt * P:(kt + 1) * P], ident[:, :])
                ins.then_inc(banked[stage], 1)

        def mem_attention(l):
            q, kvb, pr = qmT[l], kv[l], probs[l]
            for h in range(MEM_HEADS):
                for t in range(TT):
                    ins = pe.matmul(acc[:, h, t * S:(t + 1) * S], q[:, h, t * P:(t + 1) * P],
                                    kvb[:, h // 2, (h % 2) * S:(h % 2 + 1) * S], start=True, stop=True)
                ins.then_inc(mem_scored[l], 1)
            for h in range(MEM_HEADS):
                pe.wait_ge(mem_probs[l], h + 1)
                for m in range(TT):
                    for t in range(TT):
                        ins = pe.transpose(acc[:, 4 + h, m * S + t * P:m * S + (t + 1) * P], pr[:, h, t, m * P:(m + 1) * P], ident[:, :])
                ins.then_inc(mem_pT[l], 1)
            for h in range(MEM_HEADS):
                pe.wait_ge(mem_pT_copied[l], h + 1)
                for m in range(TT):
                    ins = pe.matmul(acc[:, h, 0:S], kvb[:, 2 + m, h * P:(h + 1) * P], pr[:, h, m, :], start=m == 0, stop=m == TT - 1)
                ins.then_inc(banked[f"mem_o{l}"], 1)

        pe.wait_ge(ident_made, 2)
        pe.wait_ge(rows_loaded, 16 * 18)
        for l in range(DEPTH):
            for i in range(4):
                pe.transpose(acc[:, l, i * CONV_COLS:(i + 1) * CONV_COLS], rows[0:CONV_COLS, l, i, :], ident[0:CONV_COLS, 0:CONV_COLS])
            n = TABLE - LN_COL
            pe.transpose(acc[:, l, LN_COL:TABLE], rows[0:n, l, 4, :], ident[0:n, 0:n]).then_inc(rows_transposed, 1)
        pe.wait_ge(table_made, 2)
        pe.wait_ge(x_loaded, 64)
        to_features("x", KT // 2, x_tok)
        with nc.tensor.Fori(0, 4) as c:
            features_chunk(s_pool_in, c, xT, c * 2, ready=split["x"])

        pe.wait_ge(mem_loaded, 64)
        pe.wait_ge(dT_made, 3)
        to_features("mem", KT // 2, mem_tok, lambda b: pe.wait_ge(pool_evacuated, 8) if b == 0 else None)
        with nc.tensor.Fori(0, 2) as l2:
            features_chunk(s_kv, l2 * 2, memT, l2 * 4, ready=split["mem"])
            tokens_chunk(s_kv, l2 * 2 + 1, memT, l2 * 4 + 2)

        for l in range(DEPTH):
            if l == 0:
                pe.wait_ge(kv_evacuated, 4)
                mem_attention(0)
                pe.wait_ge(split["mem_o0"], MEM_HEADS)
                for k in range(3):
                    for j in range(PIECE):
                        kt = PIECE * k + j
                        g = kt // GROUP_T
                        pe.wait_ge(lo_made, s_pool_w.granule(0, k, j) + 1)
                        for f in range(GROUP_T):
                            ft = GROUP_T * g + f
                            fs = slice(f * P, (f + 1) * P)
                            ins = product3(acc[:, ft // 2, (ft % 2) * S:(ft % 2 + 1) * S], (w_hi[:, j, fs], w_lo[:, j, fs]),
                                           (dT[:, kt, 0, :], dT[:, kt, 1, :]), kt % GROUP_T == 0 and ft % 2 == 0, kt % GROUP_T == GROUP_T - 1)
                        ins.then_inc(granule_used, 1)
                pe.wait_ge(split["pool_mix"], MIX_T // 2)
                with nc.tensor.Fori(0, 4) as c:
                    tokens_chunk(s_out[0], c, xT, c * 2)
            else:
                with nc.tensor.Fori(0, DIFF_W // CHUNK // 2) as c:
                    for s in range(2):
                        pe.wait_ge(h_evacuated[s], c)
                        tokens_chunk(s_diff, c * 2 + s, xT, 2 * s, ready=split["ln2_0"] if s == 0 else None)
                pe.wait_ge(rotated, 4)
                for n in range(HEADS + 2):
                    if n >= 8:
                        pe.wait_ge(qk_copied, n - 7)
                    for i in range(2):
                        col = i * MIX + n * P if n < HEADS else 3 * MIX + (2 * (n - HEADS) + i) * P
                        for t in range(TT):
                            ins = pe.transpose(acc[:, n % 8, i * S + t * P:i * S + (t + 1) * P], h_tok[:, t, col:col + P], ident[:, :])
                    ins.then_inc(qk_banked, 1)
                pe.wait_ge(qk_copied, HEADS + 2)
                pe.wait_ge(kv1_loaded, 16)
                mem_attention(1)
                pe.wait_ge(split["mem_o1"], MEM_HEADS)

                def score(h, t):
                    if h > 0:
                        pe.wait_ge(shifted[t], h)
                    for c in range(2):
                        rows_c = slice(c * QK, (c + 1) * QK)
                        ins = pe.matmul(acc[:, 2 * t + c, 0:(t + 1) * P], qkT[rows_c, h, 0, t * P:(t + 1) * P],
                                        qkT[rows_c, h, 1, 0:(t + 1) * P], start=True, stop=True)
                    ins.then_inc(scored[t], 1)

                for t in range(TT):
                    score(0, t)
                for h in range(HEADS):
                    if h + 1 < HEADS:
                        for t in range(TT):
                            score(h + 1, t)
                    for t in range(TT):
                        pe.wait_ge(mixed[t], h + 1)
                        if h > 0:
                            pe.wait_ge(att_copied[t], h)
                        for m in range(t + 1):
                            ins = pe.transpose(acc[:, 4 + t, m * P:(m + 1) * P], scores[:, t, 0, m * P:(m + 1) * P], ident[:, :])
                        ins.then_inc(att_T[t], 1)
                    for t in range(TT):
                        pe.wait_ge(att_copied[t], h + 1)
                        if h > 0:
                            pe.wait_ge(o_copied[t], h)
                        for m in range(t + 1):
                            v = h_tok[:, m, 2 * MIX + h * P:2 * MIX + (h + 1) * P]
                            ins = pe.matmul(acc[:, 6 + t, 0:P], attT[:, t, m * P:(m + 1) * P], v, start=m == 0, stop=m == t)
                        ins.then_inc(o_made[t], 1)
                pe.wait_ge(o_normed, TT)
                to_features("diff_mix", MIX_T // 2, h_tok)
                pe.wait_ge(split["diff_mix"], MIX_T // 2)
                with nc.tensor.Fori(0, 4) as c:
                    tokens_chunk(s_out[1], c, xT, c * 2)

            def z_ready(n):
                return lambda b: pe.wait_ge(z_made[l][n], 2 if b < 4 else 4)

            to_features(f"ln1_{l}", KT // 2, x_tok, z_ready(0))
            with nc.tensor.Fori(0, FF_CHUNKS) as g:
                for s in range(2):
                    pe.wait_ge(conv_made[l][s], g * 2)
                    features_chunk(s_up[l], g * 2 + s, xT, 2 * s, ready=split[f"ln1_{l}"] if s == 0 else None)
            pe.wait_ge(conv_made[l][0], 2 * FF_CHUNKS)
            with nc.tensor.Fori(0, 4) as c:
                tokens_chunk(s_down[l], c, act, c * 2, last_ready=act_made[l])
            if l == 0:
                to_features("ln2_0", KT // 2, x_tok, z_ready(1))

    ctx.close()


_INS = ["x", "mem", "positions", "pool_w_in", "pool_w", "pool_scale", "diff_w_in", "diff_lambda_q1", "diff_lambda_k1",
        "diff_lambda_q2", "diff_lambda_k2", "diff_subln_g", "mem_w_kv", "w_out", "ln1_g", "ln1_b", "ffn_w_up",
        "ffn_conv_w", "ffn_conv_b", "ffn_w_down", "ln2_g", "ln2_b"]


def kernel(**inputs):
    import concourse.bacc as bacc
    from concourse.bass_utils import run_bass_kernel_spmd

    nc = bacc.Bacc("TRN2", target_bir_lowering=False, num_devices=1)
    arrays, args = {}, {}
    for name in _INS:
        v = np.ascontiguousarray(inputs[name])
        arrays[f"in_{name}"] = v
        args[name] = nc.dram_tensor(f"in_{name}", v.shape, mybir.dt.from_np(v.dtype), kind="ExternalInput").ap()
    args["out"] = nc.dram_tensor("out_0", (1, S, D), F32, kind="ExternalOutput").ap()
    build(nc, args)
    r = run_bass_kernel_spmd(nc, [arrays], core_ids=[0])
    return r.results[0]["out_0"]
```

```python
import math
from contextlib import ExitStack

import numpy as np

import concourse.bass as bass
from concourse import mybir

F32 = mybir.dt.float32
F32R = mybir.dt.float32r
I32 = mybir.dt.int32
ALU = mybir.AluOpType
ACT = mybir.ActivationFunctionType
AX = mybir.AxisListType

P = 128
DEPTH = 2
S = 256
TT = S // P
D = 2048
KT = D // P
MEM_HEADS = 4
MEM_W = 512
MIX = D - MEM_W
MIX_T = MIX // P
WINDOWS = (2, 4, 8, 16)
GROUP_T = MIX_T // len(WINDOWS)
HEADS = 12
QK = 64
ROPE_HALF = 8
ROPE_THETA = 500000.0
D_FF = 5632
FF_T = D_FF // P
CHUNK = 512
PIECE = 4
SLOTS = 4
FF_CHUNKS = D_FF // CHUNK
DIFF_W = 3 * MIX + MEM_W
ALPHA = (2.0 * DEPTH) ** 0.25
LN_EPS = 1e-5
RMS_EPS = 1e-6
LAM_INIT = 0.8 - 0.6 * math.exp(-0.3 * 1)
RSQRT_MAGIC = 1597463007.0
MASKED = -1e30
PAD = max(WINDOWS)
CONV_COLS = 2 * FF_T
LN_COL = 4 * CONV_COLS
SCALE_COL = LN_COL + 4 * KT
TABLE = SCALE_COL + MIX_T
POOL_ORDER = (3, 2, 1, 0)
DIFF_ORDER = (9, 0, 3, 1, 4, 6, 2, 5, 7, 8)
POOL_W_PIECES = (2, 1, 0)
OUT_PIECES = ((3, 2, 1, 0), (0, 1, 3, 2))
POOL_KT = [PIECE * p + j for p in POOL_W_PIECES for j in range(PIECE)]
POOL_ENDS = [[f(POOL_KT.index(kt) for kt in range(GROUP_T * g, GROUP_T * g + GROUP_T)) for f in (min, max)] for g in range(4)]
POOL_BANK = (3, 2, 7, 6, 5, 4)
QK_PAIRS = [(w, half) for w in DIFF_ORDER if w == 9 or w < 6 for half in range(2)]
QK_SLOT = [4 * DIFF_ORDER.index(w) + 5 + half for w, half in QK_PAIRS]
ROTATED = {w: n + 1 for n, w in enumerate(w for w in DIFF_ORDER if w < 6)}
SCORE_SLOT = [4 * DIFF_ORDER.index(3 + h // 4) + 7 + h % 4 for h in range(HEADS)]
VALUE_SLOT = [25, 26, 27, 28, 37, 37, 38, 38]
MEM_SLOT = (5, 7)
MIX_BANK = (4, 5, 2, 3, 4, 5)


def value_bank(h):
    return 6 if h >= 10 else 7


def value_pair_end(h):
    return h + 2 - h % 2 if h >= 4 else h + 1


class Stream:

    def __init__(self, before, chunks, pieces, width=CHUNK):
        self.chunks, self.pieces, self.width = chunks, pieces, width
        self.first = before.first + before.chunks * before.pieces if before else 0
        self.uses = [len(range(s, pieces, SLOTS)) for s in range(SLOTS)]
        self.loads = [before.loads[s] + before.chunks * before.uses[s] if before else 0 for s in range(SLOTS)]
        self.tail = pieces % SLOTS != 0 or (before is not None and before.pieces % SLOTS != 0)

    def granule(self, c, k, j):
        return c * (self.pieces * PIECE) + ((self.first + k) * PIECE + j)

    def loaded(self, c, k):
        s = k % SLOTS
        return (c * self.uses[s] + (self.loads[s] + k // SLOTS + 1)) * 16

    def slot_split(self, c, k):
        back = 3 if self.tail and k < 3 else SLOTS
        return self.granule(c, k - back, PIECE)

    def used(self, c):
        return self.granule(c, self.pieces, 0)


class Order:

    def __init__(self, eng, sem):
        self.eng, self.sem, self.count, self.steps = eng, sem, 0, 0

    def then(self, ins):
        ins.then_inc(self.sem, 1)
        self.count = self.count + 1
        self.steps += 1

    def wait(self):
        self.eng.wait_ge(self.sem, self.count)

    def done(self, ins):
        self.then(ins)
        self.wait()


def build(nc, a):
    ctx = ExitStack()

    def sb(name, shape, dt=F32, stack=ctx):
        return stack.enter_context(nc.sbuf_tensor(name, shape, dt))

    def sem(name):
        return ctx.enter_context(nc.semaphore(name))

    raw = sb("raw", [P, SLOTS, PIECE * CHUNK])
    w_hi = sb("w_hi", [P, PIECE, CHUNK], F32R)
    w_lo = sb("w_lo", [P, PIECE, CHUNK], F32R)
    x_tok = sb("x_tok", [P, TT, D])
    conv = sb("conv", [P, 2, 2, 512])
    gb = sb("gb", [P, 2, CHUNK])
    table = sb("table", [P, DEPTH, TABLE])
    ident = sb("ident", [P, P])
    mask = sb("mask", [P, P])
    ident_r = sb("ident_r", [P, P], F32R)
    mask_r = sb("mask_r", [P, P], F32R)
    stats = sb("stats", [P, TT, 4, 6])
    mean_var = sb("mean_var", [P, TT, 2])
    rs_v = sb("rs_v", [P, TT, HEADS])
    rs_y = sb("rs_y", [P, TT, HEADS])
    rs_t = sb("rs_t", [P, TT, HEADS])
    mx = sb("mx", [P, 16])
    sums = sb("sums", [P, 16])
    recip = sb("recip", [P, HEADS, TT, 2])
    fold = sb("fold", [P, TT])
    lam_in = sb("lam_in", [P, 4, QK])
    lam = sb("lam", [P, 4])
    subln = sb("subln", [P, 1])
    steps16 = sb("steps16", [P, PAD], I32)
    pool_fix = sb("pool_fix", [P, len(WINDOWS), PAD])
    pos_i = sb("pos_i", [P, TT], I32)
    trig = sb("trig", [P, 7, TT, ROPE_HALF])

    def region(name, parts):
        stack = ExitStack()
        made = [sb(f"{name}_{n}", shape, dt, stack) for n, shape, dt in parts]
        stack.close()
        return made

    split_x = ("xT", [P, KT, 2, S], F32R)
    xT, act = region("ffn", [split_x, ("act", [P, FF_T, 2, S], F32R)])
    _, kvbuf, qmT0, memT, mem_tok, rows = region("memory", [
        split_x, ("kv", [P, 8, 512], F32), ("qmT", [P, MEM_HEADS, S], F32), ("memT", [P, KT, 2, S], F32R),
        ("mem", [P, TT, D], F32), ("rows", [P, DEPTH, 5, P], F32)])
    _, _, _, dT, pool_h, pool_a, pool_b, probs0 = region("pool", [
        split_x, ("kv", [P, 8, 512], F32), ("qmT", [P, MEM_HEADS, S], F32), ("dT", [P, MIX_T, 2, S], F32R),
        ("h", [P, 4, PAD + S], F32), ("a", [P, 4, PAD + S], F32), ("b", [P, 4, PAD + S], F32),
        ("probs", [P, 2, TT, S], F32)])
    _, h_tok, qkT, qmT1, kv1, probs1, scores, square, rot = region("diff", [
        split_x, ("h_tok", [P, TT, DIFF_W], F32), ("qkT", [P, HEADS, 2 * S], F32), ("qmT", [P, MEM_HEADS, S], F32),
        ("kv", [P, 4, 512], F32), ("probs", [P, 2, TT, S], F32),
        ("scores", [P, TT, 2, S], F32), ("square", [P, P], F32), ("rot", [P, 4, 128], F32)])
    (out_gb,) = region("last", [("gb", [P, 2, D], F32)])
    acc = ctx.enter_context(nc.psum_tensor("acc", [P, 8, 512], F32))
    kv1_dram = nc.dram_tensor("kv1_dram", [P, 4, 512], F32, kind="Internal").ap()
    qmT = (qmT0, qmT1)
    probs = (probs0, probs1)
    kv = (kvbuf, kv1)

    def bank(b, lo, hi):
        if isinstance(b, int):
            return acc[:, b, lo:hi]
        return acc[:, bass.ds(b, 1), lo:hi].rearrange("p a n -> p (a n)")

    def two(ap):
        return ap.rearrange("p (k s) -> p k s", k=2)

    def stage_place(b):
        return conv[:, b // 2 % 2, b % 2, :]

    s_kv = Stream(None, 4, 4)
    s_pool_in = Stream(s_kv, 4, 4)
    s_pool_w = Stream(s_pool_in, 1, 3, MIX // 4)
    s_out0 = Stream(s_pool_w, 4, 4)
    s_up0 = Stream(s_out0, 2 * FF_CHUNKS, 4)
    s_down0 = Stream(s_up0, 4, FF_T // PIECE)
    s_diff = Stream(s_down0, DIFF_W // CHUNK, 4)
    s_out1 = Stream(s_diff, 4, 4)
    s_up1 = Stream(s_out1, 2 * FF_CHUNKS, 4)
    s_down1 = Stream(s_up1, 4, FF_T // PIECE)
    s_out, s_up, s_down = (s_out0, s_out1), (s_up0, s_up1), (s_down0, s_down1)

    piece_loaded = [sem(f"piece_loaded{s}") for s in range(SLOTS)]
    hi_made = sem("hi_made")
    lo_made = sem("lo_made")
    granule_used = sem("granule_used")

    x_loaded = [sem(f"x_loaded{c}") for c in range(4)]
    mem_loaded = [sem(f"mem_loaded{c}") for c in range(4)]
    rows_loaded, small_loaded = sem("rows_loaded"), sem("small_loaded")
    zeroed, ident_made, steps_made, pads_made = sem("zeroed"), sem("ident_made"), sem("steps_made"), sem("pads_made")
    rounded = sem("rounded")
    rows_transposed, table_made = sem("rows_transposed"), sem("table_made")
    pool_evacuated, pool_diffed, dT_hi, dT_made = sem("pool_evacuated"), sem("pool_diffed"), sem("dT_hi"), sem("dT_made")
    qm_evacuated = sem("qm_evacuated")
    kv_evacuated = sem("kv_evacuated")
    kv1_stored, kv1_loaded = sem("kv1_stored"), sem("kv1_loaded")
    dve_order = sem("dve_order")
    out_gb_loaded = sem("out_gb_loaded")

    stages = ["x", "mem", "ln1_0", "ln2_0", "ln1_1", "pool_mix", "diff_mix", "mem_o0", "mem_o1"]
    banked = {s: sem(f"{s}_banked") for s in stages}
    scaled = {s: sem(f"{s}_scaled") for s in stages}
    hi_split = {s: sem(f"{s}_hi_split") for s in stages}
    split = {s: sem(f"{s}_split") for s in stages}

    mem_scored = [sem(f"mem_scored{l}") for l in range(2)]
    mem_shifted = [sem(f"mem_shifted{l}") for l in range(2)]
    mem_exped = [sem(f"mem_exped{l}") for l in range(2)]
    mem_probs = [sem(f"mem_probs{l}") for l in range(2)]
    mem_pT = [sem(f"mem_pT{l}") for l in range(2)]
    mem_pT_copied = [sem(f"mem_pT_copied{l}") for l in range(2)]
    mem_o_made = [sem(f"mem_o_made{l}") for l in range(2)]
    mem_o_copied = [sem(f"mem_o_copied{l}") for l in range(2)]
    z_made = [[sem(f"z_made{l}{n}") for n in range(2)] for l in range(2)]
    gb_loaded, gained, resid_affine = sem("gb_loaded"), sem("gained"), sem("resid_affine")
    tap_now = [[sem(f"tap_now{l}{s}") for s in range(2)] for l in range(2)]
    conv_made = [[sem(f"conv_made{l}{s}") for s in range(2)] for l in range(2)]
    silu_made = [sem(f"silu_made{l}") for l in range(2)]
    product_made = [sem(f"product_made{l}") for l in range(2)]
    act_hi = [sem(f"act_hi{l}") for l in range(2)]
    act_made = [sem(f"act_made{l}") for l in range(2)]
    h_evacuated = sem("h_evacuated")
    trig_arg, trig_made = sem("trig_arg"), sem("trig_made")
    lam_sum, lam_exp = sem("lam_sum"), sem("lam_exp")
    rotated, qk_banked, qk_copied = sem("rotated"), sem("qk_banked"), sem("qk_copied")
    scored, shifted, exped, mixed = sem("scored"), sem("shifted"), sem("exped"), sem("mixed")
    att_T, att_copied, o_made, squared = sem("att_T"), sem("att_copied"), sem("o_made"), sem("squared")
    o_normed = sem("o_normed")
    out_made, out_stored = sem("out_made"), sem("out_stored")

    block = ctx.enter_context(nc.Block())

    @block.sync
    def _(sp):
        def load_piece(st, c, k, w, col, piece=None):
            free = st.slot_split(c, k)
            if not (isinstance(free, int) and free <= 0):
                sp.wait_ge(lo_made, free)
            r = (k if piece is None else piece) * PIECE * P
            src = w[r:r + PIECE * P, bass.ds(col, st.width)].rearrange("(j p) n -> p j n", p=P)
            dst = raw[:, k % SLOTS, :].rearrange("p (j n) -> p j n", n=CHUNK)[:, :, 0:st.width]
            sp.dma_start(dst, src).then_inc(piece_loaded[k % SLOTS], 16)

        def load_chunk(st, c, w, col, pieces=None):
            for k in range(st.pieces):
                load_piece(st, c, k, w, col, pieces[k] if pieces else None)

        for c, (name, to, loaded) in enumerate((("mem", mem_tok, mem_loaded), ("x", x_tok, x_loaded))):
            src = a[name][0].rearrange("(t p) n -> p t n", p=P)
            for k in range(4):
                cs = slice(k * CHUNK, (k + 1) * CHUNK)
                sp.dma_start(to[:, :, cs], src[:, :, cs]).then_inc(loaded[k], 16)
                load_piece(s_kv, c, k, a["mem_w_kv"][0], c * CHUNK)
        for c in range(2, 4):
            load_chunk(s_kv, c, a["mem_w_kv"][1], (c - 2) * CHUNK)
        for c in range(4):
            load_chunk(s_pool_in, c, a["pool_w_in"][0], POOL_ORDER[c] * CHUNK)
        load_chunk(s_pool_w, 0, a["pool_w"][0].rearrange("g r n -> (g r) n"), 0, POOL_W_PIECES)
        for l in range(DEPTH):
            if l == 1:
                for c in range(DIFF_W // CHUNK):
                    load_chunk(s_diff, c, a["diff_w_in"][0], DIFF_ORDER[c] * CHUNK)
            for c in range(4):
                load_chunk(s_out[l], c, a["w_out"][l], c * CHUNK, OUT_PIECES[l])
            with nc.sync.Fori(0, FF_CHUNKS) as g:
                load_chunk(s_up[l], 2 * g, a["ffn_w_up"][l], g * CHUNK)
                load_chunk(s_up[l], 2 * g + 1, a["ffn_w_up"][l], g * CHUNK + D_FF)
            with nc.sync.Fori(0, 4) as c:
                load_chunk(s_down[l], c, a["ffn_w_down"][l], c * CHUNK)
        out_rows = a["out"][0].rearrange("(t p) n -> p t n", p=P)
        for n in range(4):
            t, half = n % 2, n // 2
            sp.wait_ge(out_made, n + 1)
            sp.dma_start(out_rows[:, t, half * 1024:(half + 1) * 1024],
                         x_tok[:, t, half * 1024:(half + 1) * 1024]).then_inc(out_stored, 16)
        sp.wait_ge(out_stored, 64)

    @block.gpsimd
    def _(pool):
        nc.gpsimd.memset(ident[:, :], 0.0).then_inc(zeroed, 1)
        nc.gpsimd.memset(mask[:, :], 0.0).then_inc(zeroed, 1)
        pool.wait_ge(zeroed, 2)
        nc.gpsimd.affine_select(out=ident[:, :], in_=ident[:, :], compare_op=ALU.not_equal, fill=1.0,
                                base=0, pattern=[[-1, P]], channel_multiplier=1).then_inc(ident_made, 1)
        nc.gpsimd.affine_select(out=mask[:, :], in_=mask[:, :], compare_op=ALU.is_ge, fill=MASKED,
                                base=0, pattern=[[-1, P]], channel_multiplier=1).then_inc(ident_made, 1)
        nc.gpsimd.iota(steps16[:, :], pattern=[[1, PAD]], base=1, channel_multiplier=0).then_inc(steps_made, 1)
        for l in range(DEPTH):
            vectors = [a["ffn_conv_w"][l, 0], a["ffn_conv_w"][l, 1], a["ffn_conv_w"][l, 2], a["ffn_conv_b"][l]]
            for i, v in enumerate(vectors):
                pool.dma_start(rows[0:CONV_COLS, l, i, :], v.rearrange("(r n) -> r n", n=P)).then_inc(rows_loaded, 16)
            for i, name in enumerate(("ln1_g", "ln1_b", "ln2_g", "ln2_b")):
                pool.dma_start(rows[i * KT:(i + 1) * KT, l, 4, :], a[name][l].rearrange("(r n) -> r n", n=P)).then_inc(rows_loaded, 16)
            pool.dma_start(rows[4 * KT:4 * KT + MIX_T, l, 4, :], a["pool_scale"][0].rearrange("(r n) -> r n", n=P)).then_inc(rows_loaded, 16)
        for i, name in enumerate(("diff_lambda_q1", "diff_lambda_q2", "diff_lambda_k1", "diff_lambda_k2")):
            pool.dma_start(lam_in[:, i, :], a[name][0:1, :].broadcast_to([P, QK])).then_inc(small_loaded, 16)
        pool.dma_start(subln[:, :], a["diff_subln_g"].rearrange("a p -> p a")).then_inc(small_loaded, 16)
        for t in range(TT):
            pool.dma_start(pos_i[:, t:t + 1], a["positions"][0:1, t * P:(t + 1) * P].rearrange("a p -> p a")).then_inc(small_loaded, 16)
        pool.wait_ge(granule_used, s_kv.used(3))
        nc.gpsimd.memset(pool_h[:, :, 0:PAD], 0.0).then_inc(pads_made, 1)
        pool.wait_ge(kv_evacuated, 4)
        pool.dma_start(kv1_dram[:, :, :], kvbuf[:, 4:8, :]).then_inc(kv1_stored, 16)

        for n_ln, (l, n) in enumerate(((0, 0), (0, 1), (1, 0))):
            pool.wait_ge(banked[f"ln{n + 1}_{l}"], KT // 2)
            if (l, n) == (0, 1):
                pool.wait_ge(kv1_stored, 16)
                pool.dma_start(kv1[:, :, :], kv1_dram[:, :, :]).then_inc(kv1_loaded, 16)
            for c in range(4):
                done = 4 * n_ln + c + 1
                cs = slice(c * CHUNK, (c + 1) * CHUNK)
                for i, name in enumerate((f"ln{n + 1}_g", f"ln{n + 1}_b")):
                    pool.dma_start(gb[:, i, :], a[name][l:l + 1, cs].broadcast_to([P, CHUNK])).then_inc(gb_loaded, 16)
                pool.wait_ge(gb_loaded, 32 * done)
                nc.gpsimd.tensor_tensor(x_tok[:, :, cs], x_tok[:, :, cs], gb[:, 0:1, :].broadcast_to([P, TT, CHUNK]),
                                        ALU.mult).then_inc(gained, 1)
                pool.wait_ge(gained, done)
                nc.gpsimd.tensor_tensor(x_tok[:, :, cs], x_tok[:, :, cs], gb[:, 1:2, :].broadcast_to([P, TT, CHUNK]),
                                        ALU.add).then_inc(resid_affine, 1)
                pool.wait_ge(resid_affine, done)
        pool.wait_ge(granule_used, s_up[1].used(2 * FF_CHUNKS - 1))
        for i, name in enumerate(("ln2_g", "ln2_b")):
            pool.dma_start(out_gb[:, i, :], a[name][1:2, :].broadcast_to([P, D])).then_inc(out_gb_loaded, 16)

    @block.scalar
    def _(act_e):
        def hi_granule(st, c, k, j):
            if j == 0:
                act_e.wait_ge(piece_loaded[k % SLOTS], st.loaded(c, k))
            free = st.granule(c, k, j) - PIECE + 1
            if not (isinstance(free, int) and free <= 0):
                act_e.wait_ge(granule_used, free)
            nc.scalar.activation(w_hi[:, j, 0:st.width], raw[:, k % SLOTS, j * CHUNK:j * CHUNK + st.width],
                                 ACT.Copy).then_inc(hi_made, 1)

        def hi_piece(st, c, k):
            for j in range(PIECE):
                hi_granule(st, c, k, j)

        def split_hi(stage, b, dst, kt0, src):
            if src == "staged":
                act_e.wait_ge(scaled[stage], b + 1)
                src = stage_place(b)
            else:
                act_e.wait_ge(banked[stage], b + 1)
            nc.scalar.activation(dst[:, kt0:kt0 + 2, 0, :], two(src), ACT.Copy).then_inc(hi_split[stage], 1)

        def first_chunk(st, stage):
            def split_bank(b):
                split_hi(stage, b, xT, 2 * b, "staged")
            hi_piece(st, 0, 0)
            split_bank(0)
            split_bank(1)
            for k in range(1, 4):
                hi_granule(st, 0, k, 0)
                split_bank(2 * k)
                hi_granule(st, 0, k, 1)
                hi_granule(st, 0, k, 2)
                split_bank(2 * k + 1)
                hi_granule(st, 0, k, 3)

        def mem_exp(l, h):
            act_e.wait_ge(mem_shifted[l], h + 1)
            if h >= 2:
                act_e.wait_ge(mem_probs[l], h - 1)
                act_e.wait_ge(mem_o_made[l], h - 1)
            for t in range(TT):
                i = (h % 2) * TT + t
                ins = nc.scalar.activation(probs[l][:, h % 2, t, :], acc[:, 4 + h % 2, t * S:(t + 1) * S], ACT.Exp,
                                           bias=mx[:, i:i + 1], scale=float(P) ** -0.5, accum_out=sums[:, i:i + 1])
            ins.then_inc(mem_exped[l], 1)

        def mem_pT_out(l, h):
            act_e.wait_ge(mem_pT[l], h + 1)
            nc.scalar.activation(probs[l][:, h % 2, :, :], two(acc[:, 6, :]), ACT.Copy).then_inc(mem_pT_copied[l], 1)

        def mem_o_out(l, h):
            act_e.wait_ge(mem_o_made[l], h + 1)
            nc.scalar.activation(qmT[l][:, h, :], acc[:, 7, 0:S], ACT.Copy).then_inc(mem_o_copied[l], 1)

        def mem_o_hi(l, b):
            act_e.wait_ge(mem_o_copied[l], 2 * b + 2)
            nc.scalar.activation(xT[:, MIX_T + 2 * b:MIX_T + 2 * b + 2, 0, :], qmT[l][:, 2 * b:2 * b + 2, :],
                                 ACT.Copy).then_inc(hi_split[f"mem_o{l}"], 1)

        def mem_beside(l, n, j, first):
            for h in range(MEM_HEADS):
                if (n, j) == (first + h + 1, 0):
                    mem_exp(l, h)
                if (n, j) == (first + h + 2, 1):
                    mem_pT_out(l, h)
                if (n, j) == (first + h + 3, 2):
                    mem_o_out(l, h)

        def taps(l, s, g):
            act_e.wait_ge(granule_used, s_up[l].used(2 * g + s))
            if s == 1:
                act_e.wait_ge(lo_made, s_up[l].granule(2 * g + 1, 0, 0) + 1)
            elif not isinstance(g, int):
                act_e.wait_ge(product_made[l], g * 2)
            else:
                act_e.wait_ge(split[f"ln1_{l}"], KT // 2)
            for b in range(2):
                for f in range(2):
                    col = g * 4 + (s * FF_T + 2 * b + f)
                    ins = nc.scalar.activation(conv[:, s, b, f * S:(f + 1) * S], acc[:, 2 * s + b, f * S:(f + 1) * S],
                                               ACT.Identity, bias=table[:, l, bass.ds(col + 3 * CONV_COLS, 1)],
                                               scale=table[:, l, bass.ds(col + 2 * CONV_COLS, 1)])
                ins.then_inc(tap_now[l][s], 1)

        def silu(l, b, g):
            act_e.wait_ge(conv_made[l][0], g * 2 + (b + 1))
            nc.scalar.activation(conv[:, 0, b, :], conv[:, 0, b, :], ACT.Silu).then_inc(silu_made[l], 1)

        def act_hi_part(l, b, g):
            act_e.wait_ge(product_made[l], g * 2 + (b + 1))
            nc.scalar.activation(act[:, bass.ds(g * 4 + 2 * b, 2), 0, :], two(conv[:, 1, b, :]), ACT.Copy).then_inc(act_hi[l], 1)

        def kv_out(c):
            act_e.wait_ge(granule_used, s_kv.used(c))
            b = 2 * (c % 2)
            nc.scalar.activation(kvbuf[:, 2 * c:2 * c + 2, :], acc[:, b:b + 2, :], ACT.Copy).then_inc(kv_evacuated, 1)

        for b in range(2):
            split_hi("mem", b, memT, 2 * b, acc[:, 4 + b, :])
        hi_piece(s_kv, 0, 0)
        for n in range(1, 16):
            c, k = n // 4, n % 4
            for j in range(PIECE):
                hi_granule(s_kv, c, k, j)
                if c == 0 and j in (0, 2):
                    b = 2 * k + j // 2
                    split_hi("mem", b, memT, 2 * b, acc[:, 4 + b % 4, :])
                if 5 <= n < 13 and j == 1:
                    split_hi("x", n - 5, xT, 2 * (n - 5), acc[:, 4 + (n - 5) % 4, :])
                if c > 0 and k == 0 and j == 3:
                    kv_out(c - 1)
                if (n, j) == (13, 0):
                    act_e.wait_ge(ident_made, 2)
                    nc.scalar.activation(ident_r[:, :], ident[:, :], ACT.Copy).then_inc(rounded, 1)
                    nc.scalar.activation(mask_r[:, :], mask[:, :], ACT.Copy).then_inc(rounded, 1)
                if (n, j) == (15, 1):
                    act_e.wait_ge(trig_arg, 1)
                    nc.scalar.activation(trig[:, 0:2, :, :].rearrange("p a t n -> p (a t n)"),
                                         trig[:, 2:4, :, :].rearrange("p a t n -> p (a t n)"), ACT.Sin).then_inc(trig_made, 1)

        def pool_out(c):
            act_e.wait_ge(granule_used, s_pool_in.used(c))
            if c > 1:
                act_e.wait_ge(dT_made, c - 1)
            b = 2 * (c % 2)
            nc.scalar.activation(pool_h[:, :, PAD:PAD + S], acc[:, b:b + 2, :].rearrange("p b (k s) -> p (b k) s", k=2),
                                 ACT.Copy).then_inc(pool_evacuated, 1)

        def dT_hi_part(c):
            act_e.wait_ge(pool_diffed, c)
            kt = 4 * POOL_ORDER[c]
            nc.scalar.activation(dT[:, kt:kt + 4, 0, :], pool_h[:, :, PAD:PAD + S], ACT.Copy).then_inc(dT_hi, 1)

        for n in range(16):
            c, k = n // 4, n % 4
            for j in range(PIECE):
                hi_granule(s_pool_in, c, k, j)
                mem_beside(0, n, j, MEM_SLOT[0])
                if (k, j) == (0, 3):
                    if c == 0:
                        kv_out(3)
                    elif c == 1:
                        act_e.wait_ge(granule_used, s_pool_in.used(0))
                        nc.scalar.activation(qmT0[:, :, :], acc[:, 0:2, :].rearrange("p b (k s) -> p (b k) s", k=2),
                                             ACT.Copy).then_inc(qm_evacuated, 1)
                    else:
                        pool_out(c - 1)
                if (n, j) == (2, 1):
                    act_e.wait_ge(lam_sum, 1)
                    nc.scalar.activation(lam[:, 2:4], lam[:, 0:2], ACT.Exp).then_inc(lam_exp, 1)
                if (k, j) == (2, 3) and c > 1:
                    dT_hi_part(c - 1)
        for k in range(3):
            for j in range(PIECE):
                hi_granule(s_pool_w, 0, k, j)
                if (k, j) == (0, 3):
                    pool_out(3)
                if (k, j) == (1, 1):
                    mem_o_hi(0, 0)
                    mem_o_hi(0, 1)
                if (k, j) == (2, 0):
                    dT_hi_part(3)

        for l in range(DEPTH):
            if l == 0:
                for k in range(4):
                    for j in range(PIECE):
                        hi_granule(s_out[0], 0, k, j)
                        if k < 3 and j in (1, 3):
                            i = 2 * k + j // 2
                            split_hi("pool_mix", i, xT, MIX_T - 2 - 2 * i, "staged")
            else:
                def h_out(c):
                    act_e.wait_ge(granule_used, s_diff.used(c))
                    b, col = 2 * (c % 2), DIFF_ORDER[c] * CHUNK
                    nc.scalar.activation(h_tok[:, :, col:col + CHUNK], acc[:, b:b + 2, :], ACT.Copy).then_inc(h_evacuated, 1)

                def qk_out(i):
                    act_e.wait_ge(qk_banked, i + 1)
                    w, half = QK_PAIRS[i]
                    if w == 9:
                        nc.scalar.activation(qmT1[:, 2 * half:2 * half + 2, :], two(acc[:, 6, :]), ACT.Copy).then_inc(qk_copied, 1)
                    else:
                        h, is_key = 4 * (w % 3) + 2 * half, w // 3
                        nc.scalar.activation(qkT[:, h:h + 2, is_key * S:(is_key + 1) * S], two(acc[:, 6, :]), ACT.Copy,
                                             scale=1.0 if is_key else float(QK) ** -0.5).then_inc(qk_copied, 1)

                def head_exp(h):
                    act_e.wait_ge(shifted, h + 1)
                    if h > 0:
                        act_e.wait_ge(att_T, h)
                    for t in range(TT):
                        for m in range(2):
                            i = 2 * t + m
                            keys = slice(t * P, t * P + (t + 1) * P)
                            ins = nc.scalar.activation(scores[:, t, m, 0:(t + 1) * P], acc[:, 4 + m, keys], ACT.Exp,
                                                       bias=mx[:, i:i + 1], accum_out=sums[:, i:i + 1])
                    ins.then_inc(exped, 1)

                def att_out(h):
                    act_e.wait_ge(att_T, h + 1)
                    nc.scalar.activation(qkT[:, h, P:4 * P], acc[:, 6, P:4 * P], ACT.Copy).then_inc(att_copied, 1)

                def o_out(h):
                    act_e.wait_ge(o_made, value_pair_end(h))
                    b = value_bank(h)
                    for t in range(TT):
                        o = acc[:, b, (h % 2) * S + t * P:(h % 2) * S + (t + 1) * P]
                        nc.scalar.activation(h_tok[:, t, h * P:(h + 1) * P], o, ACT.Copy, scale=recip[:, h, t, 0:1])
                        nc.scalar.activation(square[:, :], o, ACT.Square, scale=recip[:, h, t, 0:1],
                                             accum_out=rs_v[:, t, h:h + 1]).then_inc(squared, 1)
                        act_e.wait_ge(squared, 2 * h + t + 1)

                def beside(n, j):
                    mem_beside(1, n, j, MEM_SLOT[1])
                    if (n % 4, j) == (0, 3) and n > 0:
                        h_out(n // 4 - 1)
                    for i in range(len(QK_PAIRS)):
                        if (n, j) == (QK_SLOT[i] + 1, 3):
                            qk_out(i)
                    for h in range(HEADS):
                        if (n, j) == (SCORE_SLOT[h] + 1, 0):
                            head_exp(h)
                        if (n, j) == (SCORE_SLOT[h] + 2, 1):
                            att_out(h)
                        if h < 8 and (n, j) == (VALUE_SLOT[h] + 1, 2):
                            o_out(h)

                first_chunk(s_diff, "ln2_0")
                for n in range(4, 40):
                    for j in range(PIECE):
                        hi_granule(s_diff, n // 4, n % 4, j)
                        beside(n, j)
                att_out(HEADS - 1)
                hi_piece(s_out[1], 0, 0)
                h_out(9)
                for i in range(2):
                    split_hi("diff_mix", i, xT, 2 * i, "staged")
                for i in range(2, 4):
                    hi_granule(s_out[1], 0, 1, 2 * i - 4)
                    o_out(2 * i + 4)
                    o_out(2 * i + 5)
                    split_hi("diff_mix", i, xT, 2 * i, "staged")
                    hi_granule(s_out[1], 0, 1, 2 * i - 3)
                hi_granule(s_out[1], 0, 2, 0)
                mem_o_hi(1, 0)
                hi_granule(s_out[1], 0, 2, 1)
                mem_o_hi(1, 1)
                hi_granule(s_out[1], 0, 2, 2)
                split_hi("diff_mix", 4, xT, 8, "staged")
                hi_granule(s_out[1], 0, 2, 3)
                split_hi("diff_mix", 5, xT, 10, "staged")
                hi_piece(s_out[1], 0, 3)
            with nc.scalar.Fori(1, 4) as c:
                for k in range(4):
                    hi_piece(s_out[l], c, k)

            def ffn_gate(g):
                hi_piece(s_up[l], 2 * g, 0)
                taps(l, 1, g - 1)
                hi_piece(s_up[l], 2 * g, 1)
                act_hi_part(l, 0, g - 1)
                hi_piece(s_up[l], 2 * g, 2)
                act_hi_part(l, 1, g - 1)
                hi_piece(s_up[l], 2 * g, 3)

            def ffn_up(g):
                hi_piece(s_up[l], 2 * g + 1, 0)
                taps(l, 0, g)
                hi_piece(s_up[l], 2 * g + 1, 1)
                silu(l, 0, g)
                hi_piece(s_up[l], 2 * g + 1, 2)
                silu(l, 1, g)
                hi_piece(s_up[l], 2 * g + 1, 3)

            first_chunk(s_up[l], f"ln1_{l}")
            if l == 0:
                act_e.wait_ge(kv1_stored, 16)
            ffn_up(0)
            with nc.scalar.Fori(1, FF_CHUNKS) as g:
                ffn_gate(g)
                ffn_up(g)
            last = FF_CHUNKS - 1
            hi_piece(s_down[l], 0, 0)
            taps(l, 1, last)
            hi_piece(s_down[l], 0, 1)
            act_hi_part(l, 0, last)
            hi_piece(s_down[l], 0, 2)
            act_hi_part(l, 1, last)
            for k in range(3, FF_T // PIECE):
                hi_piece(s_down[l], 0, k)
            with nc.scalar.Fori(1, 4) as c:
                for k in range(FF_T // PIECE):
                    hi_piece(s_down[l], c, k)

    @block.vector
    def _(dve):
        order = Order(dve, dve_order)

        def loop(start, end, per, body):
            before, steps = order.count, order.steps
            with nc.vector.Fori(start, end) as i:
                order.count = before + (i - start) * per
                body(i)
                assert order.steps - steps == per, (order.steps - steps, per)
            order.count = before + (end - start) * per

        def lo_granule(st, c, k, j):
            dve.wait_ge(hi_made, st.granule(c, k, j) + 1)
            nc.vector.tensor_tensor(w_lo[:, j, 0:st.width], raw[:, k % SLOTS, j * CHUNK:j * CHUNK + st.width],
                                    w_hi[:, j, 0:st.width].bitcast(F32), ALU.subtract).then_inc(lo_made, 1)

        def lo_piece(st, c, k):
            for j in range(PIECE):
                lo_granule(st, c, k, j)

        def scale_bank(stage, b, src, gain, bias=None, filled=None):
            if filled is not None:
                dve.wait_ge(granule_used, filled)
            else:
                dve.wait_ge(banked[stage], b + 1)
            if b >= 4:
                dve.wait_ge(split[stage], b - 3)
            for f in range(2):
                args = (bias(f), ALU.mult, ALU.add) if bias else (1.0, ALU.mult, ALU.mult)
                ins = nc.vector.tensor_scalar(stage_place(b)[:, f * S:(f + 1) * S], src[:, f * S:(f + 1) * S], gain(f), *args)
            ins.then_inc(scaled[stage], 1)

        def split_lo(stage, b, dst, kt0, src):
            dve.wait_ge(hi_split[stage], b + 1)
            nc.vector.tensor_tensor(dst[:, kt0:kt0 + 2, 1, :], two(src), dst[:, kt0:kt0 + 2, 0, :].bitcast(F32),
                                    ALU.subtract).then_inc(split[stage], 1)

        def rsqrt(of, n_steps=3):
            v, y, t = of(rs_v), of(rs_y), of(rs_t)
            order.done(nc.vector.tensor_scalar(y.bitcast(I32), v.bitcast(I32), -0.5, RSQRT_MAGIC, ALU.mult, ALU.add))
            for _ in range(n_steps):
                order.done(nc.vector.tensor_tensor(t, y, y, ALU.mult))
                order.done(nc.vector.scalar_tensor_tensor(t, t, -0.5, v, ALU.mult, ALU.mult))
                order.done(nc.vector.scalar_tensor_tensor(y, t, 1.5, y, ALU.add, ALU.mult))

        def resid_out(st, c):
            dve.wait_ge(granule_used, st.used(c))
            for t in range(TT):
                cols = x_tok[:, t, bass.ds(c * CHUNK, CHUNK)]
                order.then(nc.vector.scalar_tensor_tensor(cols, cols, ALPHA, bank(2 * c + t, 0, CHUNK), ALU.mult, ALU.add))
            order.wait()
            for t in range(TT):
                order.then(nc.vector.bn_stats(stats[:, t, bass.ds(c, 1), :].rearrange("p a n -> p (a n)"), x_tok[:, t, bass.ds(c * CHUNK, CHUNK)]))

        def proj_chunk(st, c):
            lo_piece(st, c, 0)
            resid_out(st, c - 1)
            for k in range(1, st.pieces):
                lo_piece(st, c, k)

        def norm_stats():
            order.wait()
            for t in range(TT):
                order.then(nc.vector.bn_aggr(mean_var[:, t, :], stats[:, t, :, :]))
            order.wait()
            order.done(nc.vector.tensor_scalar(rs_v[:, :, 0:1], mean_var[:, :, 1:2], LN_EPS, None, ALU.add))
            rsqrt(lambda x: x[:, :, 0:1])

        def norm_chunk(l, n, st, nxt):
            stage = f"ln{n + 1}_{l}"
            g0 = LN_COL + 2 * n * KT
            for j in range(3):
                lo_granule(nxt, 0, 0, j)
            resid_out(st, 3)
            norm_stats()
            for q in range(4):
                for t in range(TT):
                    cols = x_tok[:, t, q * CHUNK:(q + 1) * CHUNK]
                    nc.vector.tensor_scalar(cols, cols, mean_var[:, t, 0:1], rs_y[:, t, 0:1],
                                            ALU.subtract, ALU.mult).then_inc(z_made[l][n], 1)

            def scale(b):
                scale_bank(stage, b, acc[:, 4 + b % 4, :], lambda f: table[:, l, g0 + 2 * b + f:g0 + 2 * b + f + 1],
                           lambda f: table[:, l, g0 + KT + 2 * b + f:g0 + KT + 2 * b + f + 1])

            def lo(b):
                split_lo(stage, b, xT, 2 * b, stage_place(b))

            scale(0)
            scale(1)
            lo(0)
            lo_granule(nxt, 0, 0, 3)
            lo(1)
            for k in range(1, 4):
                lo_granule(nxt, 0, k, 0)
                scale(2 * k)
                lo_granule(nxt, 0, k, 1)
                lo(2 * k)
                scale(2 * k + 1)
                lo_granule(nxt, 0, k, 2)
                lo(2 * k + 1)
                lo_granule(nxt, 0, k, 3)

        def mem_max(l, h):
            dve.wait_ge(mem_scored[l], h + 1)
            i = 2 * (h % 2)
            if h >= 2:
                dve.wait_ge(mem_exped[l], h - 1)
            order.done(nc.vector.tensor_reduce(mx[:, 8 + i:10 + i], two(acc[:, 4 + h % 2, :]), AX.X, ALU.max))
            nc.vector.tensor_scalar(mx[:, i:i + 2], mx[:, 8 + i:10 + i], -float(P) ** -0.5, None, ALU.mult).then_inc(mem_shifted[l], 1)

        def mem_normalise(l, h):
            dve.wait_ge(mem_exped[l], h + 1)
            i = 2 * (h % 2)
            order.done(nc.vector.reciprocal(sums[:, 8 + i:10 + i], sums[:, i:i + 2]))
            for t in range(TT):
                ins = nc.vector.tensor_scalar(probs[l][:, h % 2, t, :], probs[l][:, h % 2, t, :], sums[:, 8 + i + t:9 + i + t], None, ALU.mult)
            ins.then_inc(mem_probs[l], 1)

        def mem_beside(l, n, j, first):
            for h in range(MEM_HEADS):
                if (n, j) == (first + h, 3):
                    mem_max(l, h)
                if (n, j) == (first + h + 1, 1):
                    mem_normalise(l, h)

        def mem_o_lo(l, b):
            dve.wait_ge(hi_split[f"mem_o{l}"], b + 1)
            kts = slice(MIX_T + 2 * b, MIX_T + 2 * b + 2)
            nc.vector.tensor_tensor(xT[:, kts, 1, :], qmT[l][:, 2 * b:2 * b + 2, :], xT[:, kts, 0, :].bitcast(F32),
                                    ALU.subtract).then_inc(split[f"mem_o{l}"], 1)

        def conv_bank(l, s, b, g):
            dve.wait_ge(tap_now[l][s], g * 2 + (b + 1))
            for lag in (1, 2):
                for f in range(2):
                    col = g * 4 + (s * FF_T + 2 * b + f + (2 - lag) * CONV_COLS)
                    to = conv[:, s, b, f * S + lag:(f + 1) * S]
                    ins = nc.vector.scalar_tensor_tensor(to, acc[:, 2 * s + b, f * S:(f + 1) * S - lag],
                                                         table[:, l, bass.ds(col, 1)], to, ALU.mult, ALU.add)
                    if lag == 1:
                        order.then(ins)
                if lag == 1:
                    order.wait()
            ins.then_inc(conv_made[l][s], 1)

        def product(l, b, g):
            dve.wait_ge(silu_made[l], g * 2 + (b + 1))
            dve.wait_ge(conv_made[l][1], g * 2 + (b + 1))
            nc.vector.tensor_tensor(conv[:, 1, b, :], conv[:, 1, b, :], conv[:, 0, b, :], ALU.mult).then_inc(product_made[l], 1)

        def act_lo_part(l, b, g):
            dve.wait_ge(act_hi[l], g * 2 + (b + 1))
            kts = bass.ds(g * 4 + 2 * b, 2)
            nc.vector.tensor_tensor(act[:, kts, 1, :], two(conv[:, 1, b, :]), act[:, kts, 0, :].bitcast(F32),
                                    ALU.subtract).then_inc(act_made[l], 1)

        dve.wait_ge(steps_made, 1)
        for g, w in enumerate(WINDOWS):
            order.then(nc.vector.tensor_scalar(pool_fix[:, g, :], steps16[:, :], float(w), None, ALU.min))
        order.wait()
        order.done(nc.vector.reciprocal(pool_fix[:, :, :], pool_fix[:, :, :]))
        for g, w in enumerate(WINDOWS):
            order.then(nc.vector.tensor_scalar(pool_fix[:, g, :], pool_fix[:, g, :], float(w), None, ALU.mult))

        pos_f, ang, turn, part = trig[:, 6, :, 0:1], trig[:, 4, :, :], trig[:, 5, :, :], trig[:, 6, :, :]

        def angles():
            dve.wait_ge(small_loaded, 7 * 16)
            order.done(nc.vector.tensor_copy(pos_f, pos_i[:, :].rearrange("p (t a) -> p t a", a=1)))
            for n in range(ROPE_HALF):
                freq = float(np.float32(ROPE_THETA) ** np.float32(-2.0 * n / (2 * ROPE_HALF)))
                order.then(nc.vector.tensor_scalar(trig[:, 4, :, n:n + 1], pos_f, freq, None, ALU.mult))
            order.wait()

        def reduce_angles(turns):
            two_pi = rest = 2 * math.pi
            whole = 1.5 * 2.0 ** 23
            order.done(nc.vector.tensor_scalar(turn, ang, 1.0 / (two_pi * turns), None, ALU.mult))
            order.done(nc.vector.tensor_scalar(turn, turn, whole, None, ALU.add))
            order.done(nc.vector.tensor_scalar(turn, turn, whole, None, ALU.subtract))
            for bits in (7, 14, 21, 28, 36, 48):
                step = 2.0 ** (3 - bits)
                part_of_2pi = math.floor(rest / step) * step
                rest -= part_of_2pi
                order.done(nc.vector.scalar_tensor_tensor(ang, turn, -part_of_2pi * turns, ang, ALU.mult, ALU.add))

        def sine_arguments():
            pi = float(np.nextafter(np.float32(math.pi), np.float32(0)))
            order.done(nc.vector.tensor_scalar(trig[:, 3, :, :], ang, pi, -pi, ALU.min, ALU.max))
            order.done(nc.vector.tensor_scalar(part, trig[:, 3, :, :], -1.0, None, ALU.mult))
            order.done(nc.vector.tensor_tensor(part, part, trig[:, 3, :, :], ALU.max))
            nc.vector.tensor_scalar(trig[:, 2, :, :], part, -1.0, math.pi / 2, ALU.mult, ALU.add).then_inc(trig_arg, 1)

        for b in range(2):
            split_lo("mem", b, memT, 2 * b, acc[:, 4 + b, :])
        lo_piece(s_kv, 0, 0)
        for n in range(1, 16):
            c, k = n // 4, n % 4
            for j in range(PIECE):
                lo_granule(s_kv, c, k, j)
                if c == 0 and j in (0, 2):
                    b = 2 * k + j // 2
                    split_lo("mem", b, memT, 2 * b, acc[:, 4 + b % 4, :])
                if 5 <= n < 13 and j == 1:
                    split_lo("x", n - 5, xT, 2 * (n - 5), acc[:, 4 + (n - 5) % 4, :])
                if (n, j) == (13, 1):
                    for l in range(DEPTH):
                        dve.wait_ge(rows_transposed, l + 1)
                        nc.vector.tensor_copy(table[:, l, :], acc[:, 4 + l, 0:TABLE]).then_inc(table_made, 1)
                if (n, j) == (13, 3):
                    angles()
                if (n, j) == (14, 1):
                    reduce_angles(4096.0)
                if (n, j) == (14, 3):
                    reduce_angles(1.0)
                if (n, j) == (15, 0):
                    sine_arguments()

        def lambda_sums():
            order.done(nc.vector.tensor_tensor(lam_in[:, 0:2, :], lam_in[:, 0:2, :], lam_in[:, 2:4, :], ALU.mult))
            nc.vector.tensor_reduce(lam[:, 0:2], lam_in[:, 0:2, :], AX.X, ALU.add).then_inc(lam_sum, 1)

        def lambda_value():
            dve.wait_ge(lam_exp, 1)
            order.done(nc.vector.tensor_tensor(lam[:, 0:1], lam[:, 3:4], lam[:, 2:3], ALU.subtract))
            order.done(nc.vector.tensor_scalar(lam[:, 0:1], lam[:, 0:1], -LAM_INIT, None, ALU.add))
            order.then(nc.vector.tensor_scalar(subln[:, :], subln[:, :], 1.0 - LAM_INIT, None, ALU.mult))

        def pooled_run(c, f, n, g, last):
            fs, src, dst, reach = slice(f, f + n), pool_h, pool_a, 1
            while reach < WINDOWS[g]:
                lo = 2 * reach - 1
                order.done(nc.vector.tensor_tensor(dst[:, fs, lo:], src[:, fs, lo:], src[:, fs, lo - reach:PAD + S - reach], ALU.add))
                src, dst, reach = dst, (pool_b if dst is pool_a else pool_a), 2 * reach
            first = src[:, fs, PAD:2 * PAD]
            order.done(nc.vector.tensor_tensor(first, first, pool_fix[:, g:g + 1, :].broadcast_to([P, n, PAD]), ALU.mult))
            ins = nc.vector.scalar_tensor_tensor(pool_h[:, fs, PAD:PAD + S], src[:, fs, PAD:PAD + S], 1.0 / WINDOWS[g],
                                                 pool_h[:, fs, PAD:PAD + S], ALU.mult, ALU.subtract)
            if last:
                ins.then_inc(pool_diffed, 1)
            else:
                order.then(ins)

        def pooled(c):
            runs, f, w = [], 0, POOL_ORDER[c]
            while f < 4:
                g = (4 * w + f) // GROUP_T
                n = min(4 - f, GROUP_T * (g + 1) - (4 * w + f))
                runs.append((c, f, n, g))
                f += n
            return runs

        def dT_lo_part(c):
            dve.wait_ge(dT_hi, c)
            dve.wait_ge(pool_diffed, c)
            kt = 4 * POOL_ORDER[c]
            nc.vector.tensor_tensor(dT[:, kt:kt + 4, 1, :], pool_h[:, :, PAD:PAD + S],
                                    dT[:, kt:kt + 4, 0, :].bitcast(F32), ALU.subtract).then_inc(dT_made, 1)

        def pool_beside(c, k, j):
            runs = pooled(c)
            if (k, j) == (1, 0):
                dve.wait_ge(pool_evacuated, c)
                if c == 1:
                    dve.wait_ge(pads_made, 1)
                pooled_run(*runs[0], last=len(runs) == 1)
            if (k, j) == (1, 2) and len(runs) > 1:
                pooled_run(*runs[1], last=True)
            if (k, j) == (2, 3):
                dT_lo_part(c)

        for n in range(16):
            c, k = n // 4, n % 4
            for j in range(PIECE):
                lo_granule(s_pool_in, c, k, j)
                mem_beside(0, n, j, MEM_SLOT[0])
                if c > 1:
                    pool_beside(c - 1, k, j)
                if (n, j) == (1, 1):
                    lambda_sums()
                if (n, j) == (3, 1):
                    lambda_value()
        for k in range(3):
            for j in range(PIECE):
                lo_granule(s_pool_w, 0, k, j)
                if (k, j) == (1, 3):
                    mem_o_lo(0, 0)
                    mem_o_lo(0, 1)
                if (k, j) == (0, 3):
                    dve.wait_ge(pool_evacuated, 3)
                    for i, run in enumerate(pooled(3)):
                        pooled_run(*run, last=i == 1)
                if (k, j) == (2, 0):
                    dT_lo_part(3)

        for l in range(DEPTH):
            if l == 0:
                def pool_scale(i):
                    kt = MIX_T - 2 - 2 * i
                    scale_bank("pool_mix", i, acc[:, POOL_BANK[kt // 2], :], lambda f: table[:, 0, SCALE_COL + kt + f:SCALE_COL + kt + f + 1],
                               filled=s_pool_w.granule(0, 0, 1) + max(POOL_ENDS[(kt + f) // GROUP_T][1] for f in range(2)))

                def pool_lo(i):
                    split_lo("pool_mix", i, xT, MIX_T - 2 - 2 * i, stage_place(i))

                for k in range(4):
                    for j in range(PIECE):
                        lo_granule(s_out[0], 0, k, j)
                        if k < 3 and j in (0, 2):
                            pool_scale(2 * k + j // 2)
                        if k < 3 and j in (1, 3):
                            pool_lo(2 * k + j // 2)
            else:
                def rotate(c):
                    dve.wait_ge(h_evacuated, c + 1)
                    if c == 1:
                        dve.wait_ge(trig_made, 1)
                    else:
                        dve.wait_ge(rotated, ROTATED[DIFF_ORDER[c]] - 1)
                    col = DIFF_ORDER[c] * CHUNK
                    v = h_tok[:, :, col:col + CHUNK].rearrange("p t (h n) -> p t h n", n=QK)
                    x1, x2 = v[:, :, :, 0:ROPE_HALF], v[:, :, :, ROPE_HALF:2 * ROPE_HALF]
                    shape = [P, TT, CHUNK // QK, ROPE_HALF]
                    cos = trig[:, 0, :, :].rearrange("p t (a n) -> p t a n", a=1).broadcast_to(shape)
                    sin = trig[:, 1, :, :].rearrange("p t (a n) -> p t a n", a=1).broadcast_to(shape)
                    tmp = [rot[:, i, :].rearrange("p (t h n) -> p t h n", t=TT, n=ROPE_HALF) for i in range(4)]
                    order.then(nc.vector.tensor_tensor(tmp[0], x1, cos, ALU.mult))
                    order.then(nc.vector.tensor_tensor(tmp[1], x2, sin, ALU.mult))
                    order.then(nc.vector.tensor_tensor(tmp[2], x2, cos, ALU.mult))
                    order.done(nc.vector.tensor_tensor(tmp[3], x1, sin, ALU.mult))
                    order.then(nc.vector.tensor_tensor(x1, tmp[0], tmp[1], ALU.subtract))
                    nc.vector.tensor_tensor(x2, tmp[2], tmp[3], ALU.add).then_inc(rotated, 1)

                def head_max(h):
                    dve.wait_ge(scored, h + 1)
                    if h > 0:
                        dve.wait_ge(exped, h)
                    for t in range(TT):
                        ins = nc.vector.tensor_reduce(mx[:, 2 * t:2 * t + 2], acc[:, 4:6, t * P:t * P + (t + 1) * P], AX.X, ALU.max, negate=True)
                    ins.then_inc(shifted, 1)

                def head_mix(h):
                    dve.wait_ge(exped, h + 1)
                    order.done(nc.vector.reciprocal(recip[:, h, :, :], sums[:, 0:4].rearrange("p (t m) -> p t m", m=2)))
                    for t in range(TT):
                        order.then(nc.vector.tensor_scalar(fold[:, t:t + 1], sums[:, 2 * t:2 * t + 1], recip[:, h, t, 1:2], lam[:, 0:1],
                                                           ALU.mult, ALU.mult))
                    order.wait()
                    for t in range(TT):
                        keys = slice(0, (t + 1) * P)
                        ins = nc.vector.scalar_tensor_tensor(scores[:, t, 0, keys], scores[:, t, 1, keys], fold[:, t:t + 1],
                                                             scores[:, t, 0, keys], ALU.mult, ALU.add)
                    ins.then_inc(mixed, 1)

                def norm_heads(h0):
                    dve.wait_ge(squared, 2 * (h0 + 4))
                    def of(x):
                        return x[:, :, h0:h0 + 4]
                    order.done(nc.vector.tensor_scalar(of(rs_v), of(rs_v), 1.0 / P, RMS_EPS, ALU.mult, ALU.add))
                    rsqrt(of)
                    for t in range(TT):
                        o = h_tok[:, t, h0 * P:(h0 + 4) * P].rearrange("p (h n) -> p h n", n=P)
                        r = rs_y[:, t, h0:h0 + 4].rearrange("p (h a) -> p h a", a=1).broadcast_to([P, 4, P])
                        ins = nc.vector.tensor_tensor(o, o, r, ALU.mult)
                        ins.then_inc(o_normed, 1)

                def beside(n, j):
                    mem_beside(1, n, j, MEM_SLOT[1])
                    c = n // 4 - 1
                    if (n % 4, j) == (1, 0) and c > 0 and DIFF_ORDER[c] < 6:
                        rotate(c)
                    for h in range(HEADS):
                        if (n, j) == (SCORE_SLOT[h], 3):
                            head_max(h)
                        if (n, j) == (SCORE_SLOT[h] + 1, 1):
                            head_mix(h)
                    if (n, j) == (31, 2):
                        norm_heads(0)

                norm_chunk(0, 1, s_down[0], s_diff)
                for n in range(4, 40):
                    for j in range(PIECE):
                        lo_granule(s_diff, n // 4, n % 4, j)
                        beside(n, j)

                def mix_scale(i):
                    scale_bank("diff_mix", i, acc[:, MIX_BANK[i], :], lambda f: subln[:, 0:1])

                def mix_lo(i):
                    split_lo("diff_mix", i, xT, 2 * i, stage_place(i))

                lo_piece(s_out[1], 0, 0)
                norm_heads(4)
                for i in range(2):
                    mix_scale(i)
                for i in range(2):
                    mix_lo(i)
                for i in range(2, 4):
                    lo_granule(s_out[1], 0, 1, 2 * i - 4)
                    mix_scale(i)
                    mix_lo(i)
                    lo_granule(s_out[1], 0, 1, 2 * i - 3)
                norm_heads(8)
                lo_granule(s_out[1], 0, 2, 0)
                mem_o_lo(1, 0)
                lo_granule(s_out[1], 0, 2, 1)
                mem_o_lo(1, 1)
                mix_scale(4)
                lo_granule(s_out[1], 0, 2, 2)
                mix_scale(5)
                mix_lo(4)
                lo_granule(s_out[1], 0, 2, 3)
                mix_lo(5)
                lo_piece(s_out[1], 0, 3)

            if l > 0:
                dve.wait_ge(resid_affine, 8)
            loop(1, 4, 4, lambda c: proj_chunk(s_out[l], c))
            norm_chunk(l, 0, s_out[l], s_up[l])

            def ffn_gate(g):
                lo_piece(s_up[l], 2 * g, 0)
                conv_bank(l, 1, 0, g - 1)
                lo_piece(s_up[l], 2 * g, 1)
                conv_bank(l, 1, 1, g - 1)
                product(l, 0, g - 1)
                lo_piece(s_up[l], 2 * g, 2)
                product(l, 1, g - 1)
                act_lo_part(l, 0, g - 1)
                lo_piece(s_up[l], 2 * g, 3)
                act_lo_part(l, 1, g - 1)

            def ffn_up(g):
                lo_piece(s_up[l], 2 * g + 1, 0)
                conv_bank(l, 0, 0, g)
                lo_piece(s_up[l], 2 * g + 1, 1)
                conv_bank(l, 0, 1, g)
                lo_piece(s_up[l], 2 * g + 1, 2)
                lo_piece(s_up[l], 2 * g + 1, 3)

            def ffn_pair(g):
                ffn_gate(g)
                ffn_up(g)

            ffn_up(0)
            loop(1, FF_CHUNKS, 8, ffn_pair)
            last = FF_CHUNKS - 1
            lo_piece(s_down[l], 0, 0)
            conv_bank(l, 1, 0, last)
            lo_piece(s_down[l], 0, 1)
            conv_bank(l, 1, 1, last)
            product(l, 0, last)
            lo_piece(s_down[l], 0, 2)
            product(l, 1, last)
            act_lo_part(l, 0, last)
            lo_piece(s_down[l], 0, 3)
            act_lo_part(l, 1, last)
            for k in range(4, FF_T // PIECE):
                lo_piece(s_down[l], 0, k)
            dve.wait_ge(resid_affine, 8 * l + 4)
            loop(1, 4, 4, lambda c: proj_chunk(s_down[l], c))
        resid_out(s_down[1], 3)
        norm_stats()
        dve.wait_ge(out_gb_loaded, 32)
        for half in range(2):
            for t in range(TT):
                cs = slice(half * 1024, (half + 1) * 1024)
                cols = x_tok[:, t, cs]
                order.done(nc.vector.scalar_tensor_tensor(cols, cols, mean_var[:, t, 0:1], out_gb[:, 0, cs], ALU.subtract, ALU.mult))
                nc.vector.scalar_tensor_tensor(cols, cols, rs_y[:, t, 0:1], out_gb[:, 1, cs], ALU.mult, ALU.add).then_inc(out_made, 1)

    @block.tensor
    def _(pe):
        def product3(out, w, x, start, stop):
            pe.matmul(out, w[0], x[0], start=start, stop=False, skip_group_check=True)
            pe.matmul(out, w[0], x[1], start=False, stop=False, skip_group_check=True)
            return pe.matmul(out, w[1], x[0], start=False, stop=stop, skip_group_check=True)

        def features_granule(st, c, k, j, src, bank0):
            kt = PIECE * k + j
            pe.wait_ge(lo_made, st.granule(c, k, j) + 1)
            for f in range(4):
                fs = slice(f * P, (f + 1) * P)
                ins = product3(bank(bank0 + f // 2, (f % 2) * S, (f % 2 + 1) * S), (w_hi[:, j, fs], w_lo[:, j, fs]),
                               (src[:, kt, 0, :], src[:, kt, 1, :]), kt == 0 and f % 2 == 0, kt == KT - 1)
            ins.then_inc(granule_used, 1)

        def tokens_granule(st, c, k, j, src, bank0, piece=None):
            kt = PIECE * (k if piece is None else piece) + j
            pe.wait_ge(lo_made, st.granule(c, k, j) + 1)
            for t in range(TT):
                ts = slice(t * P, (t + 1) * P)
                ins = product3(bank(bank0 + t, 0, CHUNK), (src[:, kt, 0, ts], src[:, kt, 1, ts]),
                               (w_hi[:, j, :], w_lo[:, j, :]), (k, j) == (0, 0), (k, j) == (st.pieces - 1, PIECE - 1))
            ins.then_inc(granule_used, 1)

        def features_chunk(st, c, src, bank0):
            for k in range(st.pieces):
                for j in range(PIECE):
                    features_granule(st, c, k, j, src, bank0)

        def tokens_chunk(st, c, src, bank0, pieces=None, ready=None):
            for k in range(st.pieces):
                for j in range(PIECE):
                    if ready is not None and j % 2 == 0:
                        pe.wait_ge(ready, 2 * k + j // 2 + 1)
                    tokens_granule(st, c, k, j, src, bank0, pieces[k] if pieces else None)

        def transpose_bank(stage, i, b, src, kt):
            for f in range(2):
                for t in range(TT):
                    ins = pe.transpose(acc[:, b, f * S + t * P:f * S + (t + 1) * P], src[:, t, (kt + f) * P:(kt + f + 1) * P], ident[:, :])
            ins.then_inc(banked[stage], 1)

        def ahead(stage, i, src, need):
            for b in ((0, 1, 2) if i == 0 else (i + 2,)):
                if b < KT // 2:
                    need(b)
                    if b >= 4:
                        pe.wait_ge(split[stage], b - 3)
                    transpose_bank(stage, b, 4 + b % 4, src, 2 * b)
            pe.wait_ge(split[stage], i + 1)

        def mem_beside(l, n, j, first):
            q, kvb, pr = qmT[l], kv[l], probs[l]
            for h in range(MEM_HEADS):
                if (n, j) == (first + h, 0):
                    if h == 0:
                        if l == 0:
                            pe.wait_ge(qm_evacuated, 1)
                            pe.wait_ge(table_made, 2)
                            pe.wait_ge(kv_evacuated, 2)
                        else:
                            pe.wait_ge(qk_copied, 2)
                            pe.wait_ge(kv1_loaded, 16)
                    if h >= 2:
                        pe.wait_ge(mem_exped[l], h - 1)
                    for t in range(TT):
                        ins = pe.matmul(acc[:, 4 + h % 2, t * S:(t + 1) * S], q[:, h, t * P:(t + 1) * P],
                                        kvb[:, h // 2, (h % 2) * S:(h % 2 + 1) * S], start=True, stop=True)
                    ins.then_inc(mem_scored[l], 1)
                if (n, j) == (first + h + 1, 1):
                    pe.wait_ge(mem_probs[l], h + 1)
                    if h > 0:
                        pe.wait_ge(mem_pT_copied[l], h)
                    if l == 1:
                        pe.wait_ge(qk_copied, sum(s < n for s in QK_SLOT))
                    for m in range(TT):
                        for t in range(TT):
                            ins = pe.transpose(acc[:, 6, m * S + t * P:m * S + (t + 1) * P], pr[:, h % 2, t, m * P:(m + 1) * P], ident[:, :])
                    ins.then_inc(mem_pT[l], 1)
                if (n, j) == (first + h + 2, 2):
                    pe.wait_ge(mem_pT_copied[l], h + 1)
                    if h > 0:
                        pe.wait_ge(mem_o_copied[l], h)
                    for m in range(TT):
                        ins = pe.matmul(acc[:, 7, 0:S], kvb[:, 2 + m, h * P:(h + 1) * P], pr[:, h % 2, m, :], start=m == 0, stop=m == TT - 1)
                    ins.then_inc(mem_o_made[l], 1)

        pe.wait_ge(ident_made, 2)
        for n in range(16):
            c, k = n // 4, n % 4
            if c >= 2 and k == 0:
                pe.wait_ge(kv_evacuated, c - 1)
            if 4 <= n < 12:
                b = n - 4
                pe.wait_ge(x_loaded[b // 2], 16)
                if b < 4:
                    pe.wait_ge(split["mem"], 5 + b)
                else:
                    pe.wait_ge(split["x"], b - 3)
                transpose_bank("x", b, 4 + b % 4, x_tok, 2 * b)
            if n == 12:
                pe.wait_ge(rows_loaded, 16 * 18)
                pe.wait_ge(split["x"], 6)
                for l in range(DEPTH):
                    for i in range(4):
                        pe.transpose(acc[:, 4 + l, i * CONV_COLS:(i + 1) * CONV_COLS], rows[0:CONV_COLS, l, i, :], ident[0:CONV_COLS, 0:CONV_COLS])
                    cols = TABLE - LN_COL
                    pe.transpose(acc[:, 4 + l, LN_COL:TABLE], rows[0:cols, l, 4, :], ident[0:cols, 0:cols]).then_inc(rows_transposed, 1)
            for j in range(PIECE):
                if c == 0 and j % 2 == 0:
                    ahead("mem", 2 * k + j // 2, mem_tok, lambda b: pe.wait_ge(mem_loaded[b // 2], 16))
                if c % 2 == 0:
                    features_granule(s_kv, c, k, j, memT, 0)
                else:
                    tokens_granule(s_kv, c, k, j, memT, 2)

        pe.wait_ge(split["x"], KT // 2)
        for n in range(16):
            c, k = n // 4, n % 4
            if k == 0 and c < 2:
                pe.wait_ge(kv_evacuated, 3 + c)
            if k == 0 and c == 2:
                pe.wait_ge(qm_evacuated, 1)
            if k == 0 and c == 3:
                pe.wait_ge(pool_evacuated, 1)
            for j in range(PIECE):
                mem_beside(0, n, j, MEM_SLOT[0])
                features_granule(s_pool_in, c, k, j, xT, 2 * (c % 2))
        started = set()
        pe.wait_ge(mem_o_copied[0], MEM_HEADS)
        pe.wait_ge(pool_evacuated, 2)
        for k in range(3):
            pe.wait_ge(dT_made, k + 1)
            if k == 1:
                pe.wait_ge(pool_evacuated, 3)
            for j in range(PIECE):
                kt = PIECE * POOL_W_PIECES[k] + j
                g = kt // GROUP_T
                pe.wait_ge(lo_made, s_pool_w.granule(0, k, j) + 1)
                first, last = (PIECE * k + j == end for end in POOL_ENDS[g])
                for f in range(GROUP_T):
                    ft = GROUP_T * g + f
                    fs = slice(f * P, (f + 1) * P)
                    b = POOL_BANK[ft // 2]
                    ins = product3(acc[:, b, (ft % 2) * S:(ft % 2 + 1) * S], (w_hi[:, j, fs], w_lo[:, j, fs]),
                                   (dT[:, kt, 0, :], dT[:, kt, 1, :]), first and b not in started, last)
                    started.add(b)
                ins.then_inc(granule_used, 1)

        for l in range(DEPTH):
            if l == 0:
                for k in range(4):
                    for j in range(PIECE):
                        if k == 0 and j == 0:
                            pe.wait_ge(split["mem_o0"], 2)
                        if k > 0 and j == 0:
                            pe.wait_ge(split["pool_mix"], 2 * k)
                        tokens_granule(s_out[0], 0, k, j, xT, 0, OUT_PIECES[0][k])
                pe.wait_ge(split["pool_mix"], MIX_T // 2)
            else:
                def value(h):
                    pe.wait_ge(att_copied, h + 1)
                    b = value_bank(h)
                    for t in range(TT):
                        for m in range(t + 1):
                            v = h_tok[:, m, 2 * MIX + h * P:2 * MIX + (h + 1) * P]
                            ins = pe.matmul(acc[:, b, (h % 2) * S + t * P:(h % 2) * S + (t + 1) * P],
                                            qkT[:, h, (t + 1 + m) * P:(t + 2 + m) * P], v, start=m == 0, stop=m == t)
                    ins.then_inc(o_made, 1)

                def bank6_free(n, j):
                    for copied, before in ((qk_copied, sum((s, 3) < (n, j) for s in QK_SLOT)),
                                           (att_copied, sum((s + 1, 1) < (n, j) for s in SCORE_SLOT)),
                                           (mem_pT_copied[1], sum((MEM_SLOT[1] + h + 1, 1) < (n, j) for h in range(MEM_HEADS)))):
                        if before > 0:
                            pe.wait_ge(copied, before)

                def beside(n, j):
                    mem_beside(1, n, j, MEM_SLOT[1])
                    for h in range(HEADS):
                        if (n, j) == (SCORE_SLOT[h], 0):
                            pe.wait_ge(qk_copied, QK_PAIRS.index((3 + h // 4, h % 4 // 2)) + 1)
                            if h == 0:
                                pe.wait_ge(rounded, 2)
                                pe.wait_ge(mem_exped[1], MEM_HEADS)
                            if h > 0:
                                pe.wait_ge(exped, h)
                            for m in range(2):
                                mp = slice(m * QK, (m + 1) * QK)
                                for t in range(TT):
                                    pe.matmul(acc[:, 4 + m, t * P:t * P + (t + 1) * P], qkT[mp, h, t * P:(t + 1) * P],
                                              qkT[mp, h, S:S + (t + 1) * P], start=t == 0, stop=False, skip_group_check=True)
                            for m in range(2):
                                for t in range(TT):
                                    ins = pe.matmul(acc[:, 4 + m, 2 * t * P:(2 * t + 1) * P], ident_r[:, :], mask_r[:, :],
                                                    start=False, stop=True, skip_group_check=True)
                            ins.then_inc(scored, 1)
                        if (n, j) == (SCORE_SLOT[h] + 1, 1):
                            pe.wait_ge(mixed, h + 1)
                            bank6_free(n, j)
                            for t in range(TT):
                                for m in range(t + 1):
                                    ins = pe.transpose(acc[:, 6, (t + 1 + m) * P:(t + 2 + m) * P], scores[:, t, 0, m * P:(m + 1) * P], ident[:, :])
                            ins.then_inc(att_T, 1)
                        if h < 8 and (n, j) == (VALUE_SLOT[h], 2):
                            if h == 0:
                                pe.wait_ge(h_evacuated, DIFF_ORDER.index(6) + 1)
                                pe.wait_ge(mem_o_copied[1], MEM_HEADS)
                            if h == 4:
                                pe.wait_ge(h_evacuated, DIFF_ORDER.index(7) + 1)
                            if h > 0:
                                pe.wait_ge(squared, 2 * (h - 1 if VALUE_SLOT[h] == VALUE_SLOT[h - 1] else h))
                            value(h)
                    for i in range(len(QK_PAIRS)):
                        if (n, j) == (QK_SLOT[i], 3):
                            w, half = QK_PAIRS[i]
                            if w == 9:
                                pe.wait_ge(h_evacuated, 1)
                            else:
                                pe.wait_ge(rotated, ROTATED[w])
                            bank6_free(n, j)
                            for f in range(2):
                                col = w * CHUNK + (2 * half + f) * P
                                for t in range(TT):
                                    ins = pe.transpose(acc[:, 6, f * S + t * P:f * S + (t + 1) * P], h_tok[:, t, col:col + P], ident[:, :])
                            ins.then_inc(qk_banked, 1)

                for n in range(40):
                    c, k = n // 4, n % 4
                    if c >= 2 and k == 0:
                        pe.wait_ge(h_evacuated, c - 1)
                    for j in range(PIECE):
                        if c == 0 and j % 2 == 0:
                            ahead("ln2_0", n * 2 + j // 2, x_tok, lambda b: pe.wait_ge(z_made[0][1], 2 * (b // 2) + 2))
                        beside(n, j)
                        tokens_granule(s_diff, c, k, j, xT, 2 * (c % 2))

                def mix_bank(i):
                    pe.wait_ge(o_normed, 2 * (i // 2) + 2)
                    if i >= 4:
                        pe.wait_ge(split["diff_mix"], i - 3)
                    transpose_bank("diff_mix", i, MIX_BANK[i], h_tok, 2 * i)

                pe.wait_ge(squared, 16)
                pe.wait_ge(att_copied, HEADS)
                pe.wait_ge(exped, HEADS)
                pe.wait_ge(h_evacuated, 9)
                mix_bank(0)
                mix_bank(1)
                pe.wait_ge(h_evacuated, 10)
                for h in range(8, HEADS):
                    value(h)
                mix_bank(2)
                mix_bank(3)
                for k in range(4):
                    for j in range(PIECE):
                        piece = OUT_PIECES[1][k]
                        if piece == 3 and j == 0:
                            pe.wait_ge(split["mem_o1"], 2)
                            mix_bank(4)
                            mix_bank(5)
                        if piece < 3 and j % 2 == 0:
                            pe.wait_ge(split["diff_mix"], 2 * piece + j // 2 + 1)
                        tokens_granule(s_out[1], 0, k, j, xT, 0, piece)
            with nc.tensor.Fori(1, 4) as c:
                tokens_chunk(s_out[l], c, xT, c * 2, OUT_PIECES[l])

            up = s_up[l]
            for k in range(4):
                for j in range(PIECE):
                    if j % 2 == 0:
                        ahead(f"ln1_{l}", 2 * k + j // 2, x_tok, lambda b: pe.wait_ge(z_made[l][0], 2 * (b // 2) + 2))
                    features_granule(up, 0, k, j, xT, 0)
            features_chunk(up, 1, xT, 2)
            with nc.tensor.Fori(1, FF_CHUNKS) as g:
                for s in range(2):
                    pe.wait_ge(conv_made[l][s], g * 2)
                    features_chunk(up, g * 2 + s, xT, 2 * s)
            pe.wait_ge(conv_made[l][0], 2 * FF_CHUNKS)
            with nc.tensor.Fori(0, 4) as c:
                tokens_chunk(s_down[l], c, act, c * 2, ready=act_made[l])

    ctx.close()


_INS = ["x", "mem", "positions", "pool_w_in", "pool_w", "pool_scale", "diff_w_in", "diff_lambda_q1", "diff_lambda_k1",
        "diff_lambda_q2", "diff_lambda_k2", "diff_subln_g", "mem_w_kv", "w_out", "ln1_g", "ln1_b", "ffn_w_up",
        "ffn_conv_w", "ffn_conv_b", "ffn_w_down", "ln2_g", "ln2_b"]


def kernel(**inputs):
    import concourse.bacc as bacc
    from concourse.bass_utils import run_bass_kernel_spmd

    nc = bacc.Bacc("TRN2", target_bir_lowering=False, num_devices=1)
    arrays, args = {}, {}
    for name in _INS:
        v = np.ascontiguousarray(inputs[name])
        arrays[f"in_{name}"] = v
        args[name] = nc.dram_tensor(f"in_{name}", v.shape, mybir.dt.from_np(v.dtype), kind="ExternalInput").ap()
    args["out"] = nc.dram_tensor("out_0", (1, S, D), F32, kind="ExternalOutput").ap()
    build(nc, args)
    r = run_bass_kernel_spmd(nc, [arrays], core_ids=[0])
    return r.results[0]["out_0"]
```

```python
import math
from contextlib import ExitStack

import numpy as np

import concourse.bass as bass
from concourse import mybir

F32 = mybir.dt.float32
F32R = mybir.dt.float32r
I32 = mybir.dt.int32
ALU = mybir.AluOpType
ACT = mybir.ActivationFunctionType
AX = mybir.AxisListType

P = 128
DEPTH = 2
S = 256
TT = S // P
D = 2048
KT = D // P
MEM_HEADS = 4
MEM_W = 512
MIX = D - MEM_W
MIX_T = MIX // P
WINDOWS = (2, 4, 8, 16)
GROUP_T = MIX_T // len(WINDOWS)
DOUBLINGS = [w.bit_length() - 1 for w in WINDOWS]
POOL_STEPS = max(DOUBLINGS) + 2
HEADS = 12
QK = 64
ROPE_HALF = 8
ROPE_THETA = 500000.0
D_FF = 5632
FF_T = D_FF // P
CHUNK = 512
PIECE = 4
SLOTS = 4
FF_CHUNKS = D_FF // CHUNK
DIFF_W = 3 * MIX + MEM_W
OUT_PARTS = (slice(0, 1024), slice(1024, 1536), slice(1536, D))
ALPHA = (2.0 * DEPTH) ** 0.25
LN_EPS = 1e-5
RMS_EPS = 1e-6
LAM_INIT = 0.8 - 0.6 * math.exp(-0.3 * 1)
RSQRT_MAGIC, RSQRT_STEP, RSQRT_CENTRE = 1595932665.0, 0.703952253, 2.38924456
MASKED = -1e30
PAD = max(WINDOWS)
CONV_COLS = 2 * FF_T
LN_COL = 4 * CONV_COLS
SCALE_COL = LN_COL + 4 * KT
TABLE = SCALE_COL + MIX_T
POOL_ORDER = (3, 2, 1, 0)
DIFF_ORDER = (9, 0, 3, 1, 4, 6, 2, 5, 7, 8)
DIFF_LAST = DIFF_W // CHUNK - 1
POOL_W_PIECES = (2, 1, 0)
OUT_PIECES = ((3, 2, 1, 0), (3, 0, 1, 2))
POOL_KT = [PIECE * p + j for p in POOL_W_PIECES for j in range(PIECE)]
POOL_ENDS = [[f(POOL_KT.index(kt) for kt in range(GROUP_T * g, GROUP_T * g + GROUP_T)) for f in (min, max)] for g in range(4)]
POOL_BANK = (3, 2, 7, 6, 5, 4)
QK_PAIRS = [(w, half) for w in DIFF_ORDER if w == 9 or w < 6 for half in range(2)]
QK_SLOT = [4 * DIFF_ORDER.index(w) + 5 + half for w, half in QK_PAIRS]
ROTATED = {w: n + 1 for n, w in enumerate(w for w in DIFF_ORDER if w < 6)}
SCORE_SLOT = [4 * DIFF_ORDER.index(3 + h // 4) + 7 + h % 4 for h in range(HEADS)]
VALUE_AT = [(25, 2), (26, 2), (28, 2), (29, 2), (36, 2), (36, 3), (37, 2), (37, 3), (40, 1), (40, 1), (40, 2), (40, 2)]
SQUARE_AT = [(27, 2), (28, 2), (30, 2), (31, 2), (37, 2), (37, 3), (38, 2), (38, 3), (41, 1), (41, 2), (41, 2), (41, 3)]
MEM_SLOT = (5, 8)
NORM_AT = ((32, 2), (40, 2), (42, 0))
MIX_BANKED_AT = ((38, 0), (38, 1), (40, 3), (41, 0), (42, 1), (42, 2))
MIX_SCALE_AT = ((39, 1), (39, 2), (41, 1), (41, 2), (43, 0), (43, 1))
MIX_HI_AT = ((39, 2), (39, 3), (41, 2), (42, 0), (43, 0), (43, 1))
MIX_LO_AT = ((39, 3), (40, 0), (41, 3), (42, 1), (43, 1), (43, 2))
MIX_BANK = (0, 1, 4, 5, 2, 3)


def value_bank(h):
    return 6 if h >= 10 else 7


class Stream:

    def __init__(self, before, chunks, pieces, width=CHUNK):
        self.chunks, self.pieces, self.width = chunks, pieces, width
        self.first = before.first + before.chunks * before.pieces if before else 0
        self.uses = [len(range(s, pieces, SLOTS)) for s in range(SLOTS)]
        self.loads = [before.loads[s] + before.chunks * before.uses[s] if before else 0 for s in range(SLOTS)]
        self.tail = pieces % SLOTS != 0 or (before is not None and before.pieces % SLOTS != 0)

    def granule(self, c, k, j):
        return c * (self.pieces * PIECE) + ((self.first + k) * PIECE + j)

    def loaded(self, c, k):
        s = k % SLOTS
        return (c * self.uses[s] + (self.loads[s] + k // SLOTS + 1)) * 16

    def slot_split(self, c, k):
        back = 3 if self.tail and k < 3 else SLOTS
        return self.granule(c, k - back, PIECE)

    def used(self, c):
        return self.granule(c, self.pieces, 0)


class Order:

    def __init__(self, eng, sem):
        self.eng, self.sem, self.count, self.steps = eng, sem, 0, 0

    def then(self, ins):
        ins.then_inc(self.sem, 1)
        self.count = self.count + 1
        self.steps += 1

    def wait(self):
        self.eng.wait_ge(self.sem, self.count)

    def done(self, ins):
        self.then(ins)
        self.wait()


def build(nc, a):
    ctx = ExitStack()

    def sb(name, shape, dt=F32, stack=ctx):
        return stack.enter_context(nc.sbuf_tensor(name, shape, dt))

    def sem(name):
        return ctx.enter_context(nc.semaphore(name))

    raw = sb("raw", [P, SLOTS, PIECE * CHUNK])
    w_hi = sb("w_hi", [P, PIECE, CHUNK], F32R)
    w_lo = sb("w_lo", [P, PIECE, CHUNK], F32R)
    x_tok = sb("x_tok", [P, TT, D])
    conv = sb("conv", [P, 2, 2, 512])
    gb = sb("gb", [P, 2, CHUNK])
    table = sb("table", [P, DEPTH, TABLE])
    ident = sb("ident", [P, P])
    mask = sb("mask", [P, P])
    ident_r = sb("ident_r", [P, P], F32R)
    mask_r = sb("mask_r", [P, P], F32R)
    stats = sb("stats", [P, TT, 4, 6])
    mean_var = sb("mean_var", [P, TT, 2])
    rs_v = sb("rs_v", [P, TT, HEADS])
    rs_y = sb("rs_y", [P, TT, HEADS])
    rs_t = sb("rs_t", [P, TT, HEADS])
    rs_u = sb("rs_u", [P, TT, HEADS])
    mx = sb("mx", [P, 16])
    sums = sb("sums", [P, 16])
    recip = sb("recip", [P, HEADS, TT, 2])
    shift = sb("shift", [P, TT, 1])
    fold = sb("fold", [P, TT])
    lam_in = sb("lam_in", [P, 4, QK])
    lam = sb("lam", [P, 4])
    subln = sb("subln", [P, 1])
    steps16 = sb("steps16", [P, PAD], I32)
    pool_fix = sb("pool_fix", [P, len(WINDOWS), PAD])
    pos_i = sb("pos_i", [P, TT], I32)
    trig = sb("trig", [P, 7, TT, ROPE_HALF])

    def region(name, parts):
        stack = ExitStack()
        made = [sb(f"{name}_{n}", shape, dt, stack) for n, shape, dt in parts]
        stack.close()
        return made

    split_x = ("xT", [P, KT, 2, S], F32R)
    xT, act = region("ffn", [split_x, ("act", [P, FF_T, 2, S], F32R)])
    _, kvbuf, qmT0, memT, mem_tok, rows = region("memory", [
        split_x, ("kv", [P, 8, 512], F32), ("qmT", [P, MEM_HEADS, S], F32), ("memT", [P, KT, 2, S], F32R),
        ("mem", [P, TT, D], F32), ("rows", [P, DEPTH, 5, P], F32)])
    _, _, _, dT, pool_h, pool_a, pool_b, probs0 = region("pool", [
        split_x, ("kv", [P, 8, 512], F32), ("qmT", [P, MEM_HEADS, S], F32), ("dT", [P, MIX_T, 2, S], F32R),
        ("h", [P, 4, PAD + S], F32), ("a", [P, 4, PAD + S], F32), ("b", [P, 4, PAD + S], F32),
        ("probs", [P, 2, TT, S], F32)])
    _, h_tok, qkT, qmT1, kv1, probs1, scores, square, rot = region("diff", [
        split_x, ("h_tok", [P, TT, DIFF_W], F32), ("qkT", [P, HEADS, 2 * S], F32), ("qmT", [P, MEM_HEADS, S], F32),
        ("kv", [P, 4, 512], F32), ("probs", [P, 2, TT, S], F32),
        ("scores", [P, TT, 2, S], F32), ("square", [P, 2 * TT, P], F32), ("rot", [P, 4, 128], F32)])
    (out_gb,) = region("last", [("gb", [P, 2, D], F32)])
    acc = ctx.enter_context(nc.psum_tensor("acc", [P, 8, 512], F32))
    kv1_dram = nc.dram_tensor("kv1_dram", [P, 4, 512], F32, kind="Internal").ap()
    qmT = (qmT0, qmT1)
    probs = (probs0, probs1)
    kv = (kvbuf, kv1)

    def bank(b, lo, hi):
        if isinstance(b, int):
            return acc[:, b, lo:hi]
        return acc[:, bass.ds(b, 1), lo:hi].rearrange("p a n -> p (a n)")

    def two(ap):
        return ap.rearrange("p (k s) -> p k s", k=2)

    def stage_place(b):
        return conv[:, b // 2 % 2, b % 2, :]

    s_kv = Stream(None, 4, 4)
    s_pool_in = Stream(s_kv, 4, 4)
    s_pool_w = Stream(s_pool_in, 1, 3, MIX // 4)
    s_out0 = Stream(s_pool_w, 4, 4)
    s_up0 = Stream(s_out0, 2 * FF_CHUNKS, 4)
    s_down0 = Stream(s_up0, 4, FF_T // PIECE)
    s_diff = Stream(s_down0, DIFF_W // CHUNK, 4)
    s_out1 = Stream(s_diff, 4, 4)
    s_up1 = Stream(s_out1, 2 * FF_CHUNKS, 4)
    s_down1 = Stream(s_up1, 4, FF_T // PIECE)
    s_out, s_up, s_down = (s_out0, s_out1), (s_up0, s_up1), (s_down0, s_down1)

    mem_half_loaded, granule_loaded = sem("mem_half_loaded"), [sem(f"granule_loaded{j}") for j in range(PIECE - 1)]
    piece_loaded = [sem(f"piece_loaded{s}") for s in range(SLOTS)]
    hi_made = sem("hi_made")
    lo_made = sem("lo_made")
    granule_used = sem("granule_used")

    x_loaded = [sem(f"x_loaded{c}") for c in range(4)]
    mem_loaded = [sem(f"mem_loaded{c}") for c in range(4)]
    rows_loaded, small_loaded = sem("rows_loaded"), sem("small_loaded")
    zeroed, ident_made, steps_made, pads_made = sem("zeroed"), sem("ident_made"), sem("steps_made"), sem("pads_made")
    rounded = sem("rounded")
    rows_transposed, table_made = sem("rows_transposed"), sem("table_made")
    pool_evacuated, pool_diffed, dT_hi, dT_made = sem("pool_evacuated"), sem("pool_diffed"), sem("dT_hi"), sem("dT_made")
    qm_evacuated = sem("qm_evacuated")
    kv_evacuated = sem("kv_evacuated")
    kv1_stored, kv1_loaded = sem("kv1_stored"), sem("kv1_loaded")
    dve_order = sem("dve_order")
    out_gb_loaded = sem("out_gb_loaded")

    stages = ["x", "mem", "ln1_0", "ln2_0", "ln1_1", "pool_mix", "diff_mix", "mem_o0", "mem_o1"]
    banked = {s: sem(f"{s}_banked") for s in stages}
    scaled = {s: sem(f"{s}_scaled") for s in stages}
    hi_split = {s: sem(f"{s}_hi_split") for s in stages}
    split = {s: sem(f"{s}_split") for s in stages}

    head_scaled, head_hi, head_made = sem("head_scaled"), sem("head_hi"), sem("head_made")

    mem_scored = [sem(f"mem_scored{l}") for l in range(2)]
    mem_shifted = [sem(f"mem_shifted{l}") for l in range(2)]
    mem_exped = [sem(f"mem_exped{l}") for l in range(2)]
    mem_probs = [sem(f"mem_probs{l}") for l in range(2)]
    mem_pT = [sem(f"mem_pT{l}") for l in range(2)]
    mem_pT_copied = [sem(f"mem_pT_copied{l}") for l in range(2)]
    mem_o_made = [sem(f"mem_o_made{l}") for l in range(2)]
    mem_o_copied = [sem(f"mem_o_copied{l}") for l in range(2)]
    z_made = [[sem(f"z_made{l}{n}") for n in range(2)] for l in range(2)]
    tokens0_summed = sem("tokens0_summed")
    gb_loaded, gained, resid_affine = sem("gb_loaded"), sem("gained"), sem("resid_affine")
    tap_now = [[sem(f"tap_now{l}{s}") for s in range(2)] for l in range(2)]
    conv_made = [[sem(f"conv_made{l}{s}") for s in range(2)] for l in range(2)]
    silu_made = [sem(f"silu_made{l}") for l in range(2)]
    product_made = [sem(f"product_made{l}") for l in range(2)]
    act_hi = [sem(f"act_hi{l}") for l in range(2)]
    act_made = [sem(f"act_made{l}") for l in range(2)]
    h_evacuated = sem("h_evacuated")
    trig_arg, trig_made = sem("trig_arg"), sem("trig_made")
    lam_sum, lam_exp = sem("lam_sum"), sem("lam_exp")
    rotated, qk_banked, qk_copied = sem("rotated"), sem("qk_banked"), sem("qk_copied")
    scored, shifted, exped, mixed = sem("scored"), sem("shifted"), sem("exped"), sem("mixed")
    att_T, att_copied, o_made, squared = sem("att_T"), sem("att_copied"), sem("o_made"), sem("squared")
    o_normed = sem("o_normed")
    out_made, out_stored = sem("out_made"), sem("out_stored")
    shift_made, tail_normed, tail_gained, tail_made = sem("shift_made"), sem("tail_normed"), sem("tail_gained"), sem("tail_made")

    block = ctx.enter_context(nc.Block())

    @block.sync
    def _(sp):
        def load_piece(st, c, k, w, col, piece=None):
            free = st.slot_split(c, k)
            if not (isinstance(free, int) and free <= 0):
                sp.wait_ge(lo_made, free)
            r = (k if piece is None else piece) * PIECE * P
            src = w[r:r + PIECE * P, bass.ds(col, st.width)].rearrange("(j p) n -> p j n", p=P)
            dst = raw[:, k % SLOTS, :].rearrange("p (j n) -> p j n", n=CHUNK)[:, :, 0:st.width]
            sp.dma_start(dst, src).then_inc(piece_loaded[k % SLOTS], 16)

        def load_chunk(st, c, w, col, pieces=None):
            for k in range(st.pieces):
                load_piece(st, c, k, w, col, pieces[k] if pieces else None)

        for c, (name, to, loaded) in enumerate((("mem", mem_tok, mem_loaded), ("x", x_tok, x_loaded))):
            src = a[name][0].rearrange("(t p) n -> p t n", p=P)
            for k in range(4):
                cs = slice(k * CHUNK, (k + 1) * CHUNK)
                if c > 0 or k > 0:
                    sp.dma_start(to[:, :, cs], src[:, :, cs]).then_inc(loaded[k], 16)
                    load_piece(s_kv, c, k, a["mem_w_kv"][0], c * CHUNK)
                    continue
                half = CHUNK // 2
                sp.dma_start(to[:, :, 0:half], src[:, :, 0:half]).then_inc(mem_half_loaded, 16)
                for j in range(PIECE):
                    sp.dma_start(raw[:, 0, j * CHUNK:(j + 1) * CHUNK], a["mem_w_kv"][0][j * P:(j + 1) * P, 0:CHUNK]).then_inc(
                        granule_loaded[j] if j < PIECE - 1 else piece_loaded[0], 16)
                    if j == 0:
                        sp.dma_start(to[:, :, half:CHUNK], src[:, :, half:CHUNK]).then_inc(loaded[0], 16)
        for c in range(2, 4):
            load_chunk(s_kv, c, a["mem_w_kv"][1], (c - 2) * CHUNK)
        for c in range(4):
            load_chunk(s_pool_in, c, a["pool_w_in"][0], POOL_ORDER[c] * CHUNK)
        load_chunk(s_pool_w, 0, a["pool_w"][0].rearrange("g r n -> (g r) n"), 0, POOL_W_PIECES)
        for l in range(DEPTH):
            if l == 1:
                for c in range(DIFF_W // CHUNK):
                    load_chunk(s_diff, c, a["diff_w_in"][0], DIFF_ORDER[c] * CHUNK, OUT_PIECES[1] if c == DIFF_LAST else None)
            for c in range(4):
                load_chunk(s_out[l], c, a["w_out"][l], c * CHUNK, OUT_PIECES[l])
            with nc.sync.Fori(0, FF_CHUNKS) as g:
                load_chunk(s_up[l], 2 * g, a["ffn_w_up"][l], g * CHUNK)
                load_chunk(s_up[l], 2 * g + 1, a["ffn_w_up"][l], g * CHUNK + D_FF)
            with nc.sync.Fori(0, 4) as c:
                load_chunk(s_down[l], c, a["ffn_w_down"][l], c * CHUNK)
        out_rows = a["out"][0].rearrange("(t p) n -> p t n", p=P)
        for made, n, t, part in ((out_made, 1, 0, 0), (tail_made, 1, 0, 2), (out_made, 2, 1, 0), (out_made, 3, 0, 1),
                                 (tail_made, 2, 1, 2), (out_made, 4, 1, 1)):
            sp.wait_ge(made, n)
            sp.dma_start(out_rows[:, t, OUT_PARTS[part]], x_tok[:, t, OUT_PARTS[part]]).then_inc(out_stored, 16)
        sp.wait_ge(out_stored, 16 * 6)

    @block.gpsimd
    def _(pool):
        nc.gpsimd.memset(ident[:, :], 0.0).then_inc(zeroed, 1)
        nc.gpsimd.memset(mask[:, :], 0.0).then_inc(zeroed, 1)
        pool.wait_ge(zeroed, 2)
        nc.gpsimd.affine_select(out=ident[:, :], in_=ident[:, :], compare_op=ALU.not_equal, fill=1.0,
                                base=0, pattern=[[-1, P]], channel_multiplier=1).then_inc(ident_made, 1)
        nc.gpsimd.affine_select(out=mask[:, :], in_=mask[:, :], compare_op=ALU.is_ge, fill=MASKED,
                                base=0, pattern=[[-1, P]], channel_multiplier=1).then_inc(ident_made, 1)
        nc.gpsimd.iota(steps16[:, :], pattern=[[1, PAD]], base=1, channel_multiplier=0).then_inc(steps_made, 1)
        for l in range(DEPTH):
            vectors = [a["ffn_conv_w"][l, 0], a["ffn_conv_w"][l, 1], a["ffn_conv_w"][l, 2], a["ffn_conv_b"][l]]
            for i, v in enumerate(vectors):
                pool.dma_start(rows[0:CONV_COLS, l, i, :], v.rearrange("(r n) -> r n", n=P)).then_inc(rows_loaded, 16)
            for i, name in enumerate(("ln1_g", "ln1_b", "ln2_g", "ln2_b")):
                pool.dma_start(rows[i * KT:(i + 1) * KT, l, 4, :], a[name][l].rearrange("(r n) -> r n", n=P)).then_inc(rows_loaded, 16)
            pool.dma_start(rows[4 * KT:4 * KT + MIX_T, l, 4, :], a["pool_scale"][0].rearrange("(r n) -> r n", n=P)).then_inc(rows_loaded, 16)
        for i, name in enumerate(("diff_lambda_q1", "diff_lambda_q2", "diff_lambda_k1", "diff_lambda_k2")):
            pool.dma_start(lam_in[:, i, :], a[name][0:1, :].broadcast_to([P, QK])).then_inc(small_loaded, 16)
        pool.dma_start(subln[:, :], a["diff_subln_g"].rearrange("a p -> p a")).then_inc(small_loaded, 16)
        for t in range(TT):
            pool.dma_start(pos_i[:, t:t + 1], a["positions"][0:1, t * P:(t + 1) * P].rearrange("a p -> p a")).then_inc(small_loaded, 16)
        pool.wait_ge(granule_used, s_kv.used(3))
        nc.gpsimd.memset(pool_h[:, :, 0:PAD], 0.0).then_inc(pads_made, 1)
        pool.wait_ge(kv_evacuated, 4)
        pool.dma_start(kv1_dram[:, :, :], kvbuf[:, 4:8, :]).then_inc(kv1_stored, 16)

        for n_ln, (l, n) in enumerate(((0, 0), (0, 1), (1, 0))):
            pool.wait_ge(banked[f"ln{n + 1}_{l}"], KT // 2)
            if (l, n) == (0, 1):
                pool.wait_ge(kv1_stored, 16)
                pool.dma_start(kv1[:, :, :], kv1_dram[:, :, :]).then_inc(kv1_loaded, 16)
            for c in range(4):
                done = 4 * n_ln + c + 1
                cs = slice(c * CHUNK, (c + 1) * CHUNK)
                for i, name in enumerate((f"ln{n + 1}_g", f"ln{n + 1}_b")):
                    pool.dma_start(gb[:, i, :], a[name][l:l + 1, cs].broadcast_to([P, CHUNK])).then_inc(gb_loaded, 16)
                pool.wait_ge(gb_loaded, 32 * done)
                nc.gpsimd.tensor_tensor(x_tok[:, :, cs], x_tok[:, :, cs], gb[:, 0:1, :].broadcast_to([P, TT, CHUNK]),
                                        ALU.mult).then_inc(gained, 1)
                pool.wait_ge(gained, done)
                nc.gpsimd.tensor_tensor(x_tok[:, :, cs], x_tok[:, :, cs], gb[:, 1:2, :].broadcast_to([P, TT, CHUNK]),
                                        ALU.add).then_inc(resid_affine, 1)
                pool.wait_ge(resid_affine, done)
        pool.wait_ge(granule_used, s_up[1].used(2 * FF_CHUNKS - 1))
        for i, name in enumerate(("ln2_g", "ln2_b")):
            pool.dma_start(out_gb[:, i, :], a[name][1:2, :].broadcast_to([P, D])).then_inc(out_gb_loaded, 16)
        pool.wait_ge(out_gb_loaded, 32)
        for t in range(TT):
            cols = x_tok[:, t, OUT_PARTS[2]]
            pool.wait_ge(tail_normed, t + 1)
            nc.gpsimd.tensor_tensor(cols, cols, out_gb[:, 0, OUT_PARTS[2]], ALU.mult).then_inc(tail_gained, 1)
            pool.wait_ge(tail_gained, t + 1)
            nc.gpsimd.tensor_tensor(cols, cols, out_gb[:, 1, OUT_PARTS[2]], ALU.add).then_inc(tail_made, 1)

    @block.scalar
    def _(act_e):
        def hi_granule(st, c, k, j):
            if j == 0:
                act_e.wait_ge(piece_loaded[k % SLOTS], st.loaded(c, k))
            free = st.granule(c, k, j) - PIECE + 1
            if not (isinstance(free, int) and free <= 0):
                act_e.wait_ge(granule_used, free)
            nc.scalar.activation(w_hi[:, j, 0:st.width], raw[:, k % SLOTS, j * CHUNK:j * CHUNK + st.width],
                                 ACT.Copy).then_inc(hi_made, 1)

        def hi_piece(st, c, k):
            for j in range(PIECE):
                hi_granule(st, c, k, j)

        def split_hi(stage, b, dst, kt0, src):
            if src == "staged":
                act_e.wait_ge(scaled[stage], b + 1)
                src = stage_place(b)
            else:
                act_e.wait_ge(banked[stage], b + 1)
            nc.scalar.activation(dst[:, kt0:kt0 + 2, 0, :], two(src), ACT.Copy).then_inc(hi_split[stage], 1)

        def first_chunk(st, l, n):
            stage = f"ln{n + 1}_{l}"

            def affine(b, f):
                gain = LN_COL + 2 * n * KT + 2 * b + f
                return nc.scalar.activation(stage_place(b)[:, f * S:(f + 1) * S], acc[:, 4 + b % 4, f * S:(f + 1) * S], ACT.Identity,
                                            bias=table[:, l, gain + KT:gain + KT + 1], scale=table[:, l, gain:gain + 1])

            def split_bank(b):
                act_e.wait_ge(banked[stage], b + 1)
                if b >= 4:
                    act_e.wait_ge(split[stage], b - 3)
                affine(b, 0)
                affine(b, 1).then_inc(scaled[stage], 1)
                split_hi(stage, b, xT, 2 * b, "staged")

            hi_piece(st, 0, 0)
            act_e.wait_ge(banked[stage], 1)
            affine(0, 0).then_inc(head_scaled, 1)
            affine(0, 1).then_inc(scaled[stage], 1)
            act_e.wait_ge(head_scaled, 2 * l + n + 1)
            nc.scalar.activation(xT[:, 0, 0, :], stage_place(0)[:, 0:S], ACT.Copy).then_inc(head_hi, 1)
            act_e.wait_ge(scaled[stage], 1)
            nc.scalar.activation(xT[:, 1, 0, :], stage_place(0)[:, S:2 * S], ACT.Copy).then_inc(hi_split[stage], 1)
            split_bank(1)
            split_bank(2)
            for i in range(PIECE, KT):
                hi_granule(st, 0, i // PIECE, i % PIECE)
                if i % 2 == 1 and i < KT - 2:
                    split_bank((i + 1) // 2)

        def mem_exp(l, h):
            act_e.wait_ge(mem_shifted[l], h + 1)
            if h >= 2:
                act_e.wait_ge(mem_probs[l], h - 1)
                act_e.wait_ge(mem_o_made[l], h - 1)
            for t in range(TT):
                i = (h % 2) * TT + t
                ins = nc.scalar.activation(probs[l][:, h % 2, t, :], acc[:, 4 + h % 2, t * S:(t + 1) * S], ACT.Exp,
                                           bias=mx[:, i:i + 1], scale=float(P) ** -0.5, accum_out=sums[:, i:i + 1])
            ins.then_inc(mem_exped[l], 1)

        def mem_pT_out(l, h):
            act_e.wait_ge(mem_pT[l], h + 1)
            nc.scalar.activation(probs[l][:, h % 2, :, :], two(acc[:, 6, :]), ACT.Copy).then_inc(mem_pT_copied[l], 1)

        def mem_o_out(l, h):
            act_e.wait_ge(mem_o_made[l], h + 1)
            nc.scalar.activation(qmT[l][:, h, :], acc[:, 7, 0:S], ACT.Copy).then_inc(mem_o_copied[l], 1)

        def mem_o_hi(l, b):
            act_e.wait_ge(mem_o_copied[l], 2 * b + 2)
            nc.scalar.activation(xT[:, MIX_T + 2 * b:MIX_T + 2 * b + 2, 0, :], qmT[l][:, 2 * b:2 * b + 2, :],
                                 ACT.Copy).then_inc(hi_split[f"mem_o{l}"], 1)

        def mem_beside(l, n, j, first):
            for h in range(MEM_HEADS):
                if (n, j) == (first + h + 1, 0):
                    mem_exp(l, h)
                if (n, j) == (first + h + 2, 1):
                    mem_pT_out(l, h)
                if (n, j) == (first + h + 3, 0):
                    mem_o_out(l, h)

        def taps(l, s, g):
            act_e.wait_ge(granule_used, s_up[l].used(2 * g + s))
            if s == 1:
                act_e.wait_ge(lo_made, s_up[l].granule(2 * g + 1, 0, 0) + 1)
            elif not isinstance(g, int):
                act_e.wait_ge(product_made[l], g * 2)
            else:
                act_e.wait_ge(split[f"ln1_{l}"], KT // 2)
            for b in range(2):
                for f in range(2):
                    col = g * 4 + (s * FF_T + 2 * b + f)
                    ins = nc.scalar.activation(conv[:, s, b, f * S:(f + 1) * S], acc[:, 2 * s + b, f * S:(f + 1) * S],
                                               ACT.Identity, bias=table[:, l, bass.ds(col + 3 * CONV_COLS, 1)],
                                               scale=table[:, l, bass.ds(col + 2 * CONV_COLS, 1)])
                ins.then_inc(tap_now[l][s], 1)

        def silu(l, b, g):
            act_e.wait_ge(conv_made[l][0], g * 2 + (b + 1))
            nc.scalar.activation(conv[:, 0, b, :], conv[:, 0, b, :], ACT.Silu).then_inc(silu_made[l], 1)

        def act_hi_part(l, b, g):
            act_e.wait_ge(product_made[l], g * 2 + (b + 1))
            nc.scalar.activation(act[:, bass.ds(g * 4 + 2 * b, 2), 0, :], two(conv[:, 1, b, :]), ACT.Copy).then_inc(act_hi[l], 1)

        def kv_out(c):
            act_e.wait_ge(granule_used, s_kv.used(c))
            b = 2 * (c % 2)
            nc.scalar.activation(kvbuf[:, 2 * c:2 * c + 2, :], acc[:, b:b + 2, :], ACT.Copy).then_inc(kv_evacuated, 1)

        split_hi("mem", 0, memT, 0, acc[:, 4, :])
        for j in range(PIECE):
            act_e.wait_ge(granule_loaded[j] if j < PIECE - 1 else piece_loaded[0], 16)
            nc.scalar.activation(w_hi[:, j, :], raw[:, 0, j * CHUNK:(j + 1) * CHUNK], ACT.Copy).then_inc(hi_made, 1)
            if j == 0:
                split_hi("mem", 1, memT, 2, acc[:, 5, :])
        for n in range(1, 16):
            c, k = n // 4, n % 4
            for j in range(PIECE):
                hi_granule(s_kv, c, k, j)
                if c == 0 and j in (0, 2):
                    b = 2 * k + j // 2
                    split_hi("mem", b, memT, 2 * b, acc[:, 4 + b % 4, :])
                if 5 <= n < 13 and j == 1:
                    split_hi("x", n - 5, xT, 2 * (n - 5), acc[:, 4 + (n - 5) % 4, :])
                if c > 0 and k == 0 and j == 3:
                    kv_out(c - 1)
                if (n, j) == (13, 0):
                    act_e.wait_ge(ident_made, 2)
                    nc.scalar.activation(ident_r[:, :], ident[:, :], ACT.Copy).then_inc(rounded, 1)
                    nc.scalar.activation(mask_r[:, :], mask[:, :], ACT.Copy).then_inc(rounded, 1)
                if (n, j) == (15, 1):
                    act_e.wait_ge(trig_arg, 1)
                    nc.scalar.activation(trig[:, 0:2, :, :].rearrange("p a t n -> p (a t n)"),
                                         trig[:, 2:4, :, :].rearrange("p a t n -> p (a t n)"), ACT.Sin).then_inc(trig_made, 1)

        def pool_out(c):
            act_e.wait_ge(granule_used, s_pool_in.used(c))
            if c > 1:
                act_e.wait_ge(dT_made, c - 1)
            b = 2 * (c % 2)
            nc.scalar.activation(pool_h[:, :, PAD:PAD + S], acc[:, b:b + 2, :].rearrange("p b (k s) -> p (b k) s", k=2),
                                 ACT.Copy).then_inc(pool_evacuated, 1)

        def dT_hi_part(c):
            act_e.wait_ge(pool_diffed, c)
            kt = 4 * POOL_ORDER[c]
            nc.scalar.activation(dT[:, kt:kt + 4, 0, :], pool_h[:, :, PAD:PAD + S], ACT.Copy).then_inc(dT_hi, 1)

        for n in range(16):
            c, k = n // 4, n % 4
            for j in range(PIECE):
                hi_granule(s_pool_in, c, k, j)
                mem_beside(0, n, j, MEM_SLOT[0])
                if (k, j) == (0, 3):
                    if c == 0:
                        kv_out(3)
                    elif c == 1:
                        act_e.wait_ge(granule_used, s_pool_in.used(0))
                        nc.scalar.activation(qmT0[:, :, :], acc[:, 0:2, :].rearrange("p b (k s) -> p (b k) s", k=2),
                                             ACT.Copy).then_inc(qm_evacuated, 1)
                    else:
                        pool_out(c - 1)
                if (n, j) == (2, 1):
                    act_e.wait_ge(lam_sum, 1)
                    nc.scalar.activation(lam[:, 2:4], lam[:, 0:2], ACT.Exp).then_inc(lam_exp, 1)
                if (k, j) == (2, 3) and c > 1:
                    dT_hi_part(c - 1)
        for k in range(3):
            for j in range(PIECE):
                hi_granule(s_pool_w, 0, k, j)
                if (k, j) == (0, 3):
                    pool_out(3)
                if (k, j) == (1, 1):
                    mem_o_hi(0, 0)
                    mem_o_hi(0, 1)
                if (k, j) == (2, 0):
                    dT_hi_part(3)

        for l in range(DEPTH):
            if l == 0:
                for k in range(4):
                    for j in range(PIECE):
                        hi_granule(s_out[0], 0, k, j)
                        if k < 3 and j in (1, 3):
                            i = 2 * k + j // 2
                            split_hi("pool_mix", i, xT, MIX_T - 2 - 2 * i, "staged")
            else:
                def h_out(c):
                    act_e.wait_ge(granule_used, s_diff.used(c))
                    b, col = 2 * (c % 2), DIFF_ORDER[c] * CHUNK
                    nc.scalar.activation(h_tok[:, :, col:col + CHUNK], acc[:, b:b + 2, :], ACT.Copy).then_inc(h_evacuated, 1)

                def qk_out(i):
                    act_e.wait_ge(qk_banked, i + 1)
                    w, half = QK_PAIRS[i]
                    if w == 9:
                        nc.scalar.activation(qmT1[:, 2 * half:2 * half + 2, :], two(acc[:, 6, :]), ACT.Copy).then_inc(qk_copied, 1)
                    else:
                        h, is_key = 4 * (w % 3) + 2 * half, w // 3
                        nc.scalar.activation(qkT[:, h:h + 2, is_key * S:(is_key + 1) * S], two(acc[:, 6, :]), ACT.Copy,
                                             scale=1.0 if is_key else float(QK) ** -0.5).then_inc(qk_copied, 1)

                def head_exp(h):
                    act_e.wait_ge(shifted, h + 1)
                    if h > 0:
                        act_e.wait_ge(att_T, h)
                    for t in range(TT):
                        for m in range(2):
                            i = 2 * t + m
                            keys = slice(t * P, t * P + (t + 1) * P)
                            ins = nc.scalar.activation(scores[:, t, m, 0:(t + 1) * P], acc[:, 4 + m, keys], ACT.Exp,
                                                       bias=mx[:, i:i + 1], accum_out=sums[:, i:i + 1])
                    ins.then_inc(exped, 1)

                def att_out(h):
                    act_e.wait_ge(att_T, h + 1)
                    nc.scalar.activation(qkT[:, h, P:4 * P], acc[:, 6, P:4 * P], ACT.Copy).then_inc(att_copied, 1)

                def o_out(h):
                    bank_of = acc[:, value_bank(h), :].rearrange("p (h t n) -> p h t n", h=2, t=TT)
                    if h % 2 == 0:
                        act_e.wait_ge(o_made, h + 2)
                        act_e.wait_ge(squared, 2 * h)
                        nc.scalar.activation(h_tok[:, :, h * P:(h + 2) * P].rearrange("p t (h n) -> p h t n", h=2), bank_of, ACT.Copy)
                    for t in range(TT):
                        nc.scalar.activation(square[:, 2 * (h % 2) + t, :], bank_of[:, h % 2, t, :], ACT.Square, scale=recip[:, h, t, 0:1],
                                             accum_out=rs_v[:, t, h:h + 1]).then_inc(squared, 1)

                def beside(n, j):
                    mem_beside(1, n, j, MEM_SLOT[1])
                    if (n % 4, j) == (0, 3) and n > 0:
                        h_out(n // 4 - 1)
                    for i in range(len(QK_PAIRS)):
                        if (n, j) == (QK_SLOT[i] + 1, 3):
                            qk_out(i)
                    for h in range(HEADS):
                        if (n, j) == (SCORE_SLOT[h] + 1, 0):
                            head_exp(h)
                        if (n, j) == (SCORE_SLOT[h] + 2, 1):
                            att_out(h)
                        if (n, j) == SQUARE_AT[h]:
                            o_out(h)
                    for b in range(2):
                        if (n, j) == (38, b):
                            mem_o_hi(1, b)
                    for i in range(MIX_T // 2):
                        if (n, j) == MIX_HI_AT[i]:
                            split_hi("diff_mix", i, xT, 2 * i, "staged")

                first_chunk(s_diff, 0, 1)
                for n in range(4, 40):
                    for j in range(PIECE):
                        hi_granule(s_diff, n // 4, n % 4, j)
                        beside(n, j)
                for n in range(40, 44):
                    for j in range(PIECE):
                        hi_granule(s_out[1], 0, n - 40, j)
                        beside(n, j)
            with nc.scalar.Fori(1, 4) as c:
                for k in range(4):
                    hi_piece(s_out[l], c, k)

            def ffn_gate(g):
                hi_piece(s_up[l], 2 * g, 0)
                taps(l, 1, g - 1)
                hi_piece(s_up[l], 2 * g, 1)
                for b in range(2):
                    for j in range(PIECE):
                        hi_granule(s_up[l], 2 * g, 2 + b, j)
                        if j == 1:
                            act_hi_part(l, b, g - 1)

            def ffn_up(g):
                hi_piece(s_up[l], 2 * g + 1, 0)
                taps(l, 0, g)
                hi_piece(s_up[l], 2 * g + 1, 1)
                silu(l, 0, g)
                hi_piece(s_up[l], 2 * g + 1, 2)
                silu(l, 1, g)
                hi_piece(s_up[l], 2 * g + 1, 3)

            first_chunk(s_up[l], l, 0)
            if l == 0:
                act_e.wait_ge(kv1_stored, 16)
            ffn_up(0)
            with nc.scalar.Fori(1, FF_CHUNKS) as g:
                ffn_gate(g)
                ffn_up(g)
            last = FF_CHUNKS - 1
            hi_piece(s_down[l], 0, 0)
            taps(l, 1, last)
            hi_piece(s_down[l], 0, 1)
            for b in range(2):
                for j in range(PIECE):
                    hi_granule(s_down[l], 0, 2 + b, j)
                    if j == 1:
                        act_hi_part(l, b, last)
            for k in range(4, FF_T // PIECE):
                hi_piece(s_down[l], 0, k)
            with nc.scalar.Fori(1, 4) as c:
                for k in range(FF_T // PIECE):
                    hi_piece(s_down[l], c, k)
        act_e.wait_ge(shift_made, 1)
        for t in range(TT):
            cols = x_tok[:, t, OUT_PARTS[2]]
            nc.scalar.activation(cols, cols, ACT.Identity, bias=shift[:, t, :], scale=rs_y[:, t, 0:1]).then_inc(tail_normed, 1)

    @block.vector
    def _(dve):
        order = Order(dve, dve_order)

        def loop(start, end, per, body):
            before, steps = order.count, order.steps
            with nc.vector.Fori(start, end) as i:
                order.count = before + (i - start) * per
                body(i)
                assert order.steps - steps == per, (order.steps - steps, per)
            order.count = before + (end - start) * per

        def lo_granule(st, c, k, j):
            dve.wait_ge(hi_made, st.granule(c, k, j) + 1)
            nc.vector.tensor_tensor(w_lo[:, j, 0:st.width], raw[:, k % SLOTS, j * CHUNK:j * CHUNK + st.width],
                                    w_hi[:, j, 0:st.width].bitcast(F32), ALU.subtract).then_inc(lo_made, 1)

        def lo_piece(st, c, k):
            for j in range(PIECE):
                lo_granule(st, c, k, j)

        def scale_bank(stage, b, src, gain, bias=None, filled=None):
            if filled is not None:
                dve.wait_ge(granule_used, filled)
            else:
                dve.wait_ge(banked[stage], b + 1)
            if b >= 4:
                dve.wait_ge(split[stage], b - 3)
            for f in range(2):
                args = (bias(f), ALU.mult, ALU.add) if bias else (1.0, ALU.mult, ALU.mult)
                ins = nc.vector.tensor_scalar(stage_place(b)[:, f * S:(f + 1) * S], src[:, f * S:(f + 1) * S], gain(f), *args)
            ins.then_inc(scaled[stage], 1)

        def split_lo(stage, b, dst, kt0, src):
            dve.wait_ge(hi_split[stage], b + 1)
            nc.vector.tensor_tensor(dst[:, kt0:kt0 + 2, 1, :], two(src), dst[:, kt0:kt0 + 2, 0, :].bitcast(F32),
                                    ALU.subtract).then_inc(split[stage], 1)

        def rsqrt(of):
            v, y, t, u = of(rs_v), of(rs_y), of(rs_t), of(rs_u)
            order.done(nc.vector.tensor_scalar(y.bitcast(I32), v.bitcast(I32), -0.5, RSQRT_MAGIC, ALU.mult, ALU.add))
            order.done(nc.vector.tensor_tensor(t, y, y, ALU.mult))
            order.done(nc.vector.scalar_tensor_tensor(t, t, -RSQRT_STEP, v, ALU.mult, ALU.mult))
            order.done(nc.vector.scalar_tensor_tensor(y, t, RSQRT_STEP * RSQRT_CENTRE, y, ALU.add, ALU.mult))
            order.done(nc.vector.tensor_tensor(t, y, y, ALU.mult))
            order.done(nc.vector.tensor_tensor(t, t, v, ALU.mult))
            order.done(nc.vector.tensor_scalar(u, t, 0.375, -1.25, ALU.mult, ALU.add))
            order.done(nc.vector.tensor_tensor(u, u, t, ALU.mult))
            order.done(nc.vector.scalar_tensor_tensor(y, u, 1.875, y, ALU.add, ALU.mult))

        def resid_out(st, c):
            dve.wait_ge(granule_used, st.used(c))
            for t in range(TT):
                cols = x_tok[:, t, bass.ds(c * CHUNK, CHUNK)]
                order.then(nc.vector.scalar_tensor_tensor(cols, cols, ALPHA, bank(2 * c + t, 0, CHUNK), ALU.mult, ALU.add))
            order.wait()
            for t in range(TT):
                order.then(nc.vector.bn_stats(stats[:, t, bass.ds(c, 1), :].rearrange("p a n -> p (a n)"), x_tok[:, t, bass.ds(c * CHUNK, CHUNK)]))

        def proj_chunk(st, c):
            lo_piece(st, c, 0)
            resid_out(st, c - 1)
            for k in range(1, st.pieces):
                lo_piece(st, c, k)

        def resid_tile(st, t, n_norm):
            if t == 0:
                dve.wait_ge(tokens0_summed, n_norm)
            else:
                dve.wait_ge(granule_used, st.used(3))
            cols = x_tok[:, t, 3 * CHUNK:D]
            order.done(nc.vector.scalar_tensor_tensor(cols, cols, ALPHA, acc[:, 6 + t, :], ALU.mult, ALU.add))
            order.done(nc.vector.bn_stats(stats[:, t, 3, :], cols))
            order.then(nc.vector.bn_aggr(mean_var[:, t, :], stats[:, t, :, :]))

        def norm_stats():
            order.wait()
            order.done(nc.vector.tensor_scalar(rs_v[:, :, 0:1], mean_var[:, :, 1:2], LN_EPS, None, ALU.add))
            rsqrt(lambda x: x[:, :, 0:1])

        def norm_chunk(l, n, st, nxt):
            stage = f"ln{n + 1}_{l}"
            resid_tile(st, 0, 2 * l + n + 1)
            for j in range(2):
                lo_granule(nxt, 0, 0, j)
            resid_tile(st, 1, 2 * l + n + 1)
            norm_stats()

            def z(q, t, part=slice(0, CHUNK)):
                cols = x_tok[:, t, q * CHUNK + part.start:q * CHUNK + part.stop]
                nc.vector.tensor_scalar(cols, cols, mean_var[:, t, 0:1], rs_y[:, t, 0:1],
                                        ALU.subtract, ALU.mult).then_inc(z_made[l][n], 1)

            def lo(b):
                split_lo(stage, b, xT, 2 * b, stage_place(b))

            for part in (slice(0, 2 * P), slice(2 * P, CHUNK)):
                for t in range(TT):
                    z(0, t, part)
            z(1, 0)
            z(1, 1)
            lo_granule(nxt, 0, 0, 2)
            dve.wait_ge(head_hi, 2 * l + n + 1)
            nc.vector.tensor_tensor(xT[:, 0, 1, :], stage_place(0)[:, 0:S], xT[:, 0, 0, :].bitcast(F32), ALU.subtract).then_inc(head_made, 1)
            dve.wait_ge(hi_split[stage], 1)
            nc.vector.tensor_tensor(xT[:, 1, 1, :], stage_place(0)[:, S:2 * S], xT[:, 1, 0, :].bitcast(F32), ALU.subtract).then_inc(split[stage], 1)
            z(2, 0)
            z(2, 1)
            lo_granule(nxt, 0, 0, 3)
            lo(1)
            z(3, 0)
            z(3, 1)
            lo(2)
            for i in range(PIECE, KT):
                lo_granule(nxt, 0, i // PIECE, i % PIECE)
                if i % 2 == 1 and i < KT - 2:
                    lo((i + 1) // 2)

        def mem_max(l, h):
            dve.wait_ge(mem_scored[l], h + 1)
            i = 2 * (h % 2)
            if h >= 2:
                dve.wait_ge(mem_exped[l], h - 1)
            order.done(nc.vector.tensor_reduce(mx[:, 8 + i:10 + i], two(acc[:, 4 + h % 2, :]), AX.X, ALU.max))
            nc.vector.tensor_scalar(mx[:, i:i + 2], mx[:, 8 + i:10 + i], -float(P) ** -0.5, None, ALU.mult).then_inc(mem_shifted[l], 1)

        def mem_normalise(l, h):
            dve.wait_ge(mem_exped[l], h + 1)
            i = 2 * (h % 2)
            order.done(nc.vector.reciprocal(sums[:, 8 + i:10 + i], sums[:, i:i + 2]))
            for t in range(TT):
                ins = nc.vector.tensor_scalar(probs[l][:, h % 2, t, :], probs[l][:, h % 2, t, :], sums[:, 8 + i + t:9 + i + t], None, ALU.mult)
            ins.then_inc(mem_probs[l], 1)

        def mem_beside(l, n, j, first):
            for h in range(MEM_HEADS):
                if (n, j) == (first + h, 3):
                    mem_max(l, h)
                if (n, j) == (first + h + 1, 1):
                    mem_normalise(l, h)

        def mem_o_lo(l, b):
            dve.wait_ge(hi_split[f"mem_o{l}"], b + 1)
            kts = slice(MIX_T + 2 * b, MIX_T + 2 * b + 2)
            nc.vector.tensor_tensor(xT[:, kts, 1, :], qmT[l][:, 2 * b:2 * b + 2, :], xT[:, kts, 0, :].bitcast(F32),
                                    ALU.subtract).then_inc(split[f"mem_o{l}"], 1)

        def conv_bank(l, s, b, g):
            dve.wait_ge(tap_now[l][s], g * 2 + (b + 1))
            for lag in (1, 2):
                for f in range(2):
                    col = g * 4 + (s * FF_T + 2 * b + f + (2 - lag) * CONV_COLS)
                    to = conv[:, s, b, f * S + lag:(f + 1) * S]
                    ins = nc.vector.scalar_tensor_tensor(to, acc[:, 2 * s + b, f * S:(f + 1) * S - lag],
                                                         table[:, l, bass.ds(col, 1)], to, ALU.mult, ALU.add)
                    if lag == 1:
                        order.then(ins)
                if lag == 1:
                    order.wait()
            ins.then_inc(conv_made[l][s], 1)

        def product(l, b, g):
            dve.wait_ge(silu_made[l], g * 2 + (b + 1))
            dve.wait_ge(conv_made[l][1], g * 2 + (b + 1))
            nc.vector.tensor_tensor(conv[:, 1, b, :], conv[:, 1, b, :], conv[:, 0, b, :], ALU.mult).then_inc(product_made[l], 1)

        def act_lo_part(l, b, g):
            dve.wait_ge(act_hi[l], g * 2 + (b + 1))
            kts = bass.ds(g * 4 + 2 * b, 2)
            nc.vector.tensor_tensor(act[:, kts, 1, :], two(conv[:, 1, b, :]), act[:, kts, 0, :].bitcast(F32),
                                    ALU.subtract).then_inc(act_made[l], 1)

        dve.wait_ge(steps_made, 1)
        for g, w in enumerate(WINDOWS):
            order.then(nc.vector.tensor_scalar(pool_fix[:, g, :], steps16[:, :], float(w), None, ALU.min))
        order.wait()
        order.done(nc.vector.reciprocal(pool_fix[:, :, :], pool_fix[:, :, :]))
        for g, w in enumerate(WINDOWS):
            order.then(nc.vector.tensor_scalar(pool_fix[:, g, :], pool_fix[:, g, :], float(w), None, ALU.mult))

        pos_f, ang, turn, part = trig[:, 6, :, 0:1], trig[:, 4, :, :], trig[:, 5, :, :], trig[:, 6, :, :]

        def angles():
            dve.wait_ge(small_loaded, 7 * 16)
            order.done(nc.vector.tensor_copy(pos_f, pos_i[:, :].rearrange("p (t a) -> p t a", a=1)))
            for n in range(ROPE_HALF):
                freq = float(np.float32(ROPE_THETA) ** np.float32(-2.0 * n / (2 * ROPE_HALF)))
                order.then(nc.vector.tensor_scalar(trig[:, 4, :, n:n + 1], pos_f, freq, None, ALU.mult))
            order.wait()

        def reduce_angles(turns):
            two_pi = rest = 2 * math.pi
            whole = 1.5 * 2.0 ** 23
            order.done(nc.vector.tensor_scalar(turn, ang, 1.0 / (two_pi * turns), None, ALU.mult))
            order.done(nc.vector.tensor_scalar(turn, turn, whole, None, ALU.add))
            order.done(nc.vector.tensor_scalar(turn, turn, whole, None, ALU.subtract))
            for bits in (7, 14, 21, 28, 36, 48):
                step = 2.0 ** (3 - bits)
                part_of_2pi = math.floor(rest / step) * step
                rest -= part_of_2pi
                order.done(nc.vector.scalar_tensor_tensor(ang, turn, -part_of_2pi * turns, ang, ALU.mult, ALU.add))

        def sine_arguments():
            pi = float(np.nextafter(np.float32(math.pi), np.float32(0)))
            order.done(nc.vector.tensor_scalar(trig[:, 3, :, :], ang, pi, -pi, ALU.min, ALU.max))
            order.done(nc.vector.tensor_scalar(part, trig[:, 3, :, :], -1.0, None, ALU.mult))
            order.done(nc.vector.tensor_tensor(part, part, trig[:, 3, :, :], ALU.max))
            nc.vector.tensor_scalar(trig[:, 2, :, :], part, -1.0, math.pi / 2, ALU.mult, ALU.add).then_inc(trig_arg, 1)

        split_lo("mem", 0, memT, 0, acc[:, 4, :])
        lo_granule(s_kv, 0, 0, 0)
        split_lo("mem", 1, memT, 2, acc[:, 5, :])
        for j in range(1, PIECE):
            lo_granule(s_kv, 0, 0, j)
        for n in range(1, 16):
            c, k = n // 4, n % 4
            for j in range(PIECE):
                lo_granule(s_kv, c, k, j)
                if c == 0 and j in (0, 2):
                    b = 2 * k + j // 2
                    split_lo("mem", b, memT, 2 * b, acc[:, 4 + b % 4, :])
                if 5 <= n < 13 and j == 1:
                    split_lo("x", n - 5, xT, 2 * (n - 5), acc[:, 4 + (n - 5) % 4, :])
                if (n, j) == (13, 1):
                    for l in range(DEPTH):
                        dve.wait_ge(rows_transposed, l + 1)
                        nc.vector.tensor_copy(table[:, l, :], acc[:, 4 + l, 0:TABLE]).then_inc(table_made, 1)
                if (n, j) == (13, 3):
                    angles()
                if (n, j) == (14, 1):
                    reduce_angles(4096.0)
                if (n, j) == (14, 3):
                    reduce_angles(1.0)
                if (n, j) == (15, 0):
                    sine_arguments()

        def lambda_sums():
            order.done(nc.vector.tensor_tensor(lam_in[:, 0:2, :], lam_in[:, 0:2, :], lam_in[:, 2:4, :], ALU.mult))
            nc.vector.tensor_reduce(lam[:, 0:2], lam_in[:, 0:2, :], AX.X, ALU.add).then_inc(lam_sum, 1)

        def lambda_value():
            dve.wait_ge(lam_exp, 1)
            order.done(nc.vector.tensor_tensor(lam[:, 0:1], lam[:, 3:4], lam[:, 2:3], ALU.subtract))
            order.done(nc.vector.tensor_scalar(lam[:, 0:1], lam[:, 0:1], -LAM_INIT, None, ALU.add))
            order.then(nc.vector.tensor_scalar(subln[:, :], subln[:, :], 1.0 - LAM_INIT, None, ALU.mult))

        def pool_step(f, n, g, i):
            fs, sums_of = slice(f, f + n), (pool_h, pool_a, pool_b, pool_a, pool_b)
            doublings = DOUBLINGS[g]
            if i < doublings:
                reach = 2 ** i
                lo = 2 * reach - 1
                src = sums_of[i]
                order.then(nc.vector.tensor_tensor(sums_of[i + 1][:, fs, lo:], src[:, fs, lo:], src[:, fs, lo - reach:PAD + S - reach], ALU.add))
            src = sums_of[doublings]
            if i == doublings:
                first = src[:, fs, PAD:2 * PAD]
                order.then(nc.vector.tensor_tensor(first, first, pool_fix[:, g:g + 1, :].broadcast_to([P, n, PAD]), ALU.mult))
            if i == doublings + 1:
                ins = nc.vector.scalar_tensor_tensor(pool_h[:, fs, PAD:PAD + S], src[:, fs, PAD:PAD + S], 1.0 / WINDOWS[g],
                                                     pool_h[:, fs, PAD:PAD + S], ALU.mult, ALU.subtract)
                if f + n == 4:
                    ins.then_inc(pool_diffed, 1)
                else:
                    order.then(ins)

        def pool_steps(c, i):
            if i > 0:
                order.wait()
            for f, n, g in pooled(c):
                pool_step(f, n, g, i)

        def pooled(c):
            runs, f, w = [], 0, POOL_ORDER[c]
            while f < 4:
                g = (4 * w + f) // GROUP_T
                n = min(4 - f, GROUP_T * (g + 1) - (4 * w + f))
                runs.append((f, n, g))
                f += n
            return runs

        def dT_lo_part(c):
            dve.wait_ge(dT_hi, c)
            dve.wait_ge(pool_diffed, c)
            kt = 4 * POOL_ORDER[c]
            nc.vector.tensor_tensor(dT[:, kt:kt + 4, 1, :], pool_h[:, :, PAD:PAD + S],
                                    dT[:, kt:kt + 4, 0, :].bitcast(F32), ALU.subtract).then_inc(dT_made, 1)

        def pool_beside(c, k, j):
            if (k, j) == (1, 0):
                dve.wait_ge(pool_evacuated, c)
                if c == 1:
                    dve.wait_ge(pads_made, 1)
            if 0 <= (k - 1) * PIECE + j < POOL_STEPS:
                pool_steps(c, (k - 1) * PIECE + j)
            if (k, j) == (2, 3):
                dT_lo_part(c)

        for n in range(16):
            c, k = n // 4, n % 4
            for j in range(PIECE):
                lo_granule(s_pool_in, c, k, j)
                mem_beside(0, n, j, MEM_SLOT[0])
                if c > 1:
                    pool_beside(c - 1, k, j)
                if (n, j) == (1, 1):
                    lambda_sums()
                if (n, j) == (3, 1):
                    lambda_value()
        for k in range(3):
            for j in range(PIECE):
                lo_granule(s_pool_w, 0, k, j)
                if (k, j) == (1, 3):
                    mem_o_lo(0, 0)
                    mem_o_lo(0, 1)
                if (k, j) == (0, 3):
                    dve.wait_ge(pool_evacuated, 3)
                if 0 <= PIECE * k + j - 3 < POOL_STEPS:
                    pool_steps(3, PIECE * k + j - 3)
                if (k, j) == (2, 0):
                    dT_lo_part(3)

        for l in range(DEPTH):
            if l == 0:
                def pool_scale(i):
                    kt = MIX_T - 2 - 2 * i
                    scale_bank("pool_mix", i, acc[:, POOL_BANK[kt // 2], :], lambda f: table[:, 0, SCALE_COL + kt + f:SCALE_COL + kt + f + 1],
                               filled=s_pool_w.granule(0, 0, 1) + max(POOL_ENDS[(kt + f) // GROUP_T][1] for f in range(2)))

                def pool_lo(i):
                    split_lo("pool_mix", i, xT, MIX_T - 2 - 2 * i, stage_place(i))

                for k in range(4):
                    for j in range(PIECE):
                        lo_granule(s_out[0], 0, k, j)
                        if k < 3 and j in (0, 2):
                            pool_scale(2 * k + j // 2)
                        if k < 3 and j in (1, 3):
                            pool_lo(2 * k + j // 2)
            else:
                def rotate(c):
                    dve.wait_ge(h_evacuated, c + 1)
                    if c == 1:
                        dve.wait_ge(trig_made, 1)
                    else:
                        dve.wait_ge(rotated, ROTATED[DIFF_ORDER[c]] - 1)
                    col = DIFF_ORDER[c] * CHUNK
                    v = h_tok[:, :, col:col + CHUNK].rearrange("p t (h n) -> p t h n", n=QK)
                    x1, x2 = v[:, :, :, 0:ROPE_HALF], v[:, :, :, ROPE_HALF:2 * ROPE_HALF]
                    shape = [P, TT, CHUNK // QK, ROPE_HALF]
                    cos = trig[:, 0, :, :].rearrange("p t (a n) -> p t a n", a=1).broadcast_to(shape)
                    sin = trig[:, 1, :, :].rearrange("p t (a n) -> p t a n", a=1).broadcast_to(shape)
                    tmp = [rot[:, i, :].rearrange("p (t h n) -> p t h n", t=TT, n=ROPE_HALF) for i in range(4)]
                    order.then(nc.vector.tensor_tensor(tmp[0], x1, cos, ALU.mult))
                    order.then(nc.vector.tensor_tensor(tmp[1], x2, sin, ALU.mult))
                    order.then(nc.vector.tensor_tensor(tmp[2], x2, cos, ALU.mult))
                    order.done(nc.vector.tensor_tensor(tmp[3], x1, sin, ALU.mult))
                    order.then(nc.vector.tensor_tensor(x1, tmp[0], tmp[1], ALU.subtract))
                    nc.vector.tensor_tensor(x2, tmp[2], tmp[3], ALU.add).then_inc(rotated, 1)

                def head_max(h):
                    dve.wait_ge(scored, h + 1)
                    if h > 0:
                        dve.wait_ge(exped, h)
                    for t in range(TT):
                        ins = nc.vector.tensor_reduce(mx[:, 2 * t:2 * t + 2], acc[:, 4:6, t * P:t * P + (t + 1) * P], AX.X, ALU.max, negate=True)
                    ins.then_inc(shifted, 1)

                def head_mix(h):
                    dve.wait_ge(exped, h + 1)
                    order.done(nc.vector.reciprocal(recip[:, h, :, :], sums[:, 0:4].rearrange("p (t m) -> p t m", m=2)))
                    for t in range(TT):
                        order.then(nc.vector.tensor_scalar(fold[:, t:t + 1], sums[:, 2 * t:2 * t + 1], recip[:, h, t, 1:2], lam[:, 0:1],
                                                           ALU.mult, ALU.mult))
                    order.wait()
                    for t in range(TT):
                        keys = slice(0, (t + 1) * P)
                        ins = nc.vector.scalar_tensor_tensor(scores[:, t, 0, keys], scores[:, t, 1, keys], fold[:, t:t + 1],
                                                             scores[:, t, 0, keys], ALU.mult, ALU.add)
                    ins.then_inc(mixed, 1)

                def norm_heads(h0):
                    dve.wait_ge(squared, 2 * (h0 + 4))
                    def of(x):
                        return x[:, :, h0:h0 + 4]
                    order.done(nc.vector.tensor_scalar(of(rs_v), of(rs_v), 1.0 / P, RMS_EPS, ALU.mult, ALU.add))
                    rsqrt(of)
                    order.done(nc.vector.tensor_tensor(of(rs_y), of(rs_y), recip[:, h0:h0 + 4, :, 0].rearrange("p h t -> p t h"), ALU.mult))
                    for t in range(TT):
                        o = h_tok[:, t, h0 * P:(h0 + 4) * P].rearrange("p (h n) -> p h n", n=P)
                        r = rs_y[:, t, h0:h0 + 4].rearrange("p (h a) -> p h a", a=1).broadcast_to([P, 4, P])
                        ins = nc.vector.tensor_tensor(o, o, r, ALU.mult)
                        ins.then_inc(o_normed, 1)

                def beside(n, j):
                    mem_beside(1, n, j, MEM_SLOT[1])
                    c = n // 4 - 1
                    if (n % 4, j) == (1, 0) and c > 0 and DIFF_ORDER[c] < 6:
                        rotate(c)
                    for h in range(HEADS):
                        if (n, j) == (SCORE_SLOT[h], 3):
                            head_max(h)
                        if (n, j) == (SCORE_SLOT[h] + 1, 1):
                            head_mix(h)
                    for b in range(2):
                        if (n, j) == (38, b + 2):
                            mem_o_lo(1, b)
                    for i in range(MIX_T // 2):
                        if (n, j) == MIX_SCALE_AT[i]:
                            scale_bank("diff_mix", i, acc[:, MIX_BANK[i], :], lambda f: subln[:, 0:1])
                        if (n, j) == MIX_LO_AT[i]:
                            split_lo("diff_mix", i, xT, 2 * i, stage_place(i))
                    if (n, j) in NORM_AT:
                        norm_heads(4 * NORM_AT.index((n, j)))

                norm_chunk(0, 1, s_down[0], s_diff)
                for n in range(4, 40):
                    for j in range(PIECE):
                        lo_granule(s_diff, n // 4, n % 4, j)
                        beside(n, j)

                for n in range(40, 44):
                    for j in range(PIECE):
                        lo_granule(s_out[1], 0, n - 40, j)
                        beside(n, j)

            if l > 0:
                dve.wait_ge(resid_affine, 8)
            loop(1, 4, 4, lambda c: proj_chunk(s_out[l], c))
            norm_chunk(l, 0, s_out[l], s_up[l])

            def ffn_gate(g):
                lo_piece(s_up[l], 2 * g, 0)
                conv_bank(l, 1, 0, g - 1)
                lo_piece(s_up[l], 2 * g, 1)
                conv_bank(l, 1, 1, g - 1)
                product(l, 0, g - 1)
                lo_piece(s_up[l], 2 * g, 2)
                product(l, 1, g - 1)
                act_lo_part(l, 0, g - 1)
                lo_piece(s_up[l], 2 * g, 3)
                act_lo_part(l, 1, g - 1)

            def ffn_up(g):
                lo_piece(s_up[l], 2 * g + 1, 0)
                conv_bank(l, 0, 0, g)
                lo_piece(s_up[l], 2 * g + 1, 1)
                conv_bank(l, 0, 1, g)
                lo_piece(s_up[l], 2 * g + 1, 2)
                lo_piece(s_up[l], 2 * g + 1, 3)

            def ffn_pair(g):
                ffn_gate(g)
                ffn_up(g)

            ffn_up(0)
            loop(1, FF_CHUNKS, 8, ffn_pair)
            last = FF_CHUNKS - 1
            lo_piece(s_down[l], 0, 0)
            conv_bank(l, 1, 0, last)
            lo_piece(s_down[l], 0, 1)
            conv_bank(l, 1, 1, last)
            product(l, 0, last)
            lo_piece(s_down[l], 0, 2)
            product(l, 1, last)
            act_lo_part(l, 0, last)
            lo_piece(s_down[l], 0, 3)
            act_lo_part(l, 1, last)
            for k in range(4, FF_T // PIECE):
                lo_piece(s_down[l], 0, k)
            dve.wait_ge(resid_affine, 8 * l + 4)
            loop(1, 4, 4, lambda c: proj_chunk(s_down[l], c))
        def centred(t, cs):
            cols = x_tok[:, t, cs]
            order.then(nc.vector.scalar_tensor_tensor(cols, cols, mean_var[:, t, 0:1], out_gb[:, 0, cs], ALU.subtract, ALU.mult))

        def scaled_out(t, cs):
            cols = x_tok[:, t, cs]
            nc.vector.scalar_tensor_tensor(cols, cols, rs_y[:, t, 0:1], out_gb[:, 1, cs], ALU.mult, ALU.add).then_inc(out_made, 1)

        resid_tile(s_down[1], 0, 4)
        dve.wait_ge(out_gb_loaded, 32)
        order.wait()
        centred(0, OUT_PARTS[0])
        resid_tile(s_down[1], 1, 4)
        norm_stats()
        nc.vector.scalar_tensor_tensor(shift[:, :, :], mean_var[:, :, 0:1], -1.0, rs_y[:, :, 0:1], ALU.mult, ALU.mult).then_inc(shift_made, 1)
        scaled_out(0, OUT_PARTS[0])
        centred(1, OUT_PARTS[0])
        centred(0, OUT_PARTS[1])
        order.wait()
        scaled_out(1, OUT_PARTS[0])
        centred(1, OUT_PARTS[1])
        scaled_out(0, OUT_PARTS[1])
        order.wait()
        scaled_out(1, OUT_PARTS[1])

    @block.tensor
    def _(pe):
        def product3(out, w, x, start, stop):
            pe.matmul(out, w[0], x[0], start=start, stop=False, skip_group_check=True)
            pe.matmul(out, w[0], x[1], start=False, stop=False, skip_group_check=True)
            return pe.matmul(out, w[1], x[0], start=False, stop=stop, skip_group_check=True)

        def features_granule(st, c, k, j, src, bank0):
            kt = PIECE * k + j
            pe.wait_ge(lo_made, st.granule(c, k, j) + 1)
            for f in range(4):
                fs = slice(f * P, (f + 1) * P)
                ins = product3(bank(bank0 + f // 2, (f % 2) * S, (f % 2 + 1) * S), (w_hi[:, j, fs], w_lo[:, j, fs]),
                               (src[:, kt, 0, :], src[:, kt, 1, :]), kt == 0 and f % 2 == 0, kt == KT - 1)
            ins.then_inc(granule_used, 1)

        def tokens_granule(st, c, k, j, src, bank0, piece=None):
            kt = PIECE * (k if piece is None else piece) + j
            pe.wait_ge(lo_made, st.granule(c, k, j) + 1)
            for t in range(TT):
                ts = slice(t * P, (t + 1) * P)
                ins = product3(bank(bank0 + t, 0, CHUNK), (src[:, kt, 0, ts], src[:, kt, 1, ts]),
                               (w_hi[:, j, :], w_lo[:, j, :]), (k, j) == (0, 0), (k, j) == (st.pieces - 1, PIECE - 1))
            ins.then_inc(granule_used, 1)

        def features_chunk(st, c, src, bank0):
            for k in range(st.pieces):
                for j in range(PIECE):
                    features_granule(st, c, k, j, src, bank0)

        def tokens_chunk(st, c, src, bank0, pieces=None, ready=None):
            for k in range(st.pieces):
                for j in range(PIECE):
                    if ready is not None and j % 2 == 0:
                        pe.wait_ge(ready, 2 * k + j // 2 + 1)
                    tokens_granule(st, c, k, j, src, bank0, pieces[k] if pieces else None)

        def last_tokens_chunk(st, src, bank0, pieces=None, ready=None):
            c, last = 3, st.pieces - 1
            for k in range(last):
                for j in range(PIECE):
                    if ready is not None and j % 2 == 0:
                        pe.wait_ge(ready, 2 * k + j // 2 + 1)
                    tokens_granule(st, c, k, j, src, bank0, pieces[k] if pieces else None)
            for t in range(TT):
                ts = slice(t * P, (t + 1) * P)
                for j in range(PIECE):
                    kt = PIECE * (pieces[last] if pieces else last) + j
                    pe.wait_ge(lo_made, st.granule(c, last, j) + 1)
                    ins = product3(acc[:, bank0 + t, :], (src[:, kt, 0, ts], src[:, kt, 1, ts]), (w_hi[:, j, :], w_lo[:, j, :]),
                                   False, j == PIECE - 1)
                    if t == TT - 1:
                        ins.then_inc(granule_used, 1)
                    elif j == PIECE - 1:
                        ins.then_inc(tokens0_summed, 1)

        def transpose_bank(stage, i, b, src, kt):
            for f in range(2):
                for t in range(TT):
                    ins = pe.transpose(acc[:, b, f * S + t * P:f * S + (t + 1) * P], src[:, t, (kt + f) * P:(kt + f + 1) * P], ident[:, :])
            ins.then_inc(banked[stage], 1)

        def ahead(stage, i, src, need):
            for b in ((0, 1), (2, 3))[i] if i < 2 else (i + 2,):
                if b < KT // 2:
                    need(b)
                    if b >= 4:
                        pe.wait_ge(split[stage], b - 3)
                    transpose_bank(stage, b, 4 + b % 4, src, 2 * b)
            pe.wait_ge(split[stage], i + 1)

        def normed_ahead(l, n, kt):
            stage, i = f"ln{n + 1}_{l}", kt // 2
            if kt == 0:
                banks = (0, 1, 2)
            else:
                banks = (i + 2,) if kt % 2 == 0 and i + 2 < KT // 2 else ()
            for b in banks:
                pe.wait_ge(z_made[l][n], 2 * b + 2 if b < 2 else 2 * (b // 2) + 4)
                if b >= 4:
                    pe.wait_ge(split[stage], b - 3)
                transpose_bank(stage, b, 4 + b % 4, x_tok, 2 * b)
            if kt == 0:
                pe.wait_ge(head_made, 2 * l + n + 1)
            elif kt == 1 or kt % 2 == 0:
                pe.wait_ge(split[stage], i + 1)

        def mem_beside(l, n, j, first):
            q, kvb, pr = qmT[l], kv[l], probs[l]
            for h in range(MEM_HEADS):
                if (n, j) == (first + h, 0):
                    if h == 0:
                        if l == 0:
                            pe.wait_ge(qm_evacuated, 1)
                            pe.wait_ge(table_made, 2)
                            pe.wait_ge(kv_evacuated, 2)
                        else:
                            pe.wait_ge(qk_copied, 2)
                            pe.wait_ge(kv1_loaded, 16)
                    if h >= 2:
                        pe.wait_ge(mem_exped[l], h - 1)
                    for t in range(TT):
                        ins = pe.matmul(acc[:, 4 + h % 2, t * S:(t + 1) * S], q[:, h, t * P:(t + 1) * P],
                                        kvb[:, h // 2, (h % 2) * S:(h % 2 + 1) * S], start=True, stop=True)
                    ins.then_inc(mem_scored[l], 1)
                if (n, j) == (first + h + 1, 1):
                    pe.wait_ge(mem_probs[l], h + 1)
                    if h > 0:
                        pe.wait_ge(mem_pT_copied[l], h)
                    if l == 1:
                        pe.wait_ge(qk_copied, sum(s < n for s in QK_SLOT))
                    for m in range(TT):
                        for t in range(TT):
                            ins = pe.transpose(acc[:, 6, m * S + t * P:m * S + (t + 1) * P], pr[:, h % 2, t, m * P:(m + 1) * P], ident[:, :])
                    ins.then_inc(mem_pT[l], 1)
                if (n, j) == (first + h + 1, 3):
                    pe.wait_ge(mem_pT_copied[l], h + 1)
                    if h > 0:
                        pe.wait_ge(mem_o_copied[l], h)
                    for m in range(TT):
                        ins = pe.matmul(acc[:, 7, 0:S], kvb[:, 2 + m, h * P:(h + 1) * P], pr[:, h % 2, m, :], start=m == 0, stop=m == TT - 1)
                    ins.then_inc(mem_o_made[l], 1)

        pe.wait_ge(ident_made, 2)
        for n in range(16):
            c, k = n // 4, n % 4
            if c >= 2 and k == 0:
                pe.wait_ge(kv_evacuated, c - 1)
            if 4 <= n < 12:
                b = n - 4
                pe.wait_ge(x_loaded[b // 2], 16)
                if b < 4:
                    pe.wait_ge(split["mem"], 5 + b)
                else:
                    pe.wait_ge(split["x"], b - 3)
                transpose_bank("x", b, 4 + b % 4, x_tok, 2 * b)
            if n == 12:
                pe.wait_ge(rows_loaded, 16 * 18)
                pe.wait_ge(split["x"], 6)
                for l in range(DEPTH):
                    for i in range(4):
                        pe.transpose(acc[:, 4 + l, i * CONV_COLS:(i + 1) * CONV_COLS], rows[0:CONV_COLS, l, i, :], ident[0:CONV_COLS, 0:CONV_COLS])
                    cols = TABLE - LN_COL
                    pe.transpose(acc[:, 4 + l, LN_COL:TABLE], rows[0:cols, l, 4, :], ident[0:cols, 0:cols]).then_inc(rows_transposed, 1)
            for j in range(PIECE):
                if c == 0 and j % 2 == 0:
                    ahead("mem", 2 * k + j // 2, mem_tok, lambda b: pe.wait_ge(mem_loaded[b // 2] if b > 0 else mem_half_loaded, 16))
                if c % 2 == 0:
                    features_granule(s_kv, c, k, j, memT, 0)
                else:
                    tokens_granule(s_kv, c, k, j, memT, 2)

        pe.wait_ge(split["x"], KT // 2)
        for n in range(16):
            c, k = n // 4, n % 4
            if k == 0 and c < 2:
                pe.wait_ge(kv_evacuated, 3 + c)
            if k == 0 and c == 2:
                pe.wait_ge(qm_evacuated, 1)
            if k == 0 and c == 3:
                pe.wait_ge(pool_evacuated, 1)
            for j in range(PIECE):
                mem_beside(0, n, j, MEM_SLOT[0])
                features_granule(s_pool_in, c, k, j, xT, 2 * (c % 2))
        started = set()
        pe.wait_ge(mem_o_copied[0], MEM_HEADS)
        pe.wait_ge(pool_evacuated, 2)
        for k in range(3):
            pe.wait_ge(dT_made, k + 1)
            if k == 1:
                pe.wait_ge(pool_evacuated, 3)
            for j in range(PIECE):
                kt = PIECE * POOL_W_PIECES[k] + j
                g = kt // GROUP_T
                pe.wait_ge(lo_made, s_pool_w.granule(0, k, j) + 1)
                first, last = (PIECE * k + j == end for end in POOL_ENDS[g])
                for f in range(GROUP_T):
                    ft = GROUP_T * g + f
                    fs = slice(f * P, (f + 1) * P)
                    b = POOL_BANK[ft // 2]
                    ins = product3(acc[:, b, (ft % 2) * S:(ft % 2 + 1) * S], (w_hi[:, j, fs], w_lo[:, j, fs]),
                                   (dT[:, kt, 0, :], dT[:, kt, 1, :]), first and b not in started, last)
                    started.add(b)
                ins.then_inc(granule_used, 1)

        for l in range(DEPTH):
            if l == 0:
                for k in range(4):
                    for j in range(PIECE):
                        if k == 0 and j == 0:
                            pe.wait_ge(split["mem_o0"], 2)
                        if k > 0 and j == 0:
                            pe.wait_ge(split["pool_mix"], 2 * k)
                        tokens_granule(s_out[0], 0, k, j, xT, 0, OUT_PIECES[0][k])
                pe.wait_ge(split["pool_mix"], MIX_T // 2)
            else:
                def value(h):
                    pe.wait_ge(att_copied, h + 1)
                    b = value_bank(h)
                    for t in range(TT):
                        for m in range(t + 1):
                            v = h_tok[:, m, 2 * MIX + h * P:2 * MIX + (h + 1) * P]
                            ins = pe.matmul(acc[:, b, (h % 2) * S + t * P:(h % 2) * S + (t + 1) * P],
                                            qkT[:, h, (t + 1 + m) * P:(t + 2 + m) * P], v, start=m == 0, stop=m == t)
                    ins.then_inc(o_made, 1)

                def bank6_free(n, j):
                    for copied, before in ((qk_copied, sum((s, 3) < (n, j) for s in QK_SLOT)),
                                           (att_copied, sum((s + 1, 1) < (n, j) for s in SCORE_SLOT)),
                                           (mem_pT_copied[1], sum((MEM_SLOT[1] + h + 1, 1) < (n, j) for h in range(MEM_HEADS)))):
                        if before > 0:
                            pe.wait_ge(copied, before)

                def beside(n, j):
                    mem_beside(1, n, j, MEM_SLOT[1])
                    for h in range(HEADS):
                        if (n, j) == (SCORE_SLOT[h], 0):
                            pe.wait_ge(qk_copied, QK_PAIRS.index((3 + h // 4, h % 4 // 2)) + 1)
                            if h == 0:
                                pe.wait_ge(rounded, 2)
                                pe.wait_ge(mem_exped[1], MEM_HEADS)
                            if h > 0:
                                pe.wait_ge(exped, h)
                            for m in range(2):
                                mp = slice(m * QK, (m + 1) * QK)
                                for t in range(TT):
                                    pe.matmul(acc[:, 4 + m, t * P:t * P + (t + 1) * P], qkT[mp, h, t * P:(t + 1) * P],
                                              qkT[mp, h, S:S + (t + 1) * P], start=t == 0, stop=False, skip_group_check=True)
                            for m in range(2):
                                for t in range(TT):
                                    ins = pe.matmul(acc[:, 4 + m, 2 * t * P:(2 * t + 1) * P], ident_r[:, :], mask_r[:, :],
                                                    start=False, stop=True, skip_group_check=True)
                            ins.then_inc(scored, 1)
                        if (n, j) == (SCORE_SLOT[h] + 1, 1):
                            pe.wait_ge(mixed, h + 1)
                            bank6_free(n, j)
                            for t in range(TT):
                                for m in range(t + 1):
                                    ins = pe.transpose(acc[:, 6, (t + 1 + m) * P:(t + 2 + m) * P], scores[:, t, 0, m * P:(m + 1) * P], ident[:, :])
                            ins.then_inc(att_T, 1)
                        if (n, j) == VALUE_AT[h]:
                            if h % 4 == 0:
                                pe.wait_ge(h_evacuated, DIFF_ORDER.index(6 + h // 4) + 1)
                            if h == 0:
                                pe.wait_ge(mem_o_copied[1], MEM_HEADS)
                            if 0 < h < 10 and h % 2 == 0:
                                pe.wait_ge(squared, 2 * h)
                            if h == 10:
                                pe.wait_ge(att_copied, HEADS)
                            value(h)
                    for i in range(MIX_T // 2):
                        if (n, j) == MIX_BANKED_AT[i]:
                            if i == 0:
                                pe.wait_ge(h_evacuated, DIFF_LAST)
                            if i == 2:
                                pe.wait_ge(exped, HEADS)
                            pe.wait_ge(o_normed, 2 * (i // 2) + 2)
                            transpose_bank("diff_mix", i, MIX_BANK[i], h_tok, 2 * i)
                    for i in range(len(QK_PAIRS)):
                        if (n, j) == (QK_SLOT[i], 3):
                            w, half = QK_PAIRS[i]
                            if w == 9:
                                pe.wait_ge(h_evacuated, 1)
                            else:
                                pe.wait_ge(rotated, ROTATED[w])
                            bank6_free(n, j)
                            for f in range(2):
                                col = w * CHUNK + (2 * half + f) * P
                                for t in range(TT):
                                    ins = pe.transpose(acc[:, 6, f * S + t * P:f * S + (t + 1) * P], h_tok[:, t, col:col + P], ident[:, :])
                            ins.then_inc(qk_banked, 1)

                for n in range(40):
                    c, k = n // 4, n % 4
                    if c >= 2 and k == 0:
                        pe.wait_ge(h_evacuated, c - 1)
                    for j in range(PIECE):
                        if c == 0:
                            normed_ahead(0, 1, PIECE * k + j)
                        beside(n, j)
                        tokens_granule(s_diff, c, k, j, xT, 2 * (c % 2), OUT_PIECES[1][k] if c == DIFF_LAST else None)

                pe.wait_ge(scaled["diff_mix"], 2)
                for n in range(40, 44):
                    piece = OUT_PIECES[1][n - 40]
                    for j in range(PIECE):
                        beside(n, j)
                        if piece == 3 and j == 0:
                            pe.wait_ge(split["mem_o1"], 2)
                        if piece < 3 and j % 2 == 0:
                            pe.wait_ge(split["diff_mix"], 2 * piece + j // 2 + 1)
                        tokens_granule(s_out[1], 0, n - 40, j, xT, 0, piece)
            with nc.tensor.Fori(1, 3) as c:
                tokens_chunk(s_out[l], c, xT, c * 2, OUT_PIECES[l])
            last_tokens_chunk(s_out[l], xT, 6, OUT_PIECES[l])

            up = s_up[l]
            for k in range(4):
                for j in range(PIECE):
                    normed_ahead(l, 0, PIECE * k + j)
                    features_granule(up, 0, k, j, xT, 0)
            features_chunk(up, 1, xT, 2)
            with nc.tensor.Fori(1, FF_CHUNKS) as g:
                for s in range(2):
                    pe.wait_ge(conv_made[l][s], g * 2)
                    features_chunk(up, g * 2 + s, xT, 2 * s)
            pe.wait_ge(conv_made[l][0], 2 * FF_CHUNKS)
            with nc.tensor.Fori(0, 3) as c:
                tokens_chunk(s_down[l], c, act, c * 2, ready=act_made[l])
            last_tokens_chunk(s_down[l], act, 6)

    ctx.close()


_INS = ["x", "mem", "positions", "pool_w_in", "pool_w", "pool_scale", "diff_w_in", "diff_lambda_q1", "diff_lambda_k1",
        "diff_lambda_q2", "diff_lambda_k2", "diff_subln_g", "mem_w_kv", "w_out", "ln1_g", "ln1_b", "ffn_w_up",
        "ffn_conv_w", "ffn_conv_b", "ffn_w_down", "ln2_g", "ln2_b"]


def kernel(**inputs):
    import concourse.bacc as bacc
    from concourse.bass_utils import run_bass_kernel_spmd

    nc = bacc.Bacc("TRN2", target_bir_lowering=False, num_devices=1)
    arrays, args = {}, {}
    for name in _INS:
        v = np.ascontiguousarray(inputs[name])
        arrays[f"in_{name}"] = v
        args[name] = nc.dram_tensor(f"in_{name}", v.shape, mybir.dt.from_np(v.dtype), kind="ExternalInput").ap()
    args["out"] = nc.dram_tensor("out_0", (1, S, D), F32, kind="ExternalOutput").ap()
    build(nc, args)
    r = run_bass_kernel_spmd(nc, [arrays], core_ids=[0])
    return r.results[0]["out_0"]
```
